# Optimizing a Trainium2 kernel written in Bass

```python
import numpy as np
import jax
import jax.numpy as jnp
from jax import lax

D_MODEL = 1024
BATCH = 1
SEQ = 2048
DEPTH = 1

HEAD_DIM = 64
RET_WIDTH = D_MODEL // 4
RET_HEADS = RET_WIDTH // HEAD_DIM
RET_CHUNK = 128
CONV_WIDTH = D_MODEL // 4
CONV_K = 3
NSA_WIDTH = D_MODEL // 2
NSA_HEADS = NSA_WIDTH // HEAD_DIM
NSA_KV_GROUPS = 2
NSA_HPG = NSA_HEADS // NSA_KV_GROUPS
NSA_KV_WIDTH = NSA_KV_GROUPS * HEAD_DIM
CMP_LEN = 32
CMP_STRIDE = 16
SLC_LEN = 64
SLC_TOPK = 8
SLC_QBLOCK = 32
WIN_LEN = 256
WIN_QBLOCK = 128
MIX_WIDTH = RET_WIDTH + CONV_WIDTH + NSA_WIDTH
D_FF = 4 * D_MODEL
XPOS_BASE = 10000.0
EPS = 1e-6
NEG_INF = -1e30
FORCE_BONUS = 1e4
IN_WIDTHS = (RET_WIDTH,) * 4 + (CONV_WIDTH,) * 3 + (NSA_WIDTH,) + (NSA_KV_WIDTH,) * 6 + (3 * NSA_HEADS,)
IN_WIDTH = sum(IN_WIDTHS)

kernel_name = 'hybrid_retnet_shortconv_nsa_block'

def rms_norm(x, gain=None):
    xf = x.astype(jnp.float32)
    y = xf * lax.rsqrt(jnp.mean(xf * xf, axis=-1, keepdims=True) + EPS)
    if gain is not None:
        y = y * gain.astype(jnp.float32)
    return y.astype(x.dtype)

def masked_softmax(scores, mask):
    s = jnp.where(mask, scores.astype(jnp.float32), NEG_INF)
    p = jnp.exp(s - jnp.max(s, axis=-1, keepdims=True)) * mask
    return p / jnp.maximum(jnp.sum(p, axis=-1, keepdims=True), 1e-30)

def xpos_rotate(x, cos, sin):
    x1 = x[..., 0::2]
    x2 = x[..., 1::2]
    rot = jnp.stack((-x2, x1), axis=-1).reshape(x.shape)
    return x * cos + rot * sin

def retention(q, k, v, g):
    b, s, _ = q.shape
    h, d, c = RET_HEADS, HEAD_DIM, RET_CHUNK
    n = s // c
    pos = jnp.arange(s, dtype=jnp.float32)
    inv_freq = 1.0 / (XPOS_BASE ** jnp.linspace(0.0, 1.0, d // 2, dtype=jnp.float32))
    ang = jnp.repeat(pos[:, None] * inv_freq[None, :], 2, axis=-1)[:, None, :]
    cos = jnp.cos(ang).astype(q.dtype)
    sin = jnp.sin(ang).astype(q.dtype)
    qh = xpos_rotate(q.reshape(b, s, h, d), cos, sin)
    kh = xpos_rotate(k.reshape(b, s, h, d), cos, sin) * (d ** -0.5)

    def to_chunks(t):
        return t.reshape(b, n, c, h, d).transpose(0, 3, 1, 2, 4)

    qc, kc, vc = to_chunks(qh), to_chunks(kh), to_chunks(v.reshape(b, s, h, d))
    log_gamma = jnp.log(1.0 - 2.0 ** (-5.0 - jnp.arange(h, dtype=jnp.float32)))
    idx = jnp.arange(c, dtype=jnp.float32)
    rel = idx[:, None] - idx[None, :]
    intra_decay = jnp.where(rel >= 0, jnp.exp(log_gamma[:, None, None] * jnp.maximum(rel, 0.0)), 0.0)
    scores = jnp.einsum('bhncd,bhnmd->bhncm', qc, kc) * intra_decay[:, None]
    intra = jnp.einsum('bhncm,bhnmd->bhncd', scores, vc)
    k_decay = jnp.exp(log_gamma[:, None] * (c - 1.0 - idx))[:, None, :, None]
    q_decay = jnp.exp(log_gamma[:, None] * (idx + 1.0))[:, None, :, None]
    chunk_decay = jnp.exp(log_gamma * c)[:, None, None]
    kv = jnp.einsum('bhncd,bhnce->nbhde', kc * k_decay, vc)

    def step(state, kv_n):
        return state * chunk_decay + kv_n, state

    _, prev = lax.scan(step, jnp.zeros(kv.shape[1:], kv.dtype), kv)
    cross = jnp.einsum('bhncd,nbhde->bhnce', qc * q_decay, prev)
    o = (intra + cross).transpose(0, 2, 3, 1, 4).reshape(b, s, h, d)
    o = rms_norm(o).reshape(b, s, h * d)
    return (jax.nn.silu(g) * o).astype(q.dtype)

def short_conv(b_gate, c_gate, h_in, conv_w):
    u = c_gate * h_in
    y = lax.conv_general_dilated(u, conv_w[:, None, :].astype(u.dtype), window_strides=(1,),
                                 padding=[(CONV_K - 1, 0)], dimension_numbers=('NWC', 'WIO', 'NWC'),
                                 feature_group_count=u.shape[-1])
    return b_gate * y

def nsa(q, k_c, v_c, k_s, v_s, k_w, v_w, gate_logits, q_gain, k_gain,
        pe_k, w1_k, w2_k, pe_v, w1_v, w2_v):
    b, s, _ = q.shape
    G, hpg, d = NSA_KV_GROUPS, NSA_HPG, HEAD_DIM
    qh = rms_norm(q.reshape(b, s, G, hpg, d), q_gain) * (d ** -0.5)
    qh = qh.transpose(0, 2, 3, 1, 4)
    t_pos = jnp.arange(s)

    def kv_heads(t):
        return t.reshape(b, s, G, d)

    n_cmp = (s - CMP_LEN) // CMP_STRIDE + 1
    win_idx = np.arange(n_cmp)[:, None] * CMP_STRIDE + np.arange(CMP_LEN)[None, :]

    def compress(t, pe, w1, w2):
        blocks = kv_heads(t)[:, win_idx] + pe[None, None, :, None, :]
        flat = blocks.transpose(0, 1, 3, 2, 4).reshape(b, n_cmp, G, CMP_LEN * d)
        return jax.nn.silu(flat @ w1) @ w2

    k_cmp = rms_norm(compress(k_c, pe_k, w1_k, w2_k), k_gain)
    v_cmp = compress(v_c, pe_v, w1_v, w2_v)
    cmp_end = jnp.arange(n_cmp) * CMP_STRIDE + CMP_LEN - 1
    cmp_mask = cmp_end[None, :] <= t_pos[:, None]
    p_cmp = masked_softmax(jnp.einsum('bghsd,bngd->bghsn', qh, k_cmp), cmp_mask)
    o_cmp = jnp.einsum('bghsn,bngd->bghsd', p_cmp.astype(v_cmp.dtype), v_cmp)

    n_slc = s // SLC_LEN
    n_sel = min(SLC_TOPK, n_slc)
    cs = np.arange(n_cmp)[:, None] * CMP_STRIDE
    ss = np.arange(n_slc)[None, :] * SLC_LEN
    overlap = np.clip(np.minimum(cs + CMP_LEN, ss + SLC_LEN) - np.maximum(cs, ss), 0, None)
    overlap = jnp.asarray(overlap.astype(np.float32) / CMP_LEN)
    imp = jnp.einsum('bghsn,nj->bgsj', p_cmp, overlap)
    t_blk = t_pos // SLC_LEN
    j = jnp.arange(n_slc)
    eligible = j[None, :] <= t_blk[:, None]
    forced = (j[None, :] == 0) | (j[None, :] == t_blk[:, None]) | (j[None, :] == t_blk[:, None] - 1)
    sel_score = jnp.where(eligible, imp + FORCE_BONUS * forced, -1.0)
    _, sel_idx = lax.top_k(sel_score, n_sel)

    ks_blk = rms_norm(kv_heads(k_s), k_gain).transpose(0, 2, 1, 3).reshape(b, G, n_slc, SLC_LEN, d)
    vs_blk = kv_heads(v_s).transpose(0, 2, 1, 3).reshape(b, G, n_slc, SLC_LEN, d)
    gather = jax.vmap(jax.vmap(lambda blocks, ix: blocks[ix]))
    nq = s // SLC_QBLOCK
    n_keys = n_sel * SLC_LEN
    q_sw = qh.reshape(b, G, hpg, nq, SLC_QBLOCK, d).transpose(3, 0, 1, 2, 4, 5)
    idx_sw = sel_idx.reshape(b, G, nq, SLC_QBLOCK, n_sel).transpose(2, 0, 1, 3, 4)

    def sel_block(args):
        q_b, idx_b, blk = args
        t = blk * SLC_QBLOCK + jnp.arange(SLC_QBLOCK)
        k_g = gather(ks_blk, idx_b).reshape(b, G, SLC_QBLOCK, n_keys, d)
        v_g = gather(vs_blk, idx_b).reshape(b, G, SLC_QBLOCK, n_keys, d)
        key_pos = (idx_b[..., None] * SLC_LEN + jnp.arange(SLC_LEN)).reshape(b, G, SLC_QBLOCK, n_keys)
        mask = (key_pos <= t[:, None])[:, :, None]
        p = masked_softmax(jnp.einsum('bghqd,bgqkd->bghqk', q_b, k_g), mask)
        return jnp.einsum('bghqk,bgqkd->bghqd', p.astype(v_g.dtype), v_g)

    o_slc = lax.map(sel_block, (q_sw, idx_sw, jnp.arange(nq)))
    o_slc = o_slc.transpose(1, 2, 3, 0, 4, 5).reshape(b, G, hpg, s, d)

    nb = s // WIN_QBLOCK
    nw = WIN_LEN // WIN_QBLOCK

    def band(t):
        tp = jnp.pad(t.transpose(0, 2, 1, 3), ((0, 0), (0, 0), (WIN_LEN, 0), (0, 0)))
        tp = tp.reshape(b, G, nb + nw, WIN_QBLOCK, d)
        return jnp.concatenate([tp[:, :, i:i + nb] for i in range(nw + 1)], axis=3)

    kw_band = band(rms_norm(kv_heads(k_w), k_gain))
    vw_band = band(kv_heads(v_w))
    q_win = qh.reshape(b, G, hpg, nb, WIN_QBLOCK, d)
    qpos = jnp.arange(nb)[:, None] * WIN_QBLOCK + jnp.arange(WIN_QBLOCK)[None, :]
    kpos = jnp.arange(nb)[:, None] * WIN_QBLOCK - WIN_LEN + jnp.arange((nw + 1) * WIN_QBLOCK)[None, :]
    kp = kpos[:, None, :]
    qp = qpos[:, :, None]
    win_mask = (kp <= qp) & (kp > qp - WIN_LEN) & (kp >= 0)
    p_win = masked_softmax(jnp.einsum('bghiqd,bgikd->bghiqk', q_win, kw_band), win_mask)
    o_win = jnp.einsum('bghiqk,bgikd->bghiqd', p_win.astype(vw_band.dtype), vw_band).reshape(b, G, hpg, s, d)

    gates = jax.nn.sigmoid(gate_logits.astype(jnp.float32)).reshape(b, s, NSA_HEADS, 3).astype(q.dtype)

    def to_bshd(o):
        return o.transpose(0, 3, 1, 2, 4).reshape(b, s, NSA_HEADS, d)

    o = (gates[..., 0:1] * to_bshd(o_cmp) + gates[..., 1:2] * to_bshd(o_slc)
         + gates[..., 2:3] * to_bshd(o_win))
    return o.reshape(b, s, NSA_WIDTH)

def setup_inputs(seed: int = 0) -> dict:
    key = jax.random.key(seed)
    ks = jax.random.split(key, 18)
    f32 = jnp.float32

    def nrm(k, shape, scale):
        return jax.random.normal(k, shape, f32) * scale

    return {
        'x': nrm(ks[0], (BATCH, SEQ, D_MODEL), 1.0),
        'norm_mix': 1.0 + nrm(ks[1], (DEPTH, D_MODEL), 0.05),
        'w_in': nrm(ks[2], (DEPTH, D_MODEL, IN_WIDTH), D_MODEL ** -0.5),
        'conv_w': nrm(ks[3], (DEPTH, CONV_K, CONV_WIDTH), CONV_K ** -0.5),
        'nsa_q_norm': 1.0 + nrm(ks[4], (DEPTH, HEAD_DIM), 0.05),
        'nsa_k_norm': 1.0 + nrm(ks[5], (DEPTH, HEAD_DIM), 0.05),
        'cmp_pe_k': nrm(ks[6], (DEPTH, CMP_LEN, HEAD_DIM), 0.1),
        'cmp_w1_k': nrm(ks[7], (DEPTH, CMP_LEN * HEAD_DIM, HEAD_DIM), (CMP_LEN * HEAD_DIM) ** -0.5),
        'cmp_w2_k': nrm(ks[8], (DEPTH, HEAD_DIM, HEAD_DIM), HEAD_DIM ** -0.5),
        'cmp_pe_v': nrm(ks[9], (DEPTH, CMP_LEN, HEAD_DIM), 0.1),
        'cmp_w1_v': nrm(ks[10], (DEPTH, CMP_LEN * HEAD_DIM, HEAD_DIM), (CMP_LEN * HEAD_DIM) ** -0.5),
        'cmp_w2_v': nrm(ks[11], (DEPTH, HEAD_DIM, HEAD_DIM), HEAD_DIM ** -0.5),
        'w_out': nrm(ks[12], (DEPTH, MIX_WIDTH, D_MODEL), MIX_WIDTH ** -0.5),
        'norm_mlp': 1.0 + nrm(ks[13], (DEPTH, D_MODEL), 0.05),
        'w_up': nrm(ks[14], (DEPTH, D_MODEL, D_FF), D_MODEL ** -0.5),
        'w_down': nrm(ks[15], (DEPTH, D_FF, D_MODEL), D_FF ** -0.5),
    }

def reference(x, norm_mix, w_in, conv_w, nsa_q_norm, nsa_k_norm, cmp_pe_k, cmp_w1_k, cmp_w2_k,
              cmp_pe_v, cmp_w1_v, cmp_w2_v, w_out, norm_mlp, w_up, w_down):
    split_points = [int(v) for v in np.cumsum(IN_WIDTHS)[:-1]]
    for l in range(DEPTH):
        h = rms_norm(x, norm_mix[l])
        z = jnp.einsum('bsd,de->bse', h, w_in[l])
        (r_q, r_k, r_v, r_g, c_b, c_c, c_h, n_q, n_kc, n_vc, n_ks, n_vs, n_kw, n_vw, n_g) = jnp.split(
            z, split_points, axis=-1)
        y_ret = retention(r_q, r_k, r_v, r_g)
        y_conv = short_conv(c_b, c_c, c_h, conv_w[l])
        y_nsa = nsa(n_q, n_kc, n_vc, n_ks, n_vs, n_kw, n_vw, n_g, nsa_q_norm[l], nsa_k_norm[l],
                    cmp_pe_k[l], cmp_w1_k[l], cmp_w2_k[l], cmp_pe_v[l], cmp_w1_v[l], cmp_w2_v[l])
        mixed = jnp.concatenate([y_ret, y_conv, y_nsa], axis=-1)
        x = x + jnp.einsum('bse,ed->bsd', mixed, w_out[l])
        h = rms_norm(x, norm_mlp[l])
        x = x + jnp.einsum('bsf,fd->bsd', jnp.square(jax.nn.relu(jnp.einsum('bsd,df->bsf', h, w_up[l]))), w_down[l])
    return x


_drawn_inputs = setup_inputs


def setup_inputs(seed=0):
    import zlib

    import numpy as np

    out = dict(_drawn_inputs(seed))
    spreads = {}
    factors = {'nsa_q_norm': 8.0, 'nsa_k_norm': 8.0, 'cmp_pe_k': 8.0, 'cmp_pe_v': 3.375}
    for name, (base, spread) in spreads.items():
        noise = np.random.default_rng([zlib.crc32(name.encode()), seed]).standard_normal(out[name].shape)
        drawn = base * np.exp(spread * noise) if base else spread * noise
        out[name] = jnp.asarray(drawn.astype(out[name].dtype))
    for name, factor in factors.items():
        out[name] = (out[name] * factor).astype(out[name].dtype)
    return out
```

```python
from contextlib import ExitStack

import numpy as np

import concourse.bass as bass
from concourse import mybir

ALU = mybir.AluOpType
ACT = mybir.ActivationFunctionType
F32 = mybir.dt.float32
F32R = mybir.dt.float32r
BF16 = mybir.dt.bfloat16
AX_X = mybir.AxisListType.X

P = 128
BANK = 512
EPS = 1e-6


class Space:

    def __init__(self, nc, stack, phase):
        self.nc, self.stack, self.phase = nc, stack, phase

    def sb(self, name, shape, dt=F32):
        return self.stack.enter_context(self.nc.sbuf_tensor(f"{self.phase}_{name}", shape, dt))

    def ps(self, name, shape, dt=F32):
        return self.stack.enter_context(self.nc.psum_tensor(f"{self.phase}_{name}", shape, dt))

    def sem(self, name):
        return self.stack.enter_context(self.nc.semaphore(f"{self.phase}_{name}"))

    def sems(self, name, n):
        return [self.sem(f"{name}{i}") for i in range(n)]


def projection_phase(nc, x, norm_mix, w_in, identity, z):
    S, D = x.shape
    N = w_in.shape[1]
    KT = D // P
    HALVES = 2
    TT = S // P // HALVES
    NB = 9
    BW = N // NB
    RING = 3
    GB = D // BANK
    ZR = 4
    assert BW * NB == N and BW % 2 == 0 and NB % RING == 0 and TT % ZR == 0

    with ExitStack() as stack:
        m = Space(nc, stack, "proj")
        ident = m.sb("ident", [P, P])
        gain = m.sb("gain", [P, D])
        neg_half = m.sb("neg_half", [P, 1])
        xt = m.sb("x_tile", [P, 2, D])
        xn = m.sb("x_normed", [P, 2, D])
        squares = m.sb("squares", [P, 2, D], BF16)
        sum_sq = m.sb("sum_sq", [P, 2])
        mean_sq = m.sb("mean_sq", [P, 2])
        rstd = m.sb("rstd", [P, 2])
        h_hi = m.sb("hT_hi", [P, KT, TT * P], F32R)
        h_lo = m.sb("hT_lo", [P, KT, TT * P], F32R)
        w_raw = m.sb("w_raw", [P, RING, KT, BW])
        w_hi = m.sb("w_hi", [P, RING, KT, BW], F32R)
        w_lo = m.sb("w_lo", [P, RING, KT, BW], F32R)
        z_out = m.sb("z_out", [P, ZR, BW])
        tp = [m.ps(f"transposed{i}", [P, BANK]) for i in range(2 * GB)]
        acc = [m.ps(f"acc{i}", [P, BANK]) for i in range(ZR)]

        const_in = m.sem("const_in")
        const_set = m.sem("const_set")
        x_in = m.sems("x_in", 2)
        squared = m.sem("squared")
        mean_done = m.sem("mean_done")
        rstd_done = m.sem("rstd_done")
        normed = m.sem("normed")
        transposed = m.sem("transposed")
        hi_done = m.sem("hi_done")
        lo_done = m.sem("lo_done")
        w_loaded = m.sems("w_loaded", RING)
        w_hi_done = m.sem("w_hi_done")
        w_lo_done = m.sem("w_lo_done")
        product = m.sem("product")
        copied = m.sem("copied")
        z_free = m.sems("z_free", ZR)

        w_view = w_in.rearrange("(k p) n -> p k n", p=P)
        block = stack.enter_context(nc.Block())

        def blocks_of(eng, half, step):
            with eng.Fori(0, NB // RING) as r:
                for u in range(RING):
                    step(r * RING + (half * NB + u), u, r + half * (NB // RING))

        @block.sync
        def _(sp):
            AHEAD = RING - 1

            def load_w(n, u, col):
                if not isinstance(n, int) or n >= RING:
                    sp.wait_ge(w_lo_done, n - RING + 1)
                sp.dma_start(w_raw[:, u, :, :], w_view[:, :, bass.ds(col, BW)]).then_inc(w_loaded[u], 16)

            def store_z(n, half, col):
                for t in range(TT):
                    s = t % ZR
                    sp.wait_ge(copied, n * TT + (t + 1 + ZR))
                    sp.dma_start(z[(half * TT + t) * P:(half * TT + t + 1) * P, bass.ds(col, BW)],
                                 z_out[:, s, :]).then_inc(z_free[s], 16)

            sp.dma_start(ident[:, :], identity).then_inc(const_in, 16)
            sp.dma_start(gain[:, :], norm_mix.partition_broadcast(P)).then_inc(const_in, 16)
            for n in range(AHEAD):
                load_w(n, n, n * BW)
            for half in range(HALVES):
                first = half * NB
                load_w(first + AHEAD, AHEAD, AHEAD * BW)
                store_z(first, half, 0)
                with sp.Fori(0, (NB - RING) // RING) as r:
                    for u in range(1, 1 + RING):
                        load_w(r * RING + (first + u + AHEAD), (u + AHEAD) % RING, r * (RING * BW) + (u + AHEAD) * BW)
                        store_z(r * RING + (first + u), half, r * (RING * BW) + u * BW)
                for c in range(NB - AHEAD, NB):
                    if half + 1 < HALVES:
                        load_w(first + c + AHEAD, (c + AHEAD) % RING, (c + AHEAD - NB) * BW)
                    store_z(first + c, half, c * BW)
            for s in range(ZR):
                sp.wait_ge(z_free[s], 16 + 16 * HALVES * NB * TT // ZR)

        @block.scalar
        def _(act):
            def split_hi(n, u, j):
                act.wait_ge(w_loaded[u], j * 16 + 16)
                act.wait_ge(product, (n + 1) * TT)
                nc.scalar.copy(w_hi[:, u, :, :], w_raw[:, u, :, :]).then_inc(w_hi_done, 1)

            def load_x(n):
                if n < (half + 1) * TT:
                    if n >= 2:
                        act.wait_ge(normed, n - 1)
                    act.dma_start(xt[:, n % 2, :], x[n * P:(n + 1) * P, :]).then_inc(x_in[n % 2], 16)

            act.sem_inc(product, RING * TT)
            for half in range(HALVES):
                load_x(half * TT)
                load_x(half * TT + 1)
                for n in range(half * TT, (half + 1) * TT + 1):
                    if n < (half + 1) * TT:
                        act.wait_ge(x_in[n % 2], 16 * (n // 2 + 1))
                        if n >= 2:
                            act.wait_ge(mean_done, n - 1)
                        nc.scalar.activation(squares[:, n % 2, :], xt[:, n % 2, :], ACT.Square,
                                             accum_out=sum_sq[:, n % 2:n % 2 + 1]).then_inc(squared, 1)
                    if n > half * TT:
                        t = n - 1
                        act.wait_ge(transposed, t + 1)
                        c = (t - half * TT) * P
                        for g in range(GB):
                            copy = nc.scalar.copy(h_hi[:, 4 * g:4 * g + 4, c:c + P],
                                                  tp[t % 2 * GB + g][:, :].rearrange("p (k c) -> p k c", c=P))
                        copy.then_inc(hi_done, 1)
                        load_x(t + 2)
                blocks_of(act, half, split_hi)

        @block.gpsimd
        def _(pool):
            def split_lo(n, u, j):
                pool.wait_ge(w_hi_done, n + 1)
                nc.gpsimd.tensor_tensor(w_lo[:, u, :, :], w_raw[:, u, :, :], w_hi[:, u, :, :].bitcast(F32),
                                        ALU.subtract).then_inc(w_lo_done, 1)

            nc.gpsimd.memset(neg_half[:, :], -0.5).then_inc(const_set, 1)
            pool.wait_ge(const_set, 1)
            for half in range(HALVES):
                for n in range(half * TT, (half + 1) * TT):
                    b = n % 2
                    pool.wait_ge(squared, n + 1)
                    if n >= 2:
                        pool.wait_ge(normed, n - 1)
                    nc.gpsimd.tensor_scalar(mean_sq[:, b:b + 1], sum_sq[:, b:b + 1], 1.0 / D, EPS,
                                            ALU.mult, ALU.add).then_inc(mean_done, 1)
                    pool.wait_ge(mean_done, n + 1)
                    nc.gpsimd.tensor_tensor(rstd[:, b:b + 1], mean_sq[:, b:b + 1], neg_half[:, :],
                                            ALU.pow).then_inc(rstd_done, 1)
                blocks_of(pool, half, split_lo)

        @block.vector
        def _(dve):
            def evacuate(n, u, j):
                for t in range(TT):
                    s = t % ZR
                    dve.wait_ge(product, (n + RING) * TT + (t + 1))
                    dve.wait_ge(z_free[s], n * (16 * TT // ZR) + 16 * (t // ZR + 1))
                    nc.vector.tensor_copy(z_out[:, s, :], acc[s][:, 0:BW]).then_inc(copied, 1)

            dve.sem_inc(copied, ZR)
            for s in range(ZR):
                dve.sem_inc(z_free[s], 16)
            dve.wait_ge(const_in, 32)
            for half in range(HALVES):
                for n in range(half * TT, (half + 1) * TT + 1):
                    if n < (half + 1) * TT:
                        b = n % 2
                        dve.wait_ge(rstd_done, n + 1)
                        if n >= 2:
                            dve.wait_ge(transposed, n - 1)
                        nc.vector.scalar_tensor_tensor(
                            out=xn[:, b, :], in0=xt[:, b, :], scalar=rstd[:, b:b + 1], in1=gain[:, :],
                            op0=ALU.mult, op1=ALU.mult).then_inc(normed, 1)
                    if n > half * TT:
                        t = n - 1
                        dve.wait_ge(hi_done, t + 1)
                        c = (t - half * TT) * P
                        for g in range(GB):
                            sub = nc.vector.tensor_tensor(
                                h_lo[:, 4 * g:4 * g + 4, c:c + P],
                                tp[t % 2 * GB + g][:, :].rearrange("p (k c) -> p k c", c=P),
                                h_hi[:, 4 * g:4 * g + 4, c:c + P].bitcast(F32), ALU.subtract)
                        sub.then_inc(lo_done, 1)
                blocks_of(dve, half, evacuate)

        @block.tensor
        def _(pe):
            def multiply(n, u, j):
                pe.wait_ge(w_lo_done, n + 1)
                for t in range(TT):
                    s = t % ZR
                    pe.wait_ge(copied, n * TT + (t + 1))
                    rows = slice(t * P, (t + 1) * P)
                    for k in range(KT):
                        for a, w in ((h_hi, w_hi), (h_lo, w_hi), (h_hi, w_lo)):
                            mm = nc.tensor.matmul(acc[s][:, 0:BW], a[:, k, rows], w[:, u, k, :],
                                                  start=k == 0 and a is h_hi and w is w_hi,
                                                  stop=k == KT - 1 and w is w_lo)
                    mm.then_inc(product, 1)

            pe.wait_ge(const_in, 32)
            for half in range(HALVES):
                for n in range(half * TT, (half + 1) * TT):
                    pe.wait_ge(normed, n + 1)
                    if n >= 2:
                        pe.wait_ge(lo_done, n - 1)
                    for k in range(KT):
                        mm = nc.tensor.transpose(tp[n % 2 * GB + k // 4][:, k % 4 * P:k % 4 * P + P],
                                                 xn[:, n % 2, k * P:(k + 1) * P], ident[:, :])
                    mm.then_inc(transposed, 1)
                pe.wait_ge(lo_done, (half + 1) * TT)
                blocks_of(pe, half, multiply)

def chain(eng, done):
    count = [0]

    def link(instruction):
        count[0] += 1
        instruction.then_inc(done, 1)
        eng.wait_ge(done, count[0])

    return link


MASKED = -1e30
HEAD = 64
RET_HEADS = 4
GROUPS = 2
HPG = 4
NSA_HEADS = GROUPS * HPG
STRIDE, CMP_LEN, SLC_LEN, TOPK = 16, 32, 64, 8

RQ, RK, RV, RG = 0, 256, 512, 768
CB_, CC, CH = 1024, 1280, 1536
NQ = 1792
NKC, NVC, NKS, NVS, NKW, NVW = 2304, 2432, 2560, 2688, 2816, 2944
NG = 3072


def compress_phase(nc, z, weights, k_gain, identity, overlap, keys_a, keys_b, values):
    S = z.shape[0]
    NT = S // P
    NW = (S - CMP_LEN) // STRIDE + 1
    NBLK = S // SLC_LEN
    KINDS = 2

    with ExitStack() as stack:
        m = Space(nc, stack, "cmp")
        ident = m.sb("ident", [P, P])
        kv = m.sb("kv", [P, NT, KINDS * P])
        kvT = m.sb("kvT", [P, KINDS, S])
        w1 = m.sb("w1", [P, KINDS, CMP_LEN, HEAD])
        w2 = m.sb("w2", [HEAD, KINDS, HEAD])
        pe_rows = m.sb("pe_rows", [P, KINDS * HEAD])
        peT = m.sb("peT", [HEAD, KINDS, CMP_LEN])
        bias = m.sb("bias", [HEAD, KINDS])
        gain = m.sb("gain", [P, HEAD])
        pre = m.sb("pre", [HEAD, KINDS * GROUPS, P])
        den = m.sb("den", [HEAD, KINDS * GROUPS, P])
        act_out = m.sb("silu", [HEAD, KINDS * GROUPS, P])
        kc = m.sb("kc", [P, GROUPS, HEAD])
        sq = m.sb("sq", [P, GROUPS, HEAD])
        ssq = m.sb("ssq", [P, GROUPS])
        mean = m.sb("mean", [P, GROUPS])
        rstd = m.sb("rstd", [P, GROUPS])
        neg_half = m.sb("neg_half", [P, GROUPS])
        pack = m.sb("pack", [P, GROUPS, P])
        banks = [m.ps(f"bank{i}", [P, BANK]) for i in range(8)]

        loaded = m.sem("loaded")
        cleared = m.sem("cleared")
        transposed = m.sem("transposed")
        copied = m.sem("copied")
        pe_T = m.sem("pe_T")
        pe_copied = m.sem("pe_copied")
        bias_sum = m.sem("bias_sum")
        bias_set = m.sem("bias_set")
        first = m.sem("first_product")
        biased = m.sem("biased")
        exp_done = m.sem("exp_done")
        silu_done = m.sem("silu_done")
        second = m.sem("second_product")
        squares = m.sem("squares")
        powered = m.sem("powered")
        packed = m.sem("packed")
        packT = m.sem("packT")
        out_a = m.sem("keys_a_set")
        dve_done = m.sem("dve_done")
        pool_done = m.sem("pool_done")
        block = stack.enter_context(nc.Block())
        LOADS = 1 + 1 + 2 * KINDS + 1 + KINDS + KINDS + 1 + GROUPS

        @block.sync
        def _(sp):
            sp.wait_ge(cleared, 1)
            sp.dma_start(ident[:, :], identity).then_inc(loaded, 16)
            sp.dma_start(kv[:, :, :], z[:, NKC:NKC + KINDS * P].rearrange("(t p) c -> p t c", p=P)).then_inc(loaded, 16)
            for j, (pe_, w1_, w2_) in enumerate(weights):
                for g in range(GROUPS):
                    sp.dma_start(w1[g * HEAD:(g + 1) * HEAD, j, :, :],
                                 w1_.rearrange("(l d) e -> d l e", d=HEAD)).then_inc(loaded, 16)
                sp.dma_start(w2[:, j, :], w2_).then_inc(loaded, 16)
                sp.dma_start(pe_rows[0:CMP_LEN, j * HEAD:(j + 1) * HEAD], pe_).then_inc(loaded, 16)
            sp.dma_start(gain[:, :], k_gain.partition_broadcast(P)).then_inc(loaded, 16)
            for g in range(GROUPS):
                sp.dma_start(values[:, g, HEAD + 1:], overlap).then_inc(loaded, 16)

        TOTAL = 16 * (2 + KINDS * (GROUPS + 2) + 1 + GROUPS)

        @block.gpsimd
        def _(pool):
            link = chain(pool, pool_done)
            link(nc.gpsimd.memset(pe_rows[:, :], 0.0))
            link(nc.gpsimd.memset(values[:, :, :], 0.0))
            link(nc.gpsimd.memset(pack[:, :, :], 0.0))
            link(nc.gpsimd.memset(values[:, :, HEAD:HEAD + 1], 1.0))
            nc.gpsimd.memset(neg_half[:, :], -0.5).then_inc(cleared, 1)
            pool.wait_ge(squares, 1)
            link(nc.gpsimd.tensor_scalar(mean[:, :], ssq[:, :], 1.0 / HEAD, EPS, ALU.mult, ALU.add))
            nc.gpsimd.tensor_tensor(rstd[:, :], mean[:, :], neg_half[:, :], ALU.pow).then_inc(powered, 1)

        @block.tensor
        def _(pe):
            pe.wait_ge(loaded, TOTAL)
            for q in range(KINDS * NT // 4):
                j, t0 = divmod(4 * q, NT)
                for t in range(4):
                    mm = nc.tensor.transpose(banks[q][:, t * P:(t + 1) * P],
                                             kv[:, t0 + t, j * P:(j + 1) * P], ident[:, :])
                mm.then_inc(transposed, 1)
            pe.wait_ge(copied, 1)
            nc.tensor.transpose(banks[0][:, 0:P], pe_rows[:, :], ident[:, :]).then_inc(pe_T, 1)
            pe.wait_ge(pe_copied, 1)
            for j in range(KINDS):
                for l in range(CMP_LEN):
                    mm = nc.tensor.matmul(banks[0][0:HEAD, P + j:P + j + 1], w1[0:HEAD, j, l, :],
                                          peT[:, j, l:l + 1], start=l == 0, stop=l == CMP_LEN - 1)
            mm.then_inc(bias_sum, 1)
            pe.wait_ge(copied, KINDS * NT // 4)
            for j in range(KINDS):
                for g in range(GROUPS):
                    rows = slice(g * HEAD, (g + 1) * HEAD)
                    for l in range(CMP_LEN):
                        mm = nc.tensor.matmul(banks[1 + j * GROUPS + g][0:HEAD, 0:NW], w1[rows, j, l, :],
                                              kvT[rows, j, l:l + (NW - 1) * STRIDE + 1:STRIDE],
                                              start=l == 0, stop=l == CMP_LEN - 1)
                    mm.then_inc(first, 1)
            pe.wait_ge(silu_done, 1)
            for n in range(KINDS * GROUPS):
                mm = nc.tensor.matmul(banks[5][0:NW, n * HEAD:(n + 1) * HEAD], act_out[:, n, 0:NW],
                                      w2[:, n // GROUPS, :], start=True, stop=True)
            mm.then_inc(second, 1)
            pe.wait_ge(packed, 1)
            for g in range(GROUPS):
                mm = nc.tensor.transpose(banks[6][:, g * P:(g + 1) * P], pack[:, g, :], ident[:, :])
            mm.then_inc(packT, 1)

        @block.scalar
        def _(act):
            for n in range(KINDS * NT // 4):
                act.wait_ge(transposed, n + 1)
                j, t0 = divmod(4 * n, NT)
                nc.scalar.copy(kvT[:, j, t0 * P:(t0 + 4) * P], banks[n][:, :]).then_inc(copied, 1)
            act.wait_ge(bias_set, 1)
            for n in range(KINDS * GROUPS):
                act.wait_ge(first, n + 1)
                j = n // GROUPS
                nc.scalar.activation(pre[:, n, 0:NW], banks[1 + n][0:HEAD, 0:NW], ACT.Identity,
                                     bias=bias[:, j:j + 1]).then_inc(biased, 1)
            for n in range(KINDS * GROUPS):
                act.wait_ge(biased, n + 1)
                nc.scalar.activation(den[:, n, 0:NW], pre[:, n, 0:NW], ACT.Exp, scale=-1.0).then_inc(exp_done, 1)

        @block.vector
        def _(dve):
            link = chain(dve, dve_done)
            dve.wait_ge(pe_T, 1)
            for j in range(KINDS):
                copy = nc.vector.tensor_copy(peT[:, j, :], banks[0][j * HEAD:(j + 1) * HEAD, 0:CMP_LEN])
            copy.then_inc(pe_copied, 1)
            dve.wait_ge(bias_sum, 1)
            nc.vector.tensor_copy(bias[:, :], banks[0][0:HEAD, P:P + KINDS]).then_inc(bias_set, 1)
            dve.wait_ge(exp_done, KINDS * GROUPS)
            link(nc.vector.tensor_scalar(den[:, :, 0:NW], den[:, :, 0:NW], 1.0, None, ALU.add))
            link(nc.vector.reciprocal(den[:, :, 0:NW], den[:, :, 0:NW]))
            nc.vector.tensor_tensor(act_out[:, :, 0:NW], den[:, :, 0:NW], pre[:, :, 0:NW], ALU.mult)\
                .then_inc(silu_done, 1)
            dve.wait_ge(second, 1)
            dve.wait_ge(loaded, TOTAL)
            out = banks[5][0:NW, 0:KINDS * GROUPS * HEAD].rearrange("p (j g d) -> p j g d", j=KINDS, g=GROUPS)
            nc.vector.tensor_copy(values[0:NW, :, 0:HEAD], out[:, 1, :, :])
            link(nc.vector.tensor_copy(kc[0:NW, :, :], out[:, 0, :, :]))
            link(nc.vector.memset(ssq[:, :], 1.0))
            link(nc.vector.tensor_tensor(sq[0:NW, :, :], kc[0:NW, :, :], kc[0:NW, :, :], ALU.mult))
            nc.vector.tensor_reduce(ssq[0:NW, :], sq[0:NW, :, :], AX_X, ALU.add).then_inc(squares, 1)
            dve.wait_ge(powered, 1)
            link(nc.vector.tensor_tensor(kc[0:NW, :, :], kc[0:NW, :, :],
                                         rstd[0:NW, :].unsqueeze(2).to_broadcast([NW, GROUPS, HEAD]), ALU.mult))
            link(nc.vector.tensor_tensor(kc[0:NW, :, :], kc[0:NW, :, :],
                                         gain[0:NW, :].unsqueeze(1).to_broadcast([NW, GROUPS, HEAD]), ALU.mult))
            link(nc.vector.tensor_copy(pack[0:NW, :, HEAD:].bitcast(F32R), kc[0:NW, :, :]))
            nc.vector.tensor_tensor(pack[0:NW, :, 0:HEAD].bitcast(F32R), kc[0:NW, :, :], pack[0:NW, :, HEAD:],
                                    ALU.subtract).then_inc(packed, 1)
            dve.wait_ge(packT, 1)
            bank = banks[6][:, 0:GROUPS * P].rearrange("p (g n) -> p g n", g=GROUPS)
            nc.vector.tensor_copy(keys_b[:, :, :], bank)
            link(nc.vector.tensor_copy(keys_a[0:HEAD, :, :], bank[HEAD:P, :, :]))


CMP, SLC, WIN = 0, 1, 2
VCOLS = {CMP: HEAD + 1 + 32, WIN: HEAD + 1, SLC: HEAD + 1}
WIN_TILES = 256 // P + 1
PIECES = 7


class Plan:

    def __init__(self, tiles):
        self.steps = []
        self.scores_n = {}
        self.maxima_n = {}
        self.probs_n = {}
        self.output_n = {}
        units = tiles * GROUPS
        for piece in range(PIECES):
            self.steps.append(("prep", 0, piece))
        self.front(0)
        for fill in self.max_fills(0, SLC):
            self.maximum(0, SLC, fill)
        self.row(0, SLC)
        for u in range(units):
            i, g = divmod(u, GROUPS)
            extra = []
            if g == 0 and i + 1 < tiles:
                extra += [("prep", i + 1, piece) for piece in range(PIECES)]
            if u + 1 < units:
                self.front(u + 1)
                fills = [("maximum", u + 1, SLC, fill) for fill in self.max_fills(u + 1, SLC)]
                extra = [s for pair in zip(fills, extra) for s in pair] + fills[len(extra):] + extra[len(fills):]
            taken = 0
            for j in range(i + 1):
                self.scores(u, SLC, j)
                if j > 0:
                    self.values(u, SLC, j - 1)
                until = len(extra) * (j + 1) // (i + 1)
                for s in extra[taken:until]:
                    self.add(s)
                taken = until
            self.values(u, SLC, i)
            if u + 1 < units:
                self.row(u + 1, SLC)
            self.steps.append(("post", u, SLC))

    @staticmethod
    def max_fills(u, branch):
        i = u // GROUPS
        if branch == SLC:
            return [(h, c) for h in range(HPG) for c in range(i // 4 + 1)]
        return [(h, 0) for h in range(HPG)] if branch == WIN else [(0, 0)]

    @staticmethod
    def key_tiles(u, branch):
        i = u // GROUPS
        return [0] if branch == CMP else range(max(0, i - WIN_TILES + 1) if branch == WIN else 0, i + 1)

    def add(self, s):
        if s[0] == "maximum":
            self.maximum(*s[1:])
        else:
            self.steps.append(s)

    def maximum(self, u, branch, fill):
        self.maxima_n[u, branch, fill] = len(self.maxima_n)
        self.steps.append(("maximum", u, branch, fill))

    def row(self, u, branch):
        self.scores_n[u, branch, "row"] = len(self.scores_n)
        self.steps.append(("row", u, branch))

    def scores(self, u, branch, j):
        self.scores_n[u, branch, j] = len(self.scores_n)
        self.probs_n[u, branch, j] = len(self.probs_n)
        self.output_n.setdefault((u, branch), len(self.output_n))
        self.steps.append(("scores", u, branch, j))

    def values(self, u, branch, j):
        self.steps.append(("values", u, branch, j))

    def front(self, u):
        for branch in (CMP, WIN):
            for fill in self.max_fills(u, branch):
                self.maximum(u, branch, fill)
        self.row(u, CMP)
        self.row(u, WIN)
        window = list(self.key_tiles(u, WIN))
        self.scores(u, CMP, 0)
        self.scores(u, WIN, window[0])
        self.values(u, CMP, 0)
        self.steps.append(("post", u, CMP))
        for a, b in zip(window, window[1:]):
            self.scores(u, WIN, b)
            self.values(u, WIN, a)
        self.values(u, WIN, window[-1])
        self.maxima_n[u, "select"] = len(self.maxima_n)
        self.steps.append(("select", u))
        self.steps.append(("post", u, WIN))


def mixers_phase(nc, z, conv_w, q_gain, k_gain, tables, cmp_a, cmp_b, cmp_v, mixed_out):
    S = z.shape[0]
    NT = S // P
    NBLK = S // SLC_LEN
    plan = Plan(NT)
    RW = RET_HEADS * HEAD
    CW = CC - CB_
    WR = WIN_TILES + 1
    PR = 4
    LOADS = 5
    CMP_ROW, WIN_ROW = 64, 96

    with ExitStack() as stack:
        m = Space(nc, stack, "mix")
        ident = m.sb("ident", [P, P])
        ident_bf = m.sb("ident_bf", [P, P], BF16)
        ones_f = m.sb("ones_f", [P, P])
        ones = m.sb("ones", [P, P], F32R)
        cmp_mask = m.sb("cmp_mask", [P, S], BF16)
        causal = m.sb("causal", [P, P], BF16)
        beyond = m.sb("beyond", [P, P], BF16)
        block_rows = m.sb("block_rows", [P, S])
        decay = m.sb("decay", [P, RET_HEADS, P])
        row_decay = m.sb("row_decay", [P, 3, RET_HEADS])
        conv_taps = m.sb("conv_taps", [P, 3, CW])
        q_gains = m.sb("q_gains", [P, HEAD])
        k_gains = m.sb("k_gains", [P, HEAD])
        neg_half = m.sb("neg_half", [P, 16])
        zt = m.sb("z", [P, 2, z.shape[1]])
        shifted = m.sb("shifted", [P, 2, 2, 2 * CW])
        rot = m.sb("rot", [P, 2, 2, HEAD])
        sel_table = m.sb("sel_table", [P, 2, 3, NBLK])
        mixed = m.sb("mixed", [P, 2, 2 * RW + NSA_HEADS * HEAD])
        r1 = m.sb("r1", [P, 8, HEAD])
        r2 = m.sb("r2", [P, 8, HEAD])
        qq = m.sb("qq", [P, RET_HEADS, P])
        kz = m.sb("kz", [P, RET_HEADS, P])
        zk = m.sb("zk", [P, RET_HEADS, P])
        qqT = m.sb("qqT", [P, RET_HEADS, P])
        kzT = m.sb("kzT", [P, RET_HEADS, P])
        ret_scores = m.sb("ret_scores", [P, RET_HEADS, P])
        state = m.sb("state", [P, RET_HEADS, HEAD])
        o_ret = m.sb("o_ret", [P, RET_HEADS, HEAD])
        o_sq = m.sb("o_sq", [P, RET_HEADS, HEAD])
        o_mean = m.sb("o_mean", [P, RET_HEADS])
        o_ssq = m.sb("o_ssq", [P, RET_HEADS])
        o_rstd = m.sb("o_rstd", [P, RET_HEADS])
        swish = m.sb("swish", [P, 2, RW])
        gates = m.sb("gates", [P, 2, 3 * NSA_HEADS])
        taps = m.sb("taps", [P, 3, CW])
        sq = m.sb("sq", [P, NSA_HEADS + 2 * GROUPS, HEAD])
        ssq = m.sb("ssq", [P, NSA_HEADS + 2 * GROUPS])
        mean = m.sb("mean", [P, NSA_HEADS + 2 * GROUPS])
        rstd = m.sb("rstd", [P, NSA_HEADS + 2 * GROUPS])
        qn = m.sb("qn", [P, NSA_HEADS, HEAD])
        kn = m.sb("kn", [P, 2 * GROUPS, HEAD])
        q_pack = m.sb("q_pack", [P, NSA_HEADS, P])
        k_pack = m.sb("k_pack", [P, 2 * GROUPS, P])
        qb = m.sb("qb", [P, 2, NSA_HEADS, P], F32R)
        qa_cw = m.sb("qa_cw", [P, 2, NSA_HEADS, P], F32R)
        qa_s = m.sb("qa_s", [P, 2, NSA_HEADS, P], F32R)
        ka_s = m.sb("ka_s", [P, GROUPS, S], F32R)
        kb_s = m.sb("kb_s", [P, GROUPS, S], F32R)
        ka_w = m.sb("ka_w", [P, GROUPS, WR * P], F32R)
        kb_w = m.sb("kb_w", [P, GROUPS, WR * P], F32R)
        v_s = m.sb("v_s", [P, NT, GROUPS, HEAD + 1])
        v_w = m.sb("v_w", [P, WR, GROUPS, HEAD + 1])
        probs = m.sb("probs", [P, PR, HPG * P])
        part_max = m.sb("part_max", [P, HPG, NT // 4])
        top = m.sb("top", [P, HPG])
        neg_max = m.sb("neg_max", [P, HPG])
        diag = [m.sb(f"diag{br}", [P, HPG, P], F32R) for br in range(3)]
        den = m.sb("den", [P, HPG])
        weight = m.sb("weight", [P, HPG])
        importance = m.sb("importance", [P, HPG, NBLK])
        sel_score = m.sb("sel_score", [P, NBLK])
        best = m.sb("best", [P, TOPK])
        chosen = m.sb("chosen", [P, NBLK])
        selection = m.sb("selection", [P, P])
        weighted = m.sb("weighted", [P, HPG, HEAD])

        score_ps = [m.ps(f"score{b}", [P, BANK]) for b in range(2)]
        maxima_ps = [m.ps(f"maxima{b}", [P, BANK]) for b in range(2)]
        output_ps = [m.ps(f"output{b}", [P, BANK]) for b in range(2)]
        prep_ps = [m.ps(f"prep{b}", [P, BANK]) for b in range(2)]

        const_in = m.sem("const_in")
        const_set = m.sem("const_set")
        const_cast = m.sem("const_cast")
        tile_in = m.sems("tile_in", 2)
        mixed_stored = m.sems("mixed_stored", 2)
        v_ready = m.sem("v_ready")
        rot_ready = m.sem("rot_ready")
        squared = m.sem("squared")
        exps_ready = m.sem("exps_ready")
        ssq_ready = m.sem("ssq_ready")
        gates_ready = m.sem("gates_ready")
        rstd_ready = m.sem("rstd_ready")
        normed = m.sem("normed")
        high_ready = m.sem("high_ready")
        packs_ready = m.sem("packs_ready")
        prep_sum = m.sem("prep_sum")
        prep_read_act = m.sem("prep_read_act")
        prep_read_dve = m.sem("prep_read_dve")
        o_ready = m.sem("o_ready")
        o_squared = m.sem("o_squared")
        o_ssq_ready = m.sem("o_ssq_ready")
        pool_mixed = m.sem("pool_mixed")
        diag_ready = [m.sem(f"diag_ready{br}") for br in range(3)]
        score_sum = m.sem("score_sum")
        score_read = m.sem("score_read")
        maxima_sum = m.sem("maxima_sum")
        maxima_read = m.sem("maxima_read")
        probs_used = m.sem("probs_used")
        output_read = m.sem("output_read")
        sel_ready = m.sem("sel_ready")
        nsa_mixed = m.sem("nsa_mixed")
        dve_done = m.sem("dve_done")
        pool_done = m.sem("pool_done")

        CONSTS = 9
        block = stack.enter_context(nc.Block())

        def tile_loaded(eng, i):
            eng.wait_ge(tile_in[i % 2], 16 * LOADS * (i // 2 + 1))

        def prep_read(eng, f):
            i, k = divmod(f, 7)
            if k in (2, 3):
                eng.wait_ge(prep_read_dve, 2 * i + k - 1)
            else:
                eng.wait_ge(prep_read_act, 5 * i + (k if k < 2 else k - 2) + 1)

        def last_use(eng, u, branch):
            eng.wait_ge(probs_used, plan.probs_n[u, branch, plan.key_tiles(u, branch)[-1]] + 1)

        @block.sync
        def _(sp):
            sp.dma_start(ident[:, :], tables["identity"]).then_inc(const_in, 16)
            sp.dma_start(block_rows[64:64 + NBLK, :], tables["block_rows"]).then_inc(const_in, 16)
            sp.dma_start(decay[:, :, :], tables["decay"]).then_inc(const_in, 16)
            sp.dma_start(row_decay[:, :, :], tables["row_decay"]).then_inc(const_in, 16)
            for k in range(3):
                sp.dma_start(conv_taps[:, k, :], conv_w[k].partition_broadcast(P)).then_inc(const_in, 16)
            sp.dma_start(q_gains[:, :], q_gain.partition_broadcast(P)).then_inc(const_in, 16)
            sp.dma_start(k_gains[:, :], k_gain.partition_broadcast(P)).then_inc(const_in, 16)
            sp.wait_ge(const_set, 1)

            def load(i):
                b, rows = i % 2, slice(i * P, (i + 1) * P)
                if i >= 2:
                    sp.wait_ge(pool_mixed, i - 1)
                    sp.wait_ge(packs_ready, i - 1)
                    sp.wait_ge(gates_ready, i - 1)
                    sp.wait_ge(exps_ready, i - 1)
                    sp.wait_ge(prep_sum, 7 * (i - 1))
                    sp.wait_ge(sel_ready, GROUPS * (i - 1))
                sp.dma_start(zt[:, b, :], z[rows, :]).then_inc(tile_in[b], 16)
                for s in (1, 2):
                    cut = s if i == 0 else 0
                    sp.dma_start(shifted[cut:, b, s - 1, :], z[i * P - s + cut:(i + 1) * P - s, CC:CC + 2 * CW])\
                        .then_inc(tile_in[b], 16)
                sp.dma_start(rot[:, b, :, :], tables["rotation"][rows, :, :]).then_inc(tile_in[b], 16)
                sp.dma_start(sel_table[:, b, :, :], tables["selection"][rows, :, :]).then_inc(tile_in[b], 16)

            load(0)
            load(1)
            for i in range(NT):
                sp.wait_ge(pool_mixed, i + 1)
                sp.wait_ge(nsa_mixed, GROUPS * (i + 1))
                sp.dma_start(mixed_out[i * P:(i + 1) * P, :], mixed[:, i % 2, :]).then_inc(mixed_stored[i % 2], 16)
                if i + 2 < NT:
                    load(i + 2)
            for b in range(2):
                sp.wait_ge(mixed_stored[b], 16 * (NT // 2))

        @block.gpsimd
        def _(pool):
            link = chain(pool, pool_done)

            def mask(tensor, pattern, base, channel):
                link(nc.gpsimd.memset(tensor[:, :], 0.0))
                link(nc.gpsimd.affine_select(out=tensor[:, :], in_=tensor[:, :], compare_op=ALU.is_ge,
                                             fill=MASKED, base=base, pattern=pattern,
                                             channel_multiplier=channel))

            link(nc.gpsimd.memset(shifted[:, 0, :, :], 0.0))
            link(nc.gpsimd.memset(neg_half[:, :], -0.5))
            link(nc.gpsimd.memset(kz[:, :, :], 0.0))
            link(nc.gpsimd.memset(zk[:, :, :], 0.0))
            link(nc.gpsimd.memset(state[:, :, :], 0.0))
            link(nc.gpsimd.memset(selection[:, :], 0.0))
            link(nc.gpsimd.memset(ones_f[:, :], 1.0))
            link(nc.gpsimd.memset(v_s[:, :, :, HEAD:], 1.0))
            link(nc.gpsimd.memset(v_w[:, :, :, HEAD:], 1.0))
            for t in (qa_cw, qa_s):
                link(nc.gpsimd.memset(t[64:, :, :, :].bitcast(F32), 0.0))
            link(nc.gpsimd.memset(ka_w[64:, :, :].bitcast(F32), 0.0))
            link(nc.gpsimd.memset(ka_w[WIN_ROW:WIN_ROW + 1, :, :].bitcast(F32), 1.0))
            link(nc.gpsimd.memset(ka_s[WIN_ROW:WIN_ROW + 1, :, :].bitcast(F32), 1.0))
            link(nc.gpsimd.memset(cmp_a[64:, :, :].bitcast(F32), 0.0))
            link(nc.gpsimd.memset(cmp_a[CMP_ROW:CMP_ROW + 1, :, :].bitcast(F32), 1.0))
            mask(cmp_mask, [[1, S]], -(CMP_LEN - 1), -STRIDE)
            mask(causal, [[1, P]], 0, -1)
            mask(beyond, [[-1, P]], -1, 1)
            link(nc.gpsimd.memset(ident_bf[:, :], 0.0))
            nc.gpsimd.affine_select(out=ident_bf[:, :], in_=ident_bf[:, :], compare_op=ALU.not_equal,
                                    fill=1.0, base=0, pattern=[[-1, P]], channel_multiplier=1)\
                .then_inc(const_set, 1)
            pool.wait_ge(const_in, 16 * CONSTS)
            pool.wait_ge(const_set, 1)

            def bc(ap, n):
                return ap.unsqueeze(2).to_broadcast([P, ap.shape[1], n])

            for i in range(NT):
                b = i % 2
                tile_loaded(pool, i)
                if i >= WR:
                    last_use(pool, GROUPS * (i - WR) + GROUPS - 1, WIN)
                nc.gpsimd.tensor_copy(v_w[:, i % WR, :, 0:HEAD],
                                      zt[:, b, NVW:NVW + P].rearrange("p (g d) -> p g d", g=GROUPS))\
                    .then_inc(v_ready, 1)
                nc.gpsimd.tensor_copy(v_s[:, i, :, 0:HEAD],
                                      zt[:, b, NVS:NVS + P].rearrange("p (g d) -> p g d", g=GROUPS))\
                    .then_inc(v_ready, 1)
                if i >= 1:
                    pool.wait_ge(prep_sum, 7 * (i - 1) + 4)
                x = zt[:, b, 0:2 * RW].rearrange("p (h d) -> p h d", d=HEAD)
                xp = x.rearrange("p h (e two) -> p h e two", two=2)
                cos = rot[:, b, 0, :].unsqueeze(1).to_broadcast([P, 8, HEAD])
                sin = rot[:, b, 1, :].rearrange("p (e two) -> p e two", two=2)
                link(nc.gpsimd.tensor_tensor(r1[:, :, :], x, cos, ALU.mult))
                r2p = r2[:, :, :].rearrange("p h (e two) -> p h e two", two=2)
                for a in range(2):
                    link(nc.gpsimd.tensor_tensor(r2p[:, :, :, a], xp[:, :, :, 1 - a],
                                                 sin[:, :, a].unsqueeze(1).to_broadcast([P, 8, HEAD // 2]),
                                                 ALU.mult))
                link(nc.gpsimd.tensor_tensor(qq[:, :, 0:HEAD], r1[:, 0:4, :], r2[:, 0:4, :], ALU.add))
                link(nc.gpsimd.tensor_tensor(kz[:, :, 0:HEAD], r1[:, 4:8, :], r2[:, 4:8, :], ALU.add))
                link(nc.gpsimd.tensor_tensor(qq[:, :, HEAD:], qq[:, :, 0:HEAD], bc(row_decay[:, 0, :], HEAD), ALU.mult))
                nc.gpsimd.tensor_tensor(zk[:, :, HEAD:], kz[:, :, 0:HEAD], bc(row_decay[:, 1, :], HEAD), ALU.mult)\
                    .then_inc(rot_ready, 1)
                pool.wait_ge(ssq_ready, i + 1)
                if i >= 1:
                    pool.wait_ge(normed, i)
                link(nc.gpsimd.tensor_scalar(mean[:, :], ssq[:, :], 1.0 / HEAD, EPS, ALU.mult, ALU.add))
                nc.gpsimd.tensor_tensor(rstd[:, :], mean[:, :], neg_half[:, 0:NSA_HEADS + 2 * GROUPS],
                                        ALU.pow).then_inc(rstd_ready, 1)
                for k in range(3):
                    src = zt[:, b, CC:CC + 2 * CW] if k == 2 else shifted[:, b, 1 - k, :]
                    link(nc.gpsimd.tensor_tensor(taps[:, k, :], src[:, 0:CW], src[:, CW:], ALU.mult))
                link(nc.gpsimd.tensor_tensor(taps[:, :, :], taps[:, :, :], conv_taps[:, :, :], ALU.mult))
                link(nc.gpsimd.tensor_tensor(taps[:, 0, :], taps[:, 0, :], taps[:, 1, :], ALU.add))
                link(nc.gpsimd.tensor_tensor(taps[:, 0, :], taps[:, 0, :], taps[:, 2, :], ALU.add))
                if i >= 2:
                    pool.wait_ge(mixed_stored[b], 16 * (i // 2))
                link(nc.gpsimd.tensor_tensor(mixed[:, b, RW:RW + CW], taps[:, 0, :], zt[:, b, CB_:CB_ + CW], ALU.mult))
                pool.wait_ge(o_ready, i + 1)
                nc.gpsimd.tensor_tensor(o_sq[:, :, :], o_ret[:, :, :], o_ret[:, :, :], ALU.mult).then_inc(o_squared, 1)
                pool.wait_ge(o_ssq_ready, i + 1)
                link(nc.gpsimd.tensor_scalar(o_mean[:, :], o_ssq[:, :], 1.0 / HEAD, EPS, ALU.mult, ALU.add))
                link(nc.gpsimd.tensor_tensor(o_rstd[:, :], o_mean[:, :], neg_half[:, 0:RET_HEADS], ALU.pow))
                link(nc.gpsimd.tensor_tensor(o_sq[:, :, :], o_ret[:, :, :], bc(o_rstd[:, :], HEAD), ALU.mult))
                pool.wait_ge(gates_ready, i + 1)
                nc.gpsimd.tensor_tensor(mixed[:, b, 0:RW], o_sq[:, :, :].rearrange("p h d -> p (h d)"),
                                        swish[:, b, :], ALU.mult).then_inc(pool_mixed, 1)

        @block.scalar
        def _(act):
            act.wait_ge(const_in, 16 * CONSTS)
            act.wait_ge(const_set, 1)
            nc.scalar.copy(ones[:, :], ones_f[:, :])
            for g in range(GROUPS):
                nc.scalar.copy(ka_s[64:64 + NBLK, g, :], block_rows[64:64 + NBLK, :])
            nc.scalar.mul(q_gains[:, :], q_gains[:, :], HEAD ** -0.5).then_inc(const_cast, 1)
            act.wait_ge(const_cast, 1)

            for step in plan.steps:
                kind, u = step[0], step[1]
                if kind == "prep":
                    i, piece = step[1:]
                    b = i % 2
                    if piece == 0:
                        tile_loaded(act, i)
                        if i >= 1:
                            act.wait_ge(ssq_ready, i)
                        nc.scalar.activation(sq[:, 0:NSA_HEADS, :].rearrange("p h d -> p (h d)"),
                                             zt[:, b, NQ:NQ + NSA_HEADS * HEAD], ACT.Square)
                        nc.scalar.activation(
                            sq[:, NSA_HEADS:, :].rearrange("p (k g) d -> p k (g d)", k=2),
                            zt[:, b, NKS:NKS + 4 * P].rearrange("p (k c) -> p k c", k=2)[:, :, 0:P],
                            ACT.Square).then_inc(squared, 1)
                        if i >= 2:
                            act.wait_ge(pool_mixed, i - 1)
                            act.wait_ge(nsa_mixed, GROUPS * (i - 1))
                        nc.scalar.activation(swish[:, b, :], zt[:, b, RG:RG + RW], ACT.Exp, scale=-1.0)
                        nc.scalar.activation(gates[:, b, :], zt[:, b, NG:NG + 3 * NSA_HEADS], ACT.Exp,
                                             scale=-1.0).then_inc(exps_ready, 1)
                    elif piece == 1:
                        act.wait_ge(normed, i + 1)
                        if i >= 1:
                            act.wait_ge(prep_sum, 7 * i)
                        nc.scalar.copy(q_pack[:, :, 0:HEAD].bitcast(F32R), qn[:, :, :])
                        nc.scalar.copy(k_pack[:, :, HEAD:].bitcast(F32R), kn[:, :, :]).then_inc(high_ready, 1)
                        for f, dst in enumerate((qqT, kzT)):
                            act.wait_ge(prep_sum, 7 * i + f + 1)
                            nc.scalar.copy(dst[:, :, :].rearrange("p h c -> p (h c)"),
                                           prep_ps[(7 * i + f) % 2][:, :]).then_inc(prep_read_act, 1)
                    elif piece == 4:
                        act.wait_ge(prep_sum, 7 * i + 5)
                        if i >= WR:
                            last_use(act, GROUPS * (i - WR) + GROUPS - 1, WIN)
                        bank = prep_ps[(7 * i + 4) % 2][:, :].rearrange("p (k g c) -> p k g c", k=2, g=GROUPS)
                        s, w = slice(i * P, (i + 1) * P), slice(i % WR * P, (i % WR + 1) * P)
                        nc.scalar.copy(kb_s[:, :, s], bank[:, 0, :, :])
                        nc.scalar.copy(kb_w[:, :, w], bank[:, 1, :, :])
                        nc.scalar.copy(ka_s[0:HEAD, :, s], bank[HEAD:, 0, :, :])
                        nc.scalar.copy(ka_w[0:HEAD, :, w], bank[HEAD:, 1, :, :]).then_inc(prep_read_act, 1)
                    elif piece == 5:
                        if i >= 2:
                            last_use(act, GROUPS * (i - 2) + GROUPS - 1, SLC)
                        for half in range(2):
                            f = 7 * i + 5 + half
                            act.wait_ge(prep_sum, f + 1)
                            bank = prep_ps[f % 2][:, :].rearrange("p (h c) -> p h c", h=HPG)
                            h = slice(half * HPG, (half + 1) * HPG)
                            nc.scalar.copy(qb[:, b, h, :], bank)
                            nc.scalar.copy(qa_cw[0:HEAD, b, h, :], bank[0:HEAD, :, :])
                            nc.scalar.copy(qa_s[0:HEAD, b, h, :], bank[0:HEAD, :, :]).then_inc(prep_read_act, 1)
                elif kind == "row":
                    branch = step[2]
                    n = plan.scores_n[u, branch, "row"]
                    b, g = u // GROUPS % 2, u % GROUPS
                    row = CMP_ROW if branch == CMP else WIN_ROW
                    q = qa_s if branch == SLC else qa_cw
                    act.wait_ge(score_sum, n + 1)
                    nc.scalar.copy(q[row:row + 1, b, g * HPG:(g + 1) * HPG, :],
                                   score_ps[n % 2][row:row + 1, :].rearrange("p (h c) -> p h c", h=HPG))\
                        .then_inc(score_read, 1)
                elif kind == "scores":
                    n, p = plan.scores_n[step[1:]], plan.probs_n[step[1:]]
                    act.wait_ge(score_sum, n + 1)
                    if p >= PR:
                        act.wait_ge(probs_used, p - PR + 1)
                    nc.scalar.activation(probs[:, p % PR, :], score_ps[n % 2][:, :], ACT.Exp)\
                        .then_inc(score_read, 1)

        @block.vector
        def _(dve):
            link = chain(dve, dve_done)
            dve.wait_ge(const_set, 1)
            dve.wait_ge(const_cast, 1)

            def bc(ap, n):
                return ap.unsqueeze(2).to_broadcast([P, ap.shape[1], n])

            def maxima_done(u, branch):
                link(nc.vector.tensor_scalar(neg_max[:, :], top[:, :], MASKED / 10, -1.0, ALU.max, ALU.mult))
                if u > 0:
                    dve.wait_ge(score_sum, plan.scores_n[u - 1, branch, "row"] + 1)
                nc.vector.tensor_tensor(diag[branch][:, :, :], ident[:, :].unsqueeze(1).to_broadcast([P, HPG, P]),
                                        bc(neg_max[:, :], P), ALU.mult).then_inc(diag_ready[branch], 1)
                dve.wait_ge(diag_ready[branch], u + 1)

            for step in plan.steps:
                kind, u = step[0], step[1]
                if kind == "prep":
                    i, piece = step[1:]
                    b = i % 2
                    f = 7 * i + piece
                    if piece == 0:
                        dve.wait_ge(squared, i + 1)
                        if i >= 1:
                            dve.wait_ge(rstd_ready, i)
                        nc.vector.tensor_reduce(ssq[:, :], sq[:, :, :], AX_X, ALU.add).then_inc(ssq_ready, 1)
                        dve.wait_ge(exps_ready, i + 1)
                        for t in (swish, gates):
                            link(nc.vector.tensor_scalar(t[:, b, :], t[:, b, :], 1.0, None, ALU.add))
                            link(nc.vector.reciprocal(t[:, b, :], t[:, b, :]))
                        nc.vector.tensor_tensor(swish[:, b, :], swish[:, b, :], zt[:, b, RG:RG + RW],
                                                ALU.mult).then_inc(gates_ready, 1)
                    elif piece == 1:
                        dve.wait_ge(rstd_ready, i + 1)
                        H = NSA_HEADS
                        q = zt[:, b, NQ:NQ + H * HEAD].rearrange("p (h d) -> p h d", h=H)
                        if i >= 1:
                            dve.wait_ge(packs_ready, i)
                        link(nc.vector.tensor_tensor(qn[:, :, :], q, bc(rstd[:, 0:H], HEAD), ALU.mult))
                        for k, c in enumerate((NKS, NKW)):
                            part = slice(GROUPS * k, GROUPS * (k + 1))
                            link(nc.vector.tensor_tensor(
                                kn[:, part, :], zt[:, b, c:c + P].rearrange("p (g d) -> p g d", g=GROUPS),
                                bc(rstd[:, H + GROUPS * k:H + GROUPS * (k + 1)], HEAD), ALU.mult))
                        link(nc.vector.tensor_tensor(kn[:, :, :], kn[:, :, :],
                                                     k_gains[:, :].unsqueeze(1).to_broadcast([P, 2 * GROUPS, HEAD]),
                                                     ALU.mult))
                        nc.vector.tensor_tensor(qn[:, :, :], qn[:, :, :],
                                                q_gains[:, :].unsqueeze(1).to_broadcast([P, H, HEAD]),
                                                ALU.mult).then_inc(normed, 1)
                        dve.wait_ge(high_ready, i + 1)
                        nc.vector.tensor_tensor(k_pack[:, :, 0:HEAD].bitcast(F32R), kn[:, :, :], k_pack[:, :, HEAD:],
                                                ALU.subtract)
                        nc.vector.tensor_tensor(q_pack[:, :, HEAD:].bitcast(F32R), qn[:, :, :], q_pack[:, :, 0:HEAD],
                                                ALU.subtract).then_inc(packs_ready, 1)
                    elif piece == 2:
                        dve.wait_ge(prep_sum, f + 1)
                        nc.vector.tensor_tensor(ret_scores[:, :, :].rearrange("p h c -> p (h c)"),
                                                prep_ps[f % 2][:, :], decay[:, :, :].rearrange("p h c -> p (h c)"),
                                                ALU.mult).then_inc(prep_read_dve, 1)
                    elif piece == 3:
                        dve.wait_ge(prep_sum, f + 1)
                        bank = prep_ps[f % 2][:, :].rearrange("p (two h d) -> p two h d", two=2, h=RET_HEADS)
                        if i >= 1:
                            dve.wait_ge(o_ssq_ready, i)
                            dve.wait_ge(pool_mixed, i)
                        nc.vector.tensor_copy(o_ret[:, :, :], bank[:, 0, :, :]).then_inc(o_ready, 1)
                        link(nc.vector.tensor_tensor(state[:, :, :], state[:, :, :], bc(row_decay[:, 2, :], HEAD),
                                                     ALU.mult))
                        nc.vector.tensor_tensor(state[:, :, :], state[:, :, :], bank[:, 1, :, :],
                                                ALU.add).then_inc(prep_read_dve, 1)
                        dve.wait_ge(prep_read_dve, 2 * i + 2)
                    elif piece == 6:
                        dve.wait_ge(o_squared, i + 1)
                        nc.vector.tensor_reduce(o_ssq[:, :], o_sq[:, :, :], AX_X, ALU.add).then_inc(o_ssq_ready, 1)
                elif kind == "maximum":
                    branch, (h, c) = step[2:]
                    i = u // GROUPS
                    n = plan.maxima_n[u, branch, (h, c)]
                    bank = maxima_ps[n % 2]
                    dve.wait_ge(maxima_sum, n + 1)
                    if branch == CMP:
                        ins = nc.vector.tensor_reduce(top[:, :], bank[:, :].rearrange("p (h n) -> p h n", h=HPG),
                                                      AX_X, ALU.max)
                    else:
                        keys = (len(plan.key_tiles(u, branch)) if branch == WIN else min(4, i + 1 - 4 * c)) * P
                        dst = top[:, h:h + 1] if branch == WIN else part_max[:, h, c:c + 1]
                        ins = nc.vector.tensor_reduce(dst, bank[:, 0:keys], AX_X, ALU.max)
                    ins.then_inc(maxima_read, 1)
                    if (h, c) == plan.max_fills(u, branch)[-1]:
                        dve.wait_ge(maxima_read, n + 1)
                        if branch == SLC:
                            link(nc.vector.tensor_reduce(top[:, :], part_max[:, :, 0:c + 1], AX_X, ALU.max))
                        maxima_done(u, branch)
                elif kind == "select":
                    n = plan.maxima_n[u, "select"]
                    dve.wait_ge(maxima_sum, n + 1)
                    b, g = u // GROUPS % 2, u % GROUPS
                    nc.vector.tensor_copy(qa_s[64:64 + NBLK, b, g * HPG:(g + 1) * HPG, :],
                                          maxima_ps[n % 2][64:64 + NBLK, 0:P].unsqueeze(1)
                                          .to_broadcast([NBLK, HPG, P])).then_inc(maxima_read, 1)
                elif kind == "post":
                    branch = step[2]
                    i, g = divmod(u, GROUPS)
                    b = i % 2
                    last_use(dve, u, branch)
                    out = output_ps[plan.output_n[u, branch] % 2][:, 0:HPG * VCOLS[branch]]\
                        .rearrange("p (h c) -> p h c", h=HPG)
                    dst = mixed[:, b, 2 * RW + g * HPG * HEAD:2 * RW + (g + 1) * HPG * HEAD]\
                        .rearrange("p (h d) -> p h d", h=HPG)
                    gate = gates[:, b, :].rearrange("p (h c) -> p h c", c=3)[:, g * HPG:(g + 1) * HPG, branch]
                    link(nc.vector.tensor_scalar(den[:, :], out[:, :, HEAD], 1e-30, None, ALU.max))
                    link(nc.vector.reciprocal(den[:, :], den[:, :]))
                    if branch == CMP:
                        link(nc.vector.tensor_tensor(importance[:, :, :], out[:, :, HEAD + 1:],
                                                     bc(den[:, :], NBLK), ALU.mult))
                        link(nc.vector.tensor_reduce(sel_score[:, :],
                                                     importance[:, :, :].rearrange("p h j -> p j h"),
                                                     AX_X, ALU.add))
                        for t, op in ((0, ALU.add), (1, ALU.mult), (2, ALU.add)):
                            link(nc.vector.tensor_tensor(sel_score[:, :], sel_score[:, :], sel_table[:, b, t, :], op))
                        link(nc.vector.max(best[:, :], sel_score[:, :]))
                        link(nc.vector.match_replace(chosen[:, :], best[:, :], sel_score[:, :], -3e38))
                        nc.vector.tensor_scalar(selection[:, 64:64 + NBLK], chosen[:, :], -1e38, MASKED,
                                                ALU.is_gt, ALU.mult).then_inc(sel_ready, 1)
                        dve.wait_ge(sel_ready, u + 1)
                    link(nc.vector.tensor_tensor(weight[:, :], den[:, :], gate, ALU.mult))
                    if branch == CMP:
                        if i >= 2 and g == 0:
                            dve.wait_ge(mixed_stored[b], 16 * (i // 2))
                        nc.vector.tensor_tensor(dst, out[:, :, 0:HEAD], bc(weight[:, :], HEAD), ALU.mult)\
                            .then_inc(output_read, 1)
                    else:
                        nc.vector.tensor_tensor(weighted[:, :, :], out[:, :, 0:HEAD], bc(weight[:, :], HEAD),
                                                ALU.mult).then_inc(output_read, 1)
                        dve.wait_ge(output_read, plan.output_n[u, branch] + 1)
                        add = nc.vector.tensor_tensor(dst, dst, weighted[:, :, :], ALU.add)
                        if branch == SLC:
                            add.then_inc(nsa_mixed, 1)
                            dve.wait_ge(nsa_mixed, u + 1)
                        else:
                            link(add)

        @block.tensor
        def _(pe):
            pe.wait_ge(const_in, 16 * CONSTS)
            pe.wait_ge(const_set, 1)
            pe.wait_ge(const_cast, 1)

            def prep_bank(f):
                if f >= 2:
                    prep_read(pe, f - 2)
                return prep_ps[f % 2]

            for step in plan.steps:
                kind, u = step[0], step[1]
                i, g = divmod(u, GROUPS)
                b = i % 2
                if kind == "prep":
                    i, piece = step[1:]
                    b = i % 2
                    if piece == 1:
                        pe.wait_ge(rot_ready, i + 1)
                        for f, src in enumerate((qq, kz)):
                            bank = prep_bank(7 * i + f)
                            for h in range(RET_HEADS):
                                mm = nc.tensor.transpose(bank[:, h * P:(h + 1) * P], src[:, h, :], ident[:, :])
                            mm.then_inc(prep_sum, 1)
                    elif piece == 2:
                        bank = prep_bank(7 * i + 2)
                        prep_read(pe, 7 * i + 1)
                        for h in range(RET_HEADS):
                            mm = nc.tensor.matmul(bank[:, h * P:(h + 1) * P], kzT[:, h, :], qqT[:, h, :],
                                                  start=True, stop=True)
                        mm.then_inc(prep_sum, 1)
                    elif piece == 3:
                        bank = prep_bank(7 * i + 3)
                        prep_read(pe, 7 * i + 2)
                        for h in range(RET_HEADS):
                            v = zt[:, b, RV + h * HEAD:RV + (h + 1) * HEAD]
                            o = bank[:, h * HEAD:(h + 1) * HEAD]
                            nc.tensor.matmul(o, ret_scores[:, h, :], v, start=True, stop=False)
                            nc.tensor.matmul(o, qqT[:, h, :], state[:, h, :], start=False, stop=True)
                            mm = nc.tensor.matmul(bank[:, RW + h * HEAD:RW + (h + 1) * HEAD], zk[:, h, :], v,
                                                  start=True, stop=True)
                        mm.then_inc(prep_sum, 1)
                    elif piece == 4:
                        bank = prep_bank(7 * i + 4)
                        pe.wait_ge(packs_ready, i + 1)
                        for k in range(2 * GROUPS):
                            mm = nc.tensor.transpose(bank[:, k * P:(k + 1) * P], k_pack[:, k, :], ident[:, :])
                        mm.then_inc(prep_sum, 1)
                    elif piece == 5:
                        for half in range(2):
                            bank = prep_bank(7 * i + 5 + half)
                            for h in range(HPG):
                                mm = nc.tensor.transpose(bank[:, h * P:(h + 1) * P], q_pack[:, half * HPG + h, :],
                                                         ident[:, :])
                            mm.then_inc(prep_sum, 1)
                elif kind == "maximum":
                    branch, (h, c) = step[2:]
                    n = plan.maxima_n[u, branch, (h, c)]
                    bank = maxima_ps[n % 2]
                    if n >= 2:
                        pe.wait_ge(maxima_read, n - 1)
                    if branch == CMP:
                        prep_read(pe, 7 * i + 6)
                        mm = nc.tensor.matmul(bank[:, :], cmp_mask[:, i * P:(i + 1) * P],
                                              ident_bf[:, :].unsqueeze(1).to_broadcast([P, HPG, P]),
                                              start=True, stop=False, skip_group_check=True)
                        for h in range(HPG):
                            mm = nc.tensor.matmul(bank[:, h * P:(h + 1) * P], qb[0:HEAD, b, g * HPG + h, :],
                                                  cmp_a[0:HEAD, g, :], start=False, stop=h == HPG - 1,
                                                  skip_group_check=True)
                    elif branch == WIN:
                        for s, j in enumerate(plan.key_tiles(u, WIN)):
                            out = bank[:, s * P:(s + 1) * P]
                            mask = {i: causal, i - 2: beyond}.get(j)
                            mm = nc.tensor.matmul(out, qb[0:HEAD, b, g * HPG + h, :],
                                                  ka_w[0:HEAD, g, j % WR * P:(j % WR + 1) * P],
                                                  start=True, stop=mask is None)
                            if mask is not None:
                                mm = nc.tensor.matmul(out, mask[:, :], ident_bf[:, :], start=False, stop=True)
                    else:
                        if (h, c) == (0, 0):
                            pe.wait_ge(maxima_read, plan.maxima_n[u, "select"] + 1)
                        keys = min(4, i + 1 - 4 * c) * P
                        own = i // 4 == c
                        mm = nc.tensor.matmul(bank[:, 0:keys], qa_s[0:96, b, g * HPG + h, :],
                                              ka_s[0:96, g, 4 * c * P:4 * c * P + keys],
                                              start=True, stop=not own, skip_group_check=True)
                        if own:
                            mm = nc.tensor.matmul(bank[:, keys - P:keys], causal[:, :], ident_bf[:, :],
                                                  start=False, stop=True, skip_group_check=True)
                    mm.then_inc(maxima_sum, 1)
                elif kind == "select":
                    n = plan.maxima_n[u, "select"]
                    pe.wait_ge(sel_ready, u + 1)
                    if n >= 2:
                        pe.wait_ge(maxima_read, n - 1)
                    nc.tensor.transpose(maxima_ps[n % 2][:, 0:P], selection[:, :], ident[:, :]).then_inc(maxima_sum, 1)
                elif kind == "row":
                    branch = step[2]
                    n = plan.scores_n[u, branch, "row"]
                    if n >= 2:
                        pe.wait_ge(score_read, n - 1)
                    pe.wait_ge(diag_ready[branch], u + 1)
                    nc.tensor.matmul(score_ps[n % 2][:, :], ones[:, :], diag[branch][:, :, :],
                                     start=True, stop=True).then_inc(score_sum, 1)
                elif kind == "scores":
                    branch, j = step[2:]
                    n = plan.scores_n[u, branch, j]
                    if n >= 2:
                        pe.wait_ge(score_read, n - 1)
                    pe.wait_ge(score_read, plan.scores_n[u, SLC if branch == SLC else WIN, "row"] + 1)
                    heads = slice(g * HPG, (g + 1) * HPG)
                    if branch == CMP:
                        ka, kb, cols, qa = cmp_a, cmp_b, slice(0, P), qa_cw
                        mask = cmp_mask[:, i * P:(i + 1) * P]
                    elif branch == WIN:
                        ka, kb, cols, qa = ka_w, kb_w, slice(j % WR * P, (j % WR + 1) * P), qa_cw
                        mask = {i: causal[:, :], i - 2: beyond[:, :]}.get(j)
                    else:
                        ka, kb, cols, qa = ka_s, kb_s, slice(j * P, (j + 1) * P), qa_s
                        mask = causal[:, :] if j == i else None
                    bank = score_ps[n % 2]
                    nc.tensor.matmul(bank[:, :], ka[0:97, g, cols], qa[0:97, b, heads, :], start=True, stop=False)
                    mm = nc.tensor.matmul(bank[:, :], kb[:, g, cols], qb[:, b, heads, :], start=False,
                                          stop=mask is None)
                    if mask is not None:
                        mm = nc.tensor.matmul(bank[:, :], ident_bf[:, :], mask.unsqueeze(1).to_broadcast([P, HPG, P]),
                                              start=False, stop=True)
                    mm.then_inc(score_sum, 1)
                elif kind == "values":
                    branch, j = step[2:]
                    n, p = plan.scores_n[u, branch, j], plan.probs_n[u, branch, j]
                    o = plan.output_n[u, branch]
                    tiles = plan.key_tiles(u, branch)
                    pe.wait_ge(score_read, n + 1)
                    if j == tiles[0] and o >= 2:
                        pe.wait_ge(output_read, o - 1)
                    if branch != CMP:
                        pe.wait_ge(v_ready, 2 * (j + 1))
                    v = {CMP: cmp_v[:, g, :], WIN: v_w[:, j % WR, g, :], SLC: v_s[:, j, g, :]}[branch]
                    out = output_ps[o % 2][:, 0:HPG * VCOLS[branch]].rearrange("p (h c) -> p h c", h=HPG)
                    for h in range(HPG):
                        mm = nc.tensor.matmul(out[:, h, :], probs[:, p % PR, h * P:(h + 1) * P], v,
                                              start=j == tiles[0] and h == 0, stop=j == tiles[-1],
                                              skip_group_check=True)
                    mm.then_inc(probs_used, 1)


def output_phase(nc, mixed, x, w_out, identity, x2):
    S, D = x.shape
    M = mixed.shape[1]
    KT = M // P
    NT = S // P
    CB = D // BANK
    GB = M // BANK

    with ExitStack() as stack:
        m = Space(nc, stack, "out")
        ident = m.sb("ident", [P, P])
        w_raw = m.sb("w_raw", [P, 2, D])
        w_hi = m.sb("w_hi", [P, KT, D], F32R)
        w_lo = m.sb("w_lo", [P, KT, D], F32R)
        mt = m.sb("mixed", [P, 2, M])
        xt = m.sb("x", [P, 2, D])
        t_hi = m.sb("mixedT_hi", [P, 2, KT, P], F32R)
        t_lo = m.sb("mixedT_lo", [P, 2, KT, P], F32R)
        tp = [m.ps(f"transposed{i}", [P, BANK]) for i in range(2 * GB)]
        acc = [m.ps(f"acc{i}", [P, BANK]) for i in range(2 * CB)]

        ident_in = m.sem("ident_in")
        w_loaded = m.sems("w_loaded", 2)
        w_hi_done = m.sem("w_hi_done")
        w_lo_done = m.sem("w_lo_done")
        mixed_in = m.sems("mixed_in", 2)
        x_in = m.sems("x_in", 2)
        transposed = m.sem("transposed")
        hi_done = m.sem("hi_done")
        lo_done = m.sem("lo_done")
        product = m.sem("product")
        added = m.sem("added")
        stored = m.sems("stored", 2)
        block = stack.enter_context(nc.Block())

        @block.sync
        def _(sp):
            sp.dma_start(ident[:, :], identity).then_inc(ident_in, 16)
            for k in range(KT):
                if k >= 2:
                    sp.wait_ge(w_lo_done, k - 1)
                sp.dma_start(w_raw[:, k % 2, :], w_out[k * P:(k + 1) * P, :]).then_inc(w_loaded[k % 2], 16)
            for b in range(2):
                sp.sem_inc(stored[b], 16)
            with sp.Fori(0, NT // 2) as r:
                for b in range(2):
                    i = r * 2
                    sp.wait_ge(transposed, i + (b + 1))
                    sp.dma_start(mt[:, b, :], mixed[bass.ds((i + b) * P, P), :]).then_inc(mixed_in[b], 16)
                    sp.wait_ge(stored[b], i * 8 + 16)
                    sp.dma_start(xt[:, b, :], x[bass.ds((i + b) * P, P), :]).then_inc(x_in[b], 16)

        @block.gpsimd
        def _(pool):
            for k in range(KT):
                pool.wait_ge(w_hi_done, k + 1)
                nc.gpsimd.tensor_tensor(w_lo[:, k, :], w_raw[:, k % 2, :], w_hi[:, k, :].bitcast(F32),
                                        ALU.subtract).then_inc(w_lo_done, 1)

        @block.scalar
        def _(act):
            for k in range(KT):
                act.wait_ge(w_loaded[k % 2], 16 * (k // 2 + 1))
                nc.scalar.copy(w_hi[:, k, :], w_raw[:, k % 2, :]).then_inc(w_hi_done, 1)
            act.sem_inc(hi_done, 2)

            def high(i, b):
                act.wait_ge(transposed, i + (b + 3))
                act.wait_ge(product, i + (b + 1))
                for q in range(GB):
                    copy = nc.scalar.copy(t_hi[:, b, 4 * q:4 * q + 4, :],
                                          tp[b * GB + q][:, :].rearrange("p (k c) -> p k c", c=P))
                copy.then_inc(hi_done, 1)

            def store(i, b):
                act.wait_ge(added, i + (b + 3))
                act.dma_start(x2[bass.ds((i + b) * P, P), :], xt[:, b, :]).then_inc(stored[b], 16)

            high(0, 0)
            with act.Fori(0, NT // 2 - 1) as r:
                high(r * 2, 1)
                store(r * 2, 0)
                high(r * 2 + 2, 0)
                store(r * 2, 1)
            high(NT - 2, 1)
            store(NT - 2, 0)
            store(NT - 2, 1)
            for b in range(2):
                act.wait_ge(stored[b], 16 * (NT // 2 + 1))

        @block.vector
        def _(dve):
            def low(i, b):
                dve.wait_ge(hi_done, i + (b + 3))
                for q in range(GB):
                    sub = nc.vector.tensor_tensor(t_lo[:, b, 4 * q:4 * q + 4, :],
                                                  tp[b * GB + q][:, :].rearrange("p (k c) -> p k c", c=P),
                                                  t_hi[:, b, 4 * q:4 * q + 4, :].bitcast(F32), ALU.subtract)
                sub.then_inc(lo_done, 1)

            def add(i, b):
                dve.wait_ge(product, i + (b + 3))
                dve.wait_ge(x_in[b], i * 8 + 16)
                for c in range(CB):
                    cols = slice(c * BANK, (c + 1) * BANK)
                    ins = nc.vector.tensor_tensor(xt[:, b, cols], xt[:, b, cols], acc[b * CB + c][:, :], ALU.add)
                ins.then_inc(added, 1)

            dve.sem_inc(lo_done, 2)
            dve.sem_inc(added, 2)
            low(0, 0)
            with dve.Fori(0, NT - 2, 2) as i:
                low(i, 1)
                add(i, 0)
                low(i + 2, 0)
                add(i, 1)
            low(NT - 2, 1)
            add(NT - 2, 0)
            add(NT - 2, 1)

        @block.tensor
        def _(pe):
            def transpose(i, b):
                pe.wait_ge(mixed_in[b], i * 8 + 16)
                pe.wait_ge(lo_done, i + (b + 1))
                for k in range(KT):
                    mm = nc.tensor.transpose(tp[b * GB + k // 4][:, k % 4 * P:k % 4 * P + P],
                                             mt[:, b, k * P:(k + 1) * P], ident[:, :])
                mm.then_inc(transposed, 1)

            def multiply(i, b):
                pe.wait_ge(lo_done, i + (b + 3))
                pe.wait_ge(added, i + (b + 1))
                for c in range(CB):
                    for k in range(KT):
                        for a, w in ((t_hi, w_hi), (t_lo, w_hi), (t_hi, w_lo)):
                            mm = nc.tensor.matmul(acc[b * CB + c][:, :], a[:, b, k, :],
                                                  w[:, k, c * BANK:(c + 1) * BANK],
                                                  start=k == 0 and a is t_hi and w is w_hi,
                                                  stop=k == KT - 1 and w is w_lo)
                mm.then_inc(product, 1)

            pe.wait_ge(ident_in, 16)
            pe.sem_inc(transposed, 2)
            pe.sem_inc(product, 2)
            transpose(0, 0)
            pe.wait_ge(w_lo_done, KT)
            with pe.Fori(0, NT - 2, 2) as i:
                transpose(i, 1)
                multiply(i, 0)
                transpose(i + 2, 0)
                multiply(i, 1)
            transpose(NT - 2, 1)
            multiply(NT - 2, 0)
            multiply(NT - 2, 1)


def mlp_phase(nc, x2, norm_mlp, w_up, w_down, identity, out):
    S, D = x2.shape
    FF = w_up.shape[1]
    KT = D // P
    T = BANK
    TT = T // P
    GROUPS = S // T
    FB = 2 * P
    FT = FB // P
    NB = FF // FB
    CB = D // BANK
    GB = D // BANK
    SUMS = TT * CB
    AR = 4

    with ExitStack() as stack:
        m = Space(nc, stack, "mlp")
        ident = m.sb("ident", [P, P])
        gain = m.sb("gain", [P, D])
        neg_half = m.sb("neg_half", [P, 1])
        y = m.sb("y", [P, 2, TT, D])
        xn = m.sb("x_normed", [P, 2, D])
        squares = m.sb("squares", [P, 2, D], BF16)
        sum_sq = m.sb("sum_sq", [P, 2])
        mean_sq = m.sb("mean_sq", [P, 2])
        rstd = m.sb("rstd", [P, 2])
        h_hi = m.sb("hT_hi", [P, KT, T], F32R)
        h_lo = m.sb("hT_lo", [P, KT, T], F32R)
        up_raw = m.sb("up_raw", [P, KT, FB])
        up_hi = m.sb("up_hi", [P, 2, KT, FB], F32R)
        up_lo = m.sb("up_lo", [P, 2, KT, FB], F32R)
        dn_raw = m.sb("down_raw", [P, FT, D])
        dn_hi = m.sb("down_hi", [P, 2, FT, D], F32R)
        dn_lo = m.sb("down_lo", [P, 2, FT, D], F32R)
        relu = m.sb("relu", [P, 2, T])
        f = m.sb("f", [P, 2, T])
        f_hi = m.sb("f_hi", [P, 2, FT, T], F32R)
        f_lo = m.sb("f_lo", [P, 2, FT, T], F32R)
        tp = [m.ps(f"transposed{i}", [P, BANK]) for i in range(GB)]
        up_ps = [m.ps(f"up{i}", [P, BANK]) for i in range(2)]
        acc = [m.ps(f"acc{i}", [P, BANK]) for i in range(AR)]

        const_in = m.sem("const_in")
        const_set = m.sem("const_set")
        y_in = m.sems("y_in", 2)
        y_out = m.sems("y_out", 2)
        squared = m.sem("squared")
        mean_done = m.sem("mean_done")
        rstd_done = m.sem("rstd_done")
        normed = m.sem("normed")
        transposed = m.sem("transposed")
        hi_done = m.sem("hi_done")
        lo_done = m.sem("lo_done")
        up_loaded = m.sem("up_loaded")
        dn_loaded = m.sem("down_loaded")
        up_hi_done = m.sem("up_hi_done")
        dn_hi_done = m.sem("down_hi_done")
        up_lo_done = m.sem("up_lo_done")
        dn_lo_done = m.sem("down_lo_done")
        up_sum = m.sem("up_sum")
        relu_done = m.sem("relu_done")
        f_done = m.sem("f_done")
        f_hi_done = m.sem("f_hi_done")
        f_lo_done = m.sem("f_lo_done")
        dn_sum = m.sem("down_sum")
        added = m.sem("added")

        up_view = w_up.rearrange("(k p) f -> p k f", p=P)
        dn_view = w_down.rearrange("(k p) n -> p k n", p=P)
        block = stack.enter_context(nc.Block())

        @block.sync
        def _(sp):
            def load_y(g):
                b = g % 2
                sp.wait_ge(y_out[b], 16 * (g // 2 + 1))
                sp.dma_start(y[:, b, :, :], x2[g * T:(g + 1) * T, :].rearrange("(t p) d -> p t d", p=P))\
                    .then_inc(y_in[b], 16)

            def store_y(g):
                sp.wait_ge(added, (g + 1) * NB * SUMS + AR)
                sp.dma_start(out[g * T:(g + 1) * T, :].rearrange("(t p) d -> p t d", p=P), y[:, g % 2, :, :])\
                    .then_inc(y_out[g % 2], 16)

            sp.dma_start(ident[:, :], identity).then_inc(const_in, 16)
            sp.dma_start(gain[:, :], norm_mlp.partition_broadcast(P)).then_inc(const_in, 16)
            for b in range(2):
                sp.sem_inc(y_out[b], 16)
            load_y(0)
            for g in range(GROUPS):
                with sp.Fori(0, NB) as c:
                    n = c + g * NB
                    sp.wait_ge(up_lo_done, n + 1)
                    sp.dma_start(up_raw[:, :, :], up_view[:, :, bass.ds(c * FB, FB)]).then_inc(up_loaded, 16)
                    sp.wait_ge(dn_lo_done, n + 1)
                    sp.dma_start(dn_raw[:, :, :], dn_view[:, bass.ds(c * FT, FT), :]).then_inc(dn_loaded, 16)
                if g > 0:
                    store_y(g - 1)
                if g + 1 < GROUPS:
                    load_y(g + 1)
            store_y(GROUPS - 1)
            sp.wait_ge(y_out[0], 16 * (GROUPS // 2 + 1))
            sp.wait_ge(y_out[1], 16 * (GROUPS // 2 + 1))

        @block.gpsimd
        def _(pool):
            pool.sem_inc(up_lo_done, 1)
            pool.sem_inc(dn_lo_done, 1)
            nc.gpsimd.memset(neg_half[:, :], -0.5).then_inc(const_set, 1)
            pool.wait_ge(const_set, 1)

            def split_up(n, b):
                pool.wait_ge(up_hi_done, n + 1)
                nc.gpsimd.tensor_tensor(up_lo[:, b, :, :], up_raw[:, :, :], up_hi[:, b, :, :].bitcast(F32),
                                        ALU.subtract).then_inc(up_lo_done, 1)

            def split_down(n, b):
                pool.wait_ge(dn_hi_done, n + 1)
                nc.gpsimd.tensor_tensor(dn_lo[:, b, :, :], dn_raw[:, :, :], dn_hi[:, b, :, :].bitcast(F32),
                                        ALU.subtract).then_inc(dn_lo_done, 1)

            for g in range(GROUPS):
                for n in range(g * TT, (g + 1) * TT):
                    b = n % 2
                    pool.wait_ge(squared, n + 1)
                    if n >= 2:
                        pool.wait_ge(normed, n - 1)
                    nc.gpsimd.tensor_scalar(mean_sq[:, b:b + 1], sum_sq[:, b:b + 1], 1.0 / D, EPS,
                                            ALU.mult, ALU.add).then_inc(mean_done, 1)
                    pool.wait_ge(mean_done, n + 1)
                    nc.gpsimd.tensor_tensor(rstd[:, b:b + 1], mean_sq[:, b:b + 1], neg_half[:, :],
                                            ALU.pow).then_inc(rstd_done, 1)
                with pool.Fori(0, NB, 2) as c:
                    for b in range(2):
                        split_up(c + (g * NB + b), b)
                        split_down(c + (g * NB + b), b)

        @block.scalar
        def _(act):
            def split_up(n, b):
                act.wait_ge(up_loaded, n * 16 + 16)
                act.wait_ge(up_sum, (n + 1) * FT)
                nc.scalar.copy(up_hi[:, b, :, :], up_raw[:, :, :]).then_inc(up_hi_done, 1)

            def split_down(n, b):
                act.wait_ge(dn_loaded, n * 16 + 16)
                act.wait_ge(dn_sum, (n + 1) * SUMS)
                nc.scalar.copy(dn_hi[:, b, :, :], dn_raw[:, :, :]).then_inc(dn_hi_done, 1)

            def relu_and_hi(n, b):
                for t in range(FT):
                    k = n * FT + t
                    act.wait_ge(up_sum, k + (2 * FT + 1))
                    act.wait_ge(f_done, k + 1)
                    nc.scalar.activation(relu[:, t % 2, :], up_ps[t % 2][:, :], ACT.Relu).then_inc(relu_done, 1)
                for t in range(FT):
                    k = n * FT + t
                    act.wait_ge(f_done, k + 3)
                    if t == 0:
                        act.wait_ge(dn_sum, (n + 1) * SUMS)
                    nc.scalar.copy(f_hi[:, b, t, :], f[:, t % 2, :]).then_inc(f_hi_done, 1)

            act.sem_inc(up_sum, 2 * FT)
            act.sem_inc(dn_sum, 2 * SUMS)
            for g in range(GROUPS):
                act.wait_ge(y_in[g % 2], 16 * (g // 2 + 1))
                for n in range(g * TT, (g + 1) * TT + 1):
                    if n < (g + 1) * TT:
                        if n >= 2:
                            act.wait_ge(mean_done, n - 1)
                        nc.scalar.activation(squares[:, n % 2, :], y[:, g % 2, n - g * TT, :], ACT.Square,
                                             accum_out=sum_sq[:, n % 2:n % 2 + 1]).then_inc(squared, 1)
                    if n > g * TT:
                        t = n - 1
                        act.wait_ge(transposed, t + 1)
                        c = (t - g * TT) * P
                        for q in range(GB):
                            copy = nc.scalar.copy(h_hi[:, 4 * q:4 * q + 4, c:c + P],
                                                  tp[q][:, :].rearrange("p (k c) -> p k c", c=P))
                        copy.then_inc(hi_done, 1)
                split_up(g * NB, 0)
                split_down(g * NB, 0)
                with act.Fori(0, NB - 2, 2) as c:
                    for b in range(2):
                        n = c + (g * NB + b)
                        split_up(n + 1, 1 - b)
                        relu_and_hi(n, b)
                        split_down(n + 1, 1 - b)
                n = (g + 1) * NB - 2
                split_up(n + 1, 1)
                relu_and_hi(n, 0)
                split_down(n + 1, 1)
                relu_and_hi(n + 1, 1)

        @block.vector
        def _(dve):
            def square_and_lo(n, b):
                for t in range(FT):
                    k = n * FT + t
                    dve.wait_ge(relu_done, k + 3)
                    dve.wait_ge(f_lo_done, k + 1)
                    nc.vector.tensor_tensor(f[:, t % 2, :], relu[:, t % 2, :], relu[:, t % 2, :],
                                            ALU.mult).then_inc(f_done, 1)
                for t in range(FT):
                    dve.wait_ge(f_hi_done, n * FT + (t + 1))
                    nc.vector.tensor_tensor(f_lo[:, b, t, :], f[:, t % 2, :], f_hi[:, b, t, :].bitcast(F32),
                                            ALU.subtract).then_inc(f_lo_done, 1)

            def add(n, yb):
                for i in range(SUMS):
                    tt, c = divmod(i, CB)
                    cols = slice(c * BANK, (c + 1) * BANK)
                    dve.wait_ge(dn_sum, n * SUMS + (2 * SUMS + i + 1))
                    dve.wait_ge(added, n * SUMS + (i + 1))
                    nc.vector.tensor_tensor(y[:, yb, tt, cols], acc[i % AR][:, :], y[:, yb, tt, cols],
                                            ALU.add).then_inc(added, 1)

            dve.sem_inc(f_done, 2)
            dve.sem_inc(relu_done, 2)
            dve.sem_inc(f_lo_done, 2)
            dve.sem_inc(added, AR)
            dve.wait_ge(const_in, 32)
            for g in range(GROUPS):
                for n in range(g * TT, (g + 1) * TT + 1):
                    if n < (g + 1) * TT:
                        b = n % 2
                        dve.wait_ge(rstd_done, n + 1)
                        if n >= 2:
                            dve.wait_ge(transposed, n - 1)
                        nc.vector.scalar_tensor_tensor(
                            out=xn[:, b, :], in0=y[:, g % 2, n - g * TT, :], scalar=rstd[:, b:b + 1],
                            in1=gain[:, :], op0=ALU.mult, op1=ALU.mult).then_inc(normed, 1)
                    if n > g * TT:
                        t = n - 1
                        dve.wait_ge(hi_done, t + 1)
                        c = (t - g * TT) * P
                        for q in range(GB):
                            sub = nc.vector.tensor_tensor(
                                h_lo[:, 4 * q:4 * q + 4, c:c + P],
                                tp[q][:, :].rearrange("p (k c) -> p k c", c=P),
                                h_hi[:, 4 * q:4 * q + 4, c:c + P].bitcast(F32), ALU.subtract)
                        sub.then_inc(lo_done, 1)
                square_and_lo(g * NB, 0)
                with dve.Fori(0, NB - 2, 2) as c:
                    for b in range(2):
                        n = c + (g * NB + b)
                        square_and_lo(n + 1, 1 - b)
                        add(n, g % 2)
                n = (g + 1) * NB - 2
                square_and_lo(n + 1, 1)
                add(n, g % 2)
                add(n + 1, g % 2)

        @block.tensor
        def _(pe):
            def up(n, b):
                pe.wait_ge(up_lo_done, n + 2)
                for t in range(FT):
                    pe.wait_ge(relu_done, n * FT + (t + 1))
                    cols = slice(t * P, (t + 1) * P)
                    for k in range(KT):
                        for w, h in ((up_hi, h_hi), (up_lo, h_hi), (up_hi, h_lo)):
                            mm = nc.tensor.matmul(up_ps[t % 2][:, :], w[:, b, k, cols], h[:, k, :],
                                                  start=k == 0 and w is up_hi and h is h_hi,
                                                  stop=k == KT - 1 and h is h_lo)
                    mm.then_inc(up_sum, 1)

            def down(n, b):
                pe.wait_ge(dn_lo_done, n + 2)
                pe.wait_ge(f_lo_done, n * FT + (FT + 2))
                for i in range(SUMS):
                    tt, c = divmod(i, CB)
                    pe.wait_ge(added, n * SUMS + (i + 1))
                    for k in range(FT):
                        for a, w in ((f_hi, dn_hi), (f_lo, dn_hi), (f_hi, dn_lo)):
                            mm = nc.tensor.matmul(acc[i % AR][:, :], a[:, b, k, tt * P:(tt + 1) * P],
                                                  w[:, b, k, c * BANK:(c + 1) * BANK],
                                                  start=k == 0 and a is f_hi and w is dn_hi,
                                                  stop=k == FT - 1 and w is dn_lo)
                    mm.then_inc(dn_sum, 1)

            pe.wait_ge(const_in, 32)
            for g in range(GROUPS):
                for n in range(g * TT, (g + 1) * TT):
                    pe.wait_ge(normed, n + 1)
                    if n >= 1:
                        pe.wait_ge(lo_done, n)
                    for k in range(KT):
                        mm = nc.tensor.transpose(tp[k // 4][:, k % 4 * P:k % 4 * P + P],
                                                 xn[:, n % 2, k * P:(k + 1) * P], ident[:, :])
                    mm.then_inc(transposed, 1)
                pe.wait_ge(lo_done, (g + 1) * TT)
                up(g * NB, 0)
                with pe.Fori(0, NB - 2, 2) as c:
                    for b in range(2):
                        n = c + (g * NB + b)
                        up(n + 1, 1 - b)
                        down(n, b)
                n = (g + 1) * NB - 2
                up(n + 1, 1)
                down(n, 0)
                down(n + 1, 1)



def shape_tables(S, D):
    f = np.float32
    inv_freq = (f(1) / (f(10000) ** np.linspace(0, 1, HEAD // 2, dtype=f))).astype(f)
    angle = (np.arange(S, dtype=f)[:, None] * inv_freq[None, :]).astype(f)
    cos, sin = np.cos(angle), np.sin(angle)
    rotation = np.stack([np.repeat(cos, 2, axis=1), np.stack([-sin, sin], axis=-1).reshape(S, HEAD)], axis=1)
    log_gamma = np.log(f(1) - f(2) ** (f(-5) - np.arange(RET_HEADS, dtype=f))).astype(f)
    idx = np.arange(P, dtype=f)
    rel = idx[None, :] - idx[:, None]
    scale = f(HEAD ** -0.5)
    decay = np.where(rel[:, None, :] >= 0, np.exp(log_gamma[None, :, None] * np.maximum(rel, 0)[:, None, :]), 0) * scale
    row_decay = np.stack([np.exp(log_gamma[None, :] * (idx[:, None] + 1)),
                          np.exp(log_gamma[None, :] * (P - 1 - idx[:, None])) * scale,
                          np.broadcast_to(np.exp(log_gamma * P)[None, :], (P, RET_HEADS))], axis=1)
    windows = (S - CMP_LEN) // STRIDE + 1
    blocks = S // SLC_LEN
    cs = np.arange(windows)[:, None] * STRIDE
    ss = np.arange(blocks)[None, :] * SLC_LEN
    overlap = np.zeros((P, blocks), f)
    overlap[:windows] = np.clip(np.minimum(cs + CMP_LEN, ss + SLC_LEN) - np.maximum(cs, ss), 0, None) / CMP_LEN
    t_blk = (np.arange(S) // SLC_LEN)[:, None]
    j = np.arange(blocks)[None, :]
    forced = (j == 0) | (j == t_blk) | (j == t_blk - 1)
    eligible = (j <= t_blk).astype(f)
    selection = np.stack([1e4 * forced, eligible, eligible - 1], axis=1)
    block_rows = (np.arange(S)[None, :] // SLC_LEN == np.arange(blocks)[:, None])
    tables = {"identity": np.eye(P), "rotation": rotation, "decay": decay, "row_decay": row_decay,
              "overlap": overlap, "selection": selection, "block_rows": block_rows}
    return {name: np.ascontiguousarray(t, dtype=f) for name, t in tables.items()}


def build_layer(nc, a, out):
    _, S, D = a["x"].shape
    N = a["w_in"].shape[2]
    x = a["x"][0]
    z = nc.dram_tensor("z_scratch", (S, N), F32, kind="Internal").ap()
    mixed = nc.dram_tensor("mixed_scratch", (S, a["w_out"].shape[1]), F32, kind="Internal").ap()
    x2 = nc.dram_tensor("x2_scratch", (S, D), F32, kind="Internal").ap()
    ident = a["identity"]
    projection_phase(nc, x, a["norm_mix"][0], a["w_in"][0], ident, z)
    with ExitStack() as stack:
        m = Space(nc, stack, "keys")
        cmp_a = m.sb("cmp_a", [P, GROUPS, P], F32R)
        cmp_b = m.sb("cmp_b", [P, GROUPS, P], F32R)
        cmp_v = m.sb("cmp_v", [P, GROUPS, HEAD + 1 + S // SLC_LEN])
        compress_phase(nc, z, [(a["cmp_pe_k"][0], a["cmp_w1_k"][0], a["cmp_w2_k"][0]),
                               (a["cmp_pe_v"][0], a["cmp_w1_v"][0], a["cmp_w2_v"][0])],
                       a["nsa_k_norm"][0], ident, a["overlap"], cmp_a, cmp_b, cmp_v)
        mixers_phase(nc, z, a["conv_w"][0], a["nsa_q_norm"][0], a["nsa_k_norm"][0], a, cmp_a, cmp_b, cmp_v, mixed)
    output_phase(nc, mixed, x, a["w_out"][0], ident, x2)
    mlp_phase(nc, x2, a["norm_mlp"][0], a["w_up"][0], a["w_down"][0], ident, out[0])


def kernel(**inputs):
    import concourse.bacc as bacc
    from concourse.bass_utils import run_bass_kernel_spmd

    nc = bacc.Bacc("TRN2", target_bir_lowering=False, num_devices=1)
    assert inputs["x"].shape[0] == 1 and inputs["w_in"].shape[0] == 1
    arrays = {name: np.ascontiguousarray(value) for name, value in inputs.items()}
    arrays.update(shape_tables(*arrays["x"].shape[1:]))
    aps = {name: nc.dram_tensor(f"in_{name}", a.shape, mybir.dt.from_np(a.dtype), kind="ExternalInput").ap()
           for name, a in arrays.items()}
    out = nc.dram_tensor("result", arrays["x"].shape, F32, kind="ExternalOutput").ap()
    build_layer(nc, aps, out)
    r = run_bass_kernel_spmd(nc, [{f"in_{name}": a for name, a in arrays.items()}], core_ids=[0])
    return r.results[0]["result"]
```

```python
from contextlib import ExitStack

import numpy as np

import concourse.bass as bass
from concourse import mybir

ALU = mybir.AluOpType
ACT = mybir.ActivationFunctionType
F32 = mybir.dt.float32
F32R = mybir.dt.float32r
BF16 = mybir.dt.bfloat16
AX_X = mybir.AxisListType.X

P = 128
BANK = 512
EPS = 1e-6


class Space:

    def __init__(self, nc, stack, phase):
        self.nc, self.stack, self.phase = nc, stack, phase

    def sb(self, name, shape, dt=F32):
        return self.stack.enter_context(self.nc.sbuf_tensor(f"{self.phase}_{name}", shape, dt))

    def ps(self, name, shape, dt=F32):
        return self.stack.enter_context(self.nc.psum_tensor(f"{self.phase}_{name}", shape, dt))

    def sem(self, name):
        return self.stack.enter_context(self.nc.semaphore(f"{self.phase}_{name}"))

    def sems(self, name, n):
        return [self.sem(f"{name}{i}") for i in range(n)]


def projection_phase(nc, x, norm_mix, w_in, identity, z):
    S, D = x.shape
    N = w_in.shape[1]
    KT = D // P
    HALVES = 2
    TT = S // P // HALVES
    NB = 9
    BW = N // NB
    RING = 3
    GB = D // BANK
    ZR = 4
    XR = 4
    assert HALVES == 2 and NB // RING == 3
    assert BW * NB == N and BW % 2 == 0 and NB % RING == 0 and TT % ZR == 0

    with ExitStack() as stack:
        m = Space(nc, stack, "proj")
        ident = m.sb("ident", [P, P])
        gain = m.sb("gain", [P, D])
        neg_half = m.sb("neg_half", [P, 1])
        xt = m.sb("x_tile", [P, XR, D])
        xn = m.sb("x_normed", [P, 2, D])
        squares = m.sb("squares", [P, 2, D], BF16)
        sum_sq = m.sb("sum_sq", [P, 2])
        mean_sq = m.sb("mean_sq", [P, 2])
        rstd = m.sb("rstd", [P, 2])
        h_hi = m.sb("hT_hi", [P, KT, TT * P], F32R)
        h_lo = m.sb("hT_lo", [P, KT, TT * P], F32R)
        w_raw = m.sb("w_raw", [P, RING, KT, BW])
        w_hi = m.sb("w_hi", [P, RING, KT, BW], F32R)
        w_lo = m.sb("w_lo", [P, RING, KT, BW], F32R)
        z_out = m.sb("z_out", [P, ZR, BW])
        tp = [m.ps(f"transposed{i}", [P, BANK]) for i in range(2 * GB)]
        acc = [m.ps(f"acc{i}", [P, BANK]) for i in range(ZR)]

        const_in = m.sem("const_in")
        const_set = m.sem("const_set")
        x_in = m.sems("x_in", XR)
        squared = m.sem("squared")
        mean_done = m.sem("mean_done")
        rstd_done = m.sem("rstd_done")
        normed = m.sem("normed")
        transposed = m.sem("transposed")
        hi_done = m.sem("hi_done")
        lo_done = m.sem("lo_done")
        w_loaded = m.sems("w_loaded", RING)
        w_hi_done = m.sem("w_hi_done")
        w_lo_done = m.sem("w_lo_done")
        product = m.sem("product")
        copied = m.sem("copied")
        z_free = m.sems("z_free", ZR)

        w_view = w_in.rearrange("(k p) n -> p k n", p=P)
        block = stack.enter_context(nc.Block())

        def split_after(t):
            return {1: (1, None), 3: (None, NB + 1), 4: (2, None)}.get(t, (None, None))

        @block.sync
        def _(sp):
            AHEAD = RING - 1

            def load_w(n, u, col):
                if not isinstance(n, int) or n >= RING:
                    sp.wait_ge(w_lo_done, n - RING + 1)
                sp.dma_start(w_raw[:, u, :, :], w_view[:, :, bass.ds(col, BW)]).then_inc(w_loaded[u], 16)

            def store_z(n, half, col):
                for t in range(TT):
                    s = t % ZR
                    sp.wait_ge(copied, n * TT + (t + 1 + ZR))
                    sp.dma_start(z[(half * TT + t) * P:(half * TT + t + 1) * P, bass.ds(col, BW)],
                                 z_out[:, s, :]).then_inc(z_free[s], 16)

            sp.dma_start(ident[:, :], identity).then_inc(const_in, 16)
            sp.dma_start(gain[:, :], norm_mix.partition_broadcast(P)).then_inc(const_in, 16)
            for n in range(AHEAD):
                load_w(n, n, n * BW)
            for half in range(HALVES):
                first = half * NB
                load_w(first + AHEAD, AHEAD, AHEAD * BW)
                store_z(first, half, 0)
                with sp.Fori(0, (NB - RING) // RING) as r:
                    for u in range(1, 1 + RING):
                        load_w(r * RING + (first + u + AHEAD), (u + AHEAD) % RING, r * (RING * BW) + (u + AHEAD) * BW)
                        store_z(r * RING + (first + u), half, r * (RING * BW) + u * BW)
                for c in range(NB - AHEAD, NB):
                    if half + 1 < HALVES:
                        load_w(first + c + AHEAD, (c + AHEAD) % RING, (c + AHEAD - NB) * BW)
                    store_z(first + c, half, c * BW)
            for s in range(ZR):
                sp.wait_ge(z_free[s], 16 + 16 * HALVES * NB * TT // ZR)

        @block.scalar
        def _(act):
            def split_hi(n, u, j):
                act.wait_ge(w_loaded[u], j * 16 + 16)
                act.wait_ge(product, (n + 1) * TT)
                nc.scalar.copy(w_hi[:, u, :, :], w_raw[:, u, :, :]).then_inc(w_hi_done, 1)

            def load_x(n):
                if n < HALVES * TT:
                    if n >= XR:
                        act.wait_ge(normed, n - XR + 1)
                    act.dma_start(xt[:, n % XR, :], x[n * P:(n + 1) * P, :]).then_inc(x_in[n % XR], 16)

            def square(n):
                act.wait_ge(x_in[n % XR], 16 * (n // XR + 1))
                if n >= 2:
                    act.wait_ge(mean_done, n - 1)
                nc.scalar.activation(squares[:, n % 2, :], xt[:, n % XR, :], ACT.Square,
                                     accum_out=sum_sq[:, n % 2:n % 2 + 1]).then_inc(squared, 1)

            def high(n):
                act.wait_ge(transposed, n + 1)
                c = n % TT * P
                for g in range(GB):
                    copy = nc.scalar.copy(h_hi[:, 4 * g:4 * g + 4, c:c + P],
                                          tp[n % 2 * GB + g][:, :].rearrange("p (k c) -> p k c", c=P))
                copy.then_inc(hi_done, 1)

            act.sem_inc(product, RING * TT)
            for n in range(XR):
                load_x(n)
            for half in range(HALVES):
                first = half * TT
                square(first)
                square(first + 1)
                split_hi(half * NB, 0, half * NB // RING)
                for t in range(TT):
                    high(first + t)
                    load_x(first + t + XR)
                    if t + 2 < TT:
                        square(first + t + 2)
                    n = split_after(t)[half]
                    if n is not None:
                        split_hi(n, n % RING, n // RING)
                if half == 1:
                    split_hi(NB + 2, 2, NB // RING)
                with act.Fori(0, NB // RING - 1) as r:
                    for u in range(RING):
                        split_hi(r * RING + (half * NB + RING + u), u, r + (half * NB // RING + 1))

        @block.gpsimd
        def _(pool):
            def split_lo(n, u):
                pool.wait_ge(w_hi_done, n + 1)
                nc.gpsimd.tensor_tensor(w_lo[:, u, :, :], w_raw[:, u, :, :], w_hi[:, u, :, :].bitcast(F32),
                                        ALU.subtract).then_inc(w_lo_done, 1)

            nc.gpsimd.memset(neg_half[:, :], -0.5).then_inc(const_set, 1)
            pool.wait_ge(const_set, 1)

            def root(n):
                b = n % 2
                pool.wait_ge(squared, n + 1)
                if n >= 2:
                    pool.wait_ge(normed, n - 1)
                nc.gpsimd.tensor_scalar(mean_sq[:, b:b + 1], sum_sq[:, b:b + 1], 1.0 / D, EPS,
                                        ALU.mult, ALU.add).then_inc(mean_done, 1)
                pool.wait_ge(mean_done, n + 1)
                nc.gpsimd.tensor_tensor(rstd[:, b:b + 1], mean_sq[:, b:b + 1], neg_half[:, :],
                                        ALU.pow).then_inc(rstd_done, 1)

            for half in range(HALVES):
                first = half * TT
                root(first)
                root(first + 1)
                split_lo(half * NB, 0)
                for t in range(TT):
                    if t + 2 < TT:
                        root(first + t + 2)
                    n = split_after(t)[half]
                    if n is not None:
                        split_lo(n, n % RING)
                if half == 1:
                    split_lo(NB + 2, 2)
                with pool.Fori(0, NB // RING - 1) as r:
                    for u in range(RING):
                        split_lo(r * RING + (half * NB + RING + u), u)

        @block.vector
        def _(dve):
            def evacuate(n, t):
                s = t % ZR
                dve.wait_ge(product, (n + RING) * TT + (t + 1))
                dve.wait_ge(z_free[s], n * (16 * TT // ZR) + 16 * (t // ZR + 1))
                nc.vector.tensor_copy(z_out[:, s, :], acc[s][:, 0:BW]).then_inc(copied, 1)

            def norm(n):
                b = n % 2
                dve.wait_ge(rstd_done, n + 1)
                if n >= 2:
                    dve.wait_ge(transposed, n - 1)
                nc.vector.scalar_tensor_tensor(
                    out=xn[:, b, :], in0=xt[:, n % XR, :], scalar=rstd[:, b:b + 1], in1=gain[:, :],
                    op0=ALU.mult, op1=ALU.mult).then_inc(normed, 1)

            def low(n):
                dve.wait_ge(hi_done, n + 1)
                c = n % TT * P
                for g in range(GB):
                    sub = nc.vector.tensor_tensor(
                        h_lo[:, 4 * g:4 * g + 4, c:c + P],
                        tp[n % 2 * GB + g][:, :].rearrange("p (k c) -> p k c", c=P),
                        h_hi[:, 4 * g:4 * g + 4, c:c + P].bitcast(F32), ALU.subtract)
                sub.then_inc(lo_done, 1)

            dve.sem_inc(copied, ZR)
            for s in range(ZR):
                dve.sem_inc(z_free[s], 16)
            dve.wait_ge(const_in, 32)
            norm(0)
            norm(1)
            for t in range(TT):
                low(t)
                if t + 2 < TT:
                    norm(t + 2)
                if t >= 1:
                    evacuate(0, t - 1)
            evacuate(0, TT - 1)
            with dve.Fori(0, NB - 2) as r:
                for t in range(TT):
                    evacuate(r + 1, t)
            norm(TT)
            norm(TT + 1)
            for t in range(TT):
                evacuate(NB - 1, t)
                if t >= 1:
                    low(TT + t - 1)
                    if t + 1 < TT:
                        norm(TT + t + 1)
            low(2 * TT - 1)
            with dve.Fori(0, NB) as r:
                for t in range(TT):
                    evacuate(r + NB, t)

        @block.tensor
        def _(pe):
            def multiply(n, u, t):
                if t == 0:
                    pe.wait_ge(w_lo_done, n + 1)
                s = t % ZR
                pe.wait_ge(copied, n * TT + (t + 1))
                rows = slice(t * P, (t + 1) * P)
                for k in range(KT):
                    for a, w in ((h_hi, w_hi), (h_lo, w_hi), (h_hi, w_lo)):
                        mm = nc.tensor.matmul(acc[s][:, 0:BW], a[:, k, rows], w[:, u, k, :],
                                              start=k == 0 and a is h_hi and w is w_hi,
                                              stop=k == KT - 1 and w is w_lo)
                mm.then_inc(product, 1)

            def transpose(n):
                pe.wait_ge(normed, n + 1)
                if n >= 2:
                    pe.wait_ge(lo_done, n - 1)
                for k in range(KT):
                    mm = nc.tensor.transpose(tp[n % 2 * GB + k // 4][:, k % 4 * P:k % 4 * P + P],
                                             xn[:, n % 2, k * P:(k + 1) * P], ident[:, :])
                mm.then_inc(transposed, 1)

            pe.wait_ge(const_in, 32)
            transpose(0)
            transpose(1)
            for half in range(HALVES):
                first = half * NB
                for t in range(TT):
                    pe.wait_ge(lo_done, half * TT + t + 1)
                    multiply(first, 0, t)
                    if half == 0 and t + 2 < TT:
                        transpose(t + 2)
                with pe.Fori(0, NB // RING - 1) as r:
                    for u in range(1, 1 + RING):
                        for t in range(TT):
                            multiply(r * RING + (first + u), u % RING, t)
                for t in range(TT):
                    multiply(first + NB - 2, (NB - 2) % RING, t)
                for t in range(TT):
                    multiply(first + NB - 1, (NB - 1) % RING, t)
                    if half == 0 and t >= 1:
                        transpose(TT + t - 1)
                if half == 0:
                    transpose(2 * TT - 1)

def chain(eng, done):
    count = [0]

    def link(instruction):
        count[0] += 1
        instruction.then_inc(done, 1)
        eng.wait_ge(done, count[0])

    return link


MASKED = -1e30
HEAD = 64
RET_HEADS = 4
GROUPS = 2
HPG = 4
NSA_HEADS = GROUPS * HPG
STRIDE, CMP_LEN, SLC_LEN, TOPK = 16, 32, 64, 8

RQ, RK, RV, RG = 0, 256, 512, 768
CB_, CC, CH = 1024, 1280, 1536
NQ = 1792
NKC, NVC, NKS, NVS, NKW, NVW = 2304, 2432, 2560, 2688, 2816, 2944
NG = 3072


def compress_phase(nc, z, weights, k_gain, identity, overlap, keys_a, keys_b, values):
    S = z.shape[0]
    NT = S // P
    NW = (S - CMP_LEN) // STRIDE + 1
    NBLK = S // SLC_LEN
    KINDS = 2

    with ExitStack() as stack:
        m = Space(nc, stack, "cmp")
        ident = m.sb("ident", [P, P])
        kv = m.sb("kv", [P, NT, KINDS * P])
        kvT = m.sb("kvT", [P, KINDS, S])
        w1 = m.sb("w1", [P, KINDS, CMP_LEN, HEAD])
        w2 = m.sb("w2", [HEAD, KINDS, HEAD])
        pe_rows = m.sb("pe_rows", [P, KINDS * HEAD])
        peT = m.sb("peT", [HEAD, KINDS, CMP_LEN])
        bias = m.sb("bias", [HEAD, KINDS])
        gain = m.sb("gain", [P, HEAD])
        pre = m.sb("pre", [HEAD, KINDS * GROUPS, P])
        den = m.sb("den", [HEAD, KINDS * GROUPS, P])
        act_out = m.sb("silu", [HEAD, KINDS * GROUPS, P])
        kc = m.sb("kc", [P, GROUPS, HEAD])
        sq = m.sb("sq", [P, GROUPS, HEAD])
        ssq = m.sb("ssq", [P, GROUPS])
        mean = m.sb("mean", [P, GROUPS])
        rstd = m.sb("rstd", [P, GROUPS])
        neg_half = m.sb("neg_half", [P, GROUPS])
        pack = m.sb("pack", [P, GROUPS, P])
        banks = [m.ps(f"bank{i}", [P, BANK]) for i in range(8)]

        loaded = m.sem("loaded")
        cleared = m.sem("cleared")
        transposed = m.sem("transposed")
        copied = m.sem("copied")
        pe_T = m.sem("pe_T")
        pe_copied = m.sem("pe_copied")
        bias_sum = m.sem("bias_sum")
        bias_set = m.sem("bias_set")
        first = m.sem("first_product")
        biased = m.sem("biased")
        exp_done = m.sem("exp_done")
        silu_done = m.sem("silu_done")
        second = m.sem("second_product")
        squares = m.sem("squares")
        powered = m.sem("powered")
        packed = m.sem("packed")
        packT = m.sem("packT")
        out_a = m.sem("keys_a_set")
        dve_done = m.sem("dve_done")
        pool_done = m.sem("pool_done")
        block = stack.enter_context(nc.Block())
        LOADS = 1 + 1 + 2 * KINDS + 1 + KINDS + KINDS + 1 + GROUPS

        @block.sync
        def _(sp):
            sp.wait_ge(cleared, 1)
            sp.dma_start(ident[:, :], identity).then_inc(loaded, 16)
            sp.dma_start(kv[:, :, :], z[:, NKC:NKC + KINDS * P].rearrange("(t p) c -> p t c", p=P)).then_inc(loaded, 16)
            for j, (pe_, w1_, w2_) in enumerate(weights):
                for g in range(GROUPS):
                    sp.dma_start(w1[g * HEAD:(g + 1) * HEAD, j, :, :],
                                 w1_.rearrange("(l d) e -> d l e", d=HEAD)).then_inc(loaded, 16)
                sp.dma_start(w2[:, j, :], w2_).then_inc(loaded, 16)
                sp.dma_start(pe_rows[0:CMP_LEN, j * HEAD:(j + 1) * HEAD], pe_).then_inc(loaded, 16)
            sp.dma_start(gain[:, :], k_gain.partition_broadcast(P)).then_inc(loaded, 16)
            for g in range(GROUPS):
                sp.dma_start(values[:, g, HEAD:], overlap).then_inc(loaded, 16)

        TOTAL = 16 * (2 + KINDS * (GROUPS + 2) + 1 + GROUPS)

        @block.gpsimd
        def _(pool):
            link = chain(pool, pool_done)
            link(nc.gpsimd.memset(pe_rows[:, :], 0.0))
            link(nc.gpsimd.memset(values[:, :, :], 0.0))
            link(nc.gpsimd.memset(pack[:, :, :], 0.0))
            nc.gpsimd.memset(neg_half[:, :], -0.5).then_inc(cleared, 1)
            pool.wait_ge(squares, 1)
            link(nc.gpsimd.tensor_scalar(mean[:, :], ssq[:, :], 1.0 / HEAD, EPS, ALU.mult, ALU.add))
            nc.gpsimd.tensor_tensor(rstd[:, :], mean[:, :], neg_half[:, :], ALU.pow).then_inc(powered, 1)

        @block.tensor
        def _(pe):
            pe.wait_ge(loaded, TOTAL)
            for q in range(KINDS * NT // 4):
                j, t0 = divmod(4 * q, NT)
                for t in range(4):
                    mm = nc.tensor.transpose(banks[q][:, t * P:(t + 1) * P],
                                             kv[:, t0 + t, j * P:(j + 1) * P], ident[:, :])
                mm.then_inc(transposed, 1)
            pe.wait_ge(copied, 1)
            nc.tensor.transpose(banks[0][:, 0:P], pe_rows[:, :], ident[:, :]).then_inc(pe_T, 1)
            pe.wait_ge(pe_copied, 1)
            for j in range(KINDS):
                for l in range(CMP_LEN):
                    mm = nc.tensor.matmul(banks[0][0:HEAD, P + j:P + j + 1], w1[0:HEAD, j, l, :],
                                          peT[:, j, l:l + 1], start=l == 0, stop=l == CMP_LEN - 1)
            mm.then_inc(bias_sum, 1)
            pe.wait_ge(copied, KINDS * NT // 4)
            for j in range(KINDS):
                for g in range(GROUPS):
                    rows = slice(g * HEAD, (g + 1) * HEAD)
                    for l in range(CMP_LEN):
                        mm = nc.tensor.matmul(banks[1 + j * GROUPS + g][0:HEAD, 0:NW], w1[rows, j, l, :],
                                              kvT[rows, j, l:l + (NW - 1) * STRIDE + 1:STRIDE],
                                              start=l == 0, stop=l == CMP_LEN - 1)
                    mm.then_inc(first, 1)
            pe.wait_ge(silu_done, 1)
            for n in range(KINDS * GROUPS):
                mm = nc.tensor.matmul(banks[5][0:NW, n * HEAD:(n + 1) * HEAD], act_out[:, n, 0:NW],
                                      w2[:, n // GROUPS, :], start=True, stop=True)
            mm.then_inc(second, 1)
            pe.wait_ge(packed, 1)
            for g in range(GROUPS):
                mm = nc.tensor.transpose(banks[6][:, g * P:(g + 1) * P], pack[:, g, :], ident[:, :])
            mm.then_inc(packT, 1)

        @block.scalar
        def _(act):
            for n in range(KINDS * NT // 4):
                act.wait_ge(transposed, n + 1)
                j, t0 = divmod(4 * n, NT)
                nc.scalar.copy(kvT[:, j, t0 * P:(t0 + 4) * P], banks[n][:, :]).then_inc(copied, 1)
            act.wait_ge(bias_set, 1)
            for n in range(KINDS * GROUPS):
                act.wait_ge(first, n + 1)
                j = n // GROUPS
                nc.scalar.activation(pre[:, n, 0:NW], banks[1 + n][0:HEAD, 0:NW], ACT.Identity,
                                     bias=bias[:, j:j + 1]).then_inc(biased, 1)
            for n in range(KINDS * GROUPS):
                act.wait_ge(biased, n + 1)
                nc.scalar.activation(den[:, n, 0:NW], pre[:, n, 0:NW], ACT.Exp, scale=-1.0).then_inc(exp_done, 1)

        @block.vector
        def _(dve):
            link = chain(dve, dve_done)
            dve.wait_ge(pe_T, 1)
            for j in range(KINDS):
                copy = nc.vector.tensor_copy(peT[:, j, :], banks[0][j * HEAD:(j + 1) * HEAD, 0:CMP_LEN])
            copy.then_inc(pe_copied, 1)
            dve.wait_ge(bias_sum, 1)
            nc.vector.tensor_copy(bias[:, :], banks[0][0:HEAD, P:P + KINDS]).then_inc(bias_set, 1)
            dve.wait_ge(exp_done, KINDS * GROUPS)
            link(nc.vector.tensor_scalar(den[:, :, 0:NW], den[:, :, 0:NW], 1.0, None, ALU.add))
            link(nc.vector.reciprocal(den[:, :, 0:NW], den[:, :, 0:NW]))
            nc.vector.tensor_tensor(act_out[:, :, 0:NW], den[:, :, 0:NW], pre[:, :, 0:NW], ALU.mult)\
                .then_inc(silu_done, 1)
            dve.wait_ge(second, 1)
            dve.wait_ge(loaded, TOTAL)
            out = banks[5][0:NW, 0:KINDS * GROUPS * HEAD].rearrange("p (j g d) -> p j g d", j=KINDS, g=GROUPS)
            nc.vector.tensor_copy(values[0:NW, :, 0:HEAD], out[:, 1, :, :])
            link(nc.vector.tensor_copy(kc[0:NW, :, :], out[:, 0, :, :]))
            link(nc.vector.memset(ssq[:, :], 1.0))
            link(nc.vector.tensor_tensor(sq[0:NW, :, :], kc[0:NW, :, :], kc[0:NW, :, :], ALU.mult))
            nc.vector.tensor_reduce(ssq[0:NW, :], sq[0:NW, :, :], AX_X, ALU.add).then_inc(squares, 1)
            dve.wait_ge(powered, 1)
            link(nc.vector.tensor_tensor(kc[0:NW, :, :], kc[0:NW, :, :],
                                         rstd[0:NW, :].unsqueeze(2).to_broadcast([NW, GROUPS, HEAD]), ALU.mult))
            link(nc.vector.tensor_tensor(kc[0:NW, :, :], kc[0:NW, :, :],
                                         gain[0:NW, :].unsqueeze(1).to_broadcast([NW, GROUPS, HEAD]), ALU.mult))
            link(nc.vector.tensor_copy(pack[0:NW, :, HEAD:].bitcast(F32R), kc[0:NW, :, :]))
            nc.vector.tensor_tensor(pack[0:NW, :, 0:HEAD].bitcast(F32R), kc[0:NW, :, :], pack[0:NW, :, HEAD:],
                                    ALU.subtract).then_inc(packed, 1)
            dve.wait_ge(packT, 1)
            bank = banks[6][:, 0:GROUPS * P].rearrange("p (g n) -> p g n", g=GROUPS)
            nc.vector.tensor_copy(keys_b[:, :, :], bank)
            link(nc.vector.tensor_copy(keys_a[0:HEAD, :, :], bank[HEAD:P, :, :]))


CMP, SLC, WIN = 0, 1, 2
NBLKS = 32
VCOLS = {CMP: HEAD + NBLKS, WIN: HEAD + 1, SLC: HEAD + 1}
WIN_TILES = 256 // P + 1

PIECES = ("squares", "fill qq", "sums", "read qq", "normalise", "fill kz", "high", "read kz", "low",
          "fill scores", "read scores", "fill output", "read output", "fill k", "read k",
          "fill q0", "read q0", "fill q1", "read q1", "output sums")
FILLS = [piece[5:] for piece in PIECES if piece.startswith("fill")]
DVE_FILLS = ("scores", "output")


def merge(a, b):
    done_a = done_b = 0
    merged = []
    while done_a < len(a) or done_b < len(b):
        if done_b == len(b) or (done_a < len(a) and (2 * done_a + 1) * len(b) <= (2 * done_b + 1) * len(a)):
            merged.append(a[done_a])
            done_a += 1
        else:
            merged.append(b[done_b])
            done_b += 1
    return merged


class Plan:

    def __init__(self, tiles):
        units = tiles * GROUPS
        self.steps = [s for i in range(min(2, tiles)) for s in self.prep(i)]
        self.steps += self.front(0) + self.front(1) + self.selected_maxima(0)
        for u in range(units):
            i, g = divmod(u, GROUPS)
            own = [("scores", u, SLC, 0)]
            for j in range(1, i + 1):
                own += [("scores", u, SLC, j), ("values", u, SLC, j - 1)]
            ahead = []
            if u + 2 < units:
                pieces = self.prep(i + 2) if i + 2 < tiles else []
                half = len(pieces) // GROUPS
                ahead = merge(self.front(u + 2), pieces[g * half:(g + 1) * half])
            if u + 1 < units:
                ahead = merge(self.selected_maxima(u + 1), ahead)
            self.steps += merge(own, ahead) + [("values", u, SLC, i), ("post", u, SLC)]

        self.scores_n = {}
        self.maxima_n = {}
        self.probs_n = {}
        self.values_n = {}
        for s in self.steps:
            if s[0] == "row":
                self.scores_n[s[1], s[2], "row"] = len(self.scores_n)
            elif s[0] == "scores":
                self.scores_n[s[1:]] = len(self.scores_n)
                self.probs_n[s[1:]] = len(self.probs_n)
            elif s[0] == "maximum":
                self.maxima_n[s[1:]] = len(self.maxima_n)
            elif s[0] == "values":
                self.values_n[s[1:]] = len(self.values_n)
        self.probs_by = list(self.probs_n)

    @staticmethod
    def prep(i):
        return [("prep", i, piece) for piece in PIECES]

    @staticmethod
    def max_fills(u, branch):
        i = u // GROUPS
        if branch == SLC:
            return [(h, c) for h in range(HPG) for c in range(i // 4 + 1)]
        return [(h, 0) for h in range(HPG)]

    @staticmethod
    def key_tiles(u, branch):
        i = u // GROUPS
        return [0] if branch == CMP else range(max(0, i - WIN_TILES + 1) if branch == WIN else 0, i + 1)

    def selected_maxima(self, u):
        return [("maximum", u, SLC, fill) for fill in self.max_fills(u, SLC)] + [("row", u, SLC)]

    def front(self, u):
        steps = [("compressed", u)] + [("maximum", u, WIN, fill) for fill in self.max_fills(u, WIN)]
        steps.insert(3, ("weights", u))
        window = list(self.key_tiles(u, WIN))
        steps += [("scores", u, CMP, 0), ("row", u, WIN), ("values", u, CMP, 0), ("post", u, CMP),
                  ("scores", u, WIN, window[0])]
        for a, b in zip(window, window[1:]):
            steps += [("scores", u, WIN, b), ("values", u, WIN, a)]
        return steps + [("values", u, WIN, window[-1]), ("post", u, WIN), ("select", u), ("selected", u)]


def mixers_phase(nc, z, conv_w, q_gain, k_gain, tables, cmp_a, cmp_b, cmp_v, mixed_out):
    S = z.shape[0]
    NT = S // P
    NBLK = S // SLC_LEN
    assert NBLK == NBLKS
    plan = Plan(NT)
    RW = RET_HEADS * HEAD
    CW = CC - CB_
    WR = WIN_TILES + 1
    PR = 6
    QR = 3
    SR = 4
    LOADS = 5
    MAX_ROW = 96

    with ExitStack() as stack:
        m = Space(nc, stack, "mix")
        ident = m.sb("ident", [P, P])
        ident_bf = m.sb("ident_bf", [P, P], BF16)
        ones = m.sb("ones", [P, P], F32R)
        cmp_mask = m.sb("cmp_mask", [P, S], BF16)
        causal = m.sb("causal", [P, P], BF16)
        beyond = m.sb("beyond", [P, P], BF16)
        decay = m.sb("decay", [P, RET_HEADS, P])
        row_decay = m.sb("row_decay", [P, 3, RET_HEADS])
        conv_taps = m.sb("conv_taps", [P, 3, CW])
        q_gains = m.sb("q_gains", [P, HEAD])
        k_gains = m.sb("k_gains", [P, HEAD])
        neg_half = m.sb("neg_half", [P, 16])
        zt = m.sb("z", [P, 2, z.shape[1]])
        shifted = m.sb("shifted", [P, 2, 2, 2 * CW])
        rot = m.sb("rot", [P, 2, 2, HEAD])
        sel_table = m.sb("sel_table", [P, SR, 3, NBLK])
        mixed = m.sb("mixed", [P, QR, 2 * RW + NSA_HEADS * HEAD])
        r1 = m.sb("r1", [P, 8, HEAD])
        r2 = m.sb("r2", [P, 8, HEAD])
        qq = m.sb("qq", [P, RET_HEADS, P])
        kz = m.sb("kz", [P, RET_HEADS, P])
        zk = m.sb("zk", [P, RET_HEADS, P])
        qqT = m.sb("qqT", [P, RET_HEADS, P])
        kzT = m.sb("kzT", [P, RET_HEADS, P])
        ret_scores = m.sb("ret_scores", [P, RET_HEADS, P])
        state = m.sb("state", [P, RET_HEADS, HEAD])
        o_ret = m.sb("o_ret", [P, RET_HEADS, HEAD])
        o_sq = m.sb("o_sq", [P, RET_HEADS, HEAD])
        o_mean = m.sb("o_mean", [P, RET_HEADS])
        o_ssq = m.sb("o_ssq", [P, RET_HEADS])
        o_rstd = m.sb("o_rstd", [P, RET_HEADS])
        swish = m.sb("swish", [P, QR, RW])
        gates = m.sb("gates", [P, QR, 3 * NSA_HEADS])
        taps = m.sb("taps", [P, 3, CW])
        sq = m.sb("sq", [P, NSA_HEADS + 2 * GROUPS, HEAD])
        ssq = m.sb("ssq", [P, NSA_HEADS + 2 * GROUPS])
        mean = m.sb("mean", [P, NSA_HEADS + 2 * GROUPS])
        rstd = m.sb("rstd", [P, NSA_HEADS + 2 * GROUPS])
        qn = m.sb("qn", [P, NSA_HEADS, HEAD])
        kn = m.sb("kn", [P, 2 * GROUPS, HEAD])
        q_pack = m.sb("q_pack", [P, NSA_HEADS, P])
        k_pack = m.sb("k_pack", [P, 2 * GROUPS, P])
        qb = m.sb("qb", [P, QR, NSA_HEADS, P], F32R)
        qa_w = m.sb("qa_w", [P, QR, NSA_HEADS, P], F32R)
        qa_s = m.sb("qa_s", [P, QR, NSA_HEADS, P], F32R)
        ka_s = m.sb("ka_s", [P, GROUPS, S], F32R)
        kb_s = m.sb("kb_s", [P, GROUPS, S], F32R)
        ka_w = m.sb("ka_w", [P, GROUPS, WR * P], F32R)
        kb_w = m.sb("kb_w", [P, GROUPS, WR * P], F32R)
        v_s = m.sb("v_s", [P, NT, GROUPS, HEAD + 1])
        v_w = m.sb("v_w", [P, WR, GROUPS, HEAD + 1])
        probs = m.sb("probs", [P, PR, HPG * P])
        block_rows = probs[:, :, :].rearrange("p r c -> p (r c)")[64:64 + NBLK, 0:S]
        part_max = m.sb("part_max", [P, HPG, NT // 4])
        top = m.sb("top", [P, 3, HPG])
        neg_max = m.sb("neg_max", [P, 3, HPG])
        diag = {SLC: m.sb("diag_selected", [P, HPG, P], F32R), WIN: m.sb("diag_window", [P, HPG, P], F32R)}
        cmp_weights = m.sb("cmp_weights", [P, HPG, P])
        cmp_sum = m.sb("cmp_sum", [P, HPG])
        den = m.sb("den", [P, HPG])
        weight = m.sb("weight", [P, HPG])
        importance = m.sb("importance", [P, HPG, NBLK])
        sel_score = m.sb("sel_score", [P, NBLK])
        best = m.sb("best", [P, TOPK])
        chosen = m.sb("chosen", [P, NBLK])
        selection = m.sb("selection", [P, P])
        weighted = m.sb("weighted", [P, HPG, HEAD])

        score_ps = [m.ps(f"score{b}", [P, BANK]) for b in range(2)]
        maxima_ps = [m.ps(f"maxima{b}", [P, BANK]) for b in range(2)]
        selected_ps = [m.ps(f"selected{b}", [P, BANK]) for b in range(2)]
        front_ps = m.ps("front", [P, BANK])
        prep_ps = m.ps("prep", [P, BANK])

        const_in = m.sem("const_in")
        const_set = m.sem("const_set")
        const_cast = m.sem("const_cast")
        tile_in = m.sems("tile_in", 2)
        mixed_stored = m.sems("mixed_stored", QR)
        v_ready = m.sem("v_ready")
        rot_ready = m.sem("rot_ready")
        squared = m.sem("squared")
        exps_ready = m.sem("exps_ready")
        ssq_ready = m.sem("ssq_ready")
        gates_ready = m.sem("gates_ready")
        rstd_ready = m.sem("rstd_ready")
        normed = m.sem("normed")
        high_ready = m.sem("high_ready")
        packs_ready = m.sem("packs_ready")
        prep_sum = m.sem("prep_sum")
        prep_read_act = m.sem("prep_read_act")
        prep_read_dve = m.sem("prep_read_dve")
        o_ready = m.sem("o_ready")
        o_squared = m.sem("o_squared")
        o_ssq_ready = m.sem("o_ssq_ready")
        pool_mixed = m.sem("pool_mixed")
        compressed_sum = m.sem("compressed_sum")
        cmp_max_ready = m.sem("cmp_max_ready")
        cmp_weighted = m.sem("cmp_weighted")
        diag_ready = {SLC: m.sem("diag_selected_ready"), WIN: m.sem("diag_window_ready")}
        score_sum = m.sem("score_sum")
        score_read = m.sem("score_read")
        maxima_sum = m.sem("maxima_sum")
        maxima_read = m.sem("maxima_read")
        probs_used = m.sem("probs_used")
        front_read = m.sem("front_read")
        selected_read = m.sem("selected_read")
        sel_ready = m.sem("sel_ready")
        select_sum = m.sem("select_sum")
        rows_set = m.sem("rows_set")
        nsa_mixed = m.sem("nsa_mixed")
        dve_done = m.sem("dve_done")
        pool_done = m.sem("pool_done")

        CONSTS = 9
        block = stack.enter_context(nc.Block())

        def tile_loaded(eng, i):
            eng.wait_ge(tile_in[i % 2], 16 * LOADS * (i // 2 + 1))

        def fill_n(i, name):
            return len(FILLS) * i + FILLS.index(name)

        def prep_read(eng, i, name):
            mine, sem = (True, prep_read_dve) if name in DVE_FILLS else (False, prep_read_act)
            same = [f for f in FILLS if (f in DVE_FILLS) == mine]
            eng.wait_ge(sem, len(same) * i + same.index(name) + 1)

        def last_use(eng, u, branch):
            eng.wait_ge(probs_used, plan.values_n[u, branch, plan.key_tiles(u, branch)[-1]] + 1)

        @block.sync
        def _(sp):
            sp.dma_start(ident[:, :], tables["identity"]).then_inc(const_in, 16)
            sp.dma_start(block_rows, tables["block_rows"]).then_inc(const_in, 16)
            sp.dma_start(decay[:, :, :], tables["decay"]).then_inc(const_in, 16)
            sp.dma_start(row_decay[:, :, :], tables["row_decay"]).then_inc(const_in, 16)
            for k in range(3):
                sp.dma_start(conv_taps[:, k, :], conv_w[k].partition_broadcast(P)).then_inc(const_in, 16)
            sp.dma_start(q_gains[:, :], q_gain.partition_broadcast(P)).then_inc(const_in, 16)
            sp.dma_start(k_gains[:, :], k_gain.partition_broadcast(P)).then_inc(const_in, 16)
            sp.wait_ge(const_set, 1)

            def load(i):
                b, rows = i % 2, slice(i * P, (i + 1) * P)
                if i >= 2:
                    sp.wait_ge(pool_mixed, i - 1)
                    sp.wait_ge(packs_ready, i - 1)
                    sp.wait_ge(gates_ready, i - 1)
                    sp.wait_ge(exps_ready, i - 1)
                    sp.wait_ge(prep_sum, fill_n(i - 2, "output") + 1)
                if i >= SR:
                    sp.wait_ge(sel_ready, GROUPS * (i - SR + 1))
                sp.dma_start(zt[:, b, :], z[rows, :]).then_inc(tile_in[b], 16)
                for s in (1, 2):
                    cut = s if i == 0 else 0
                    sp.dma_start(shifted[cut:, b, s - 1, :], z[i * P - s + cut:(i + 1) * P - s, CC:CC + 2 * CW])\
                        .then_inc(tile_in[b], 16)
                sp.dma_start(rot[:, b, :, :], tables["rotation"][rows, :, :]).then_inc(tile_in[b], 16)
                sp.dma_start(sel_table[:, i % SR, :, :], tables["selection"][rows, :, :]).then_inc(tile_in[b], 16)

            for i in range(3):
                load(i)
            for i in range(NT):
                if i + 3 < NT:
                    load(i + 3)
                sp.wait_ge(pool_mixed, i + 1)
                sp.wait_ge(nsa_mixed, GROUPS * (i + 1))
                sp.dma_start(mixed_out[i * P:(i + 1) * P, :], mixed[:, i % QR, :]).then_inc(mixed_stored[i % QR], 16)
            for b in range(QR):
                sp.wait_ge(mixed_stored[b], 16 * len(range(b, NT, QR)))

        @block.gpsimd
        def _(pool):
            link = chain(pool, pool_done)

            def mask(tensor, pattern, base, channel):
                link(nc.gpsimd.memset(tensor[:, :], 0.0))
                link(nc.gpsimd.affine_select(out=tensor[:, :], in_=tensor[:, :], compare_op=ALU.is_ge,
                                             fill=MASKED, base=base, pattern=pattern,
                                             channel_multiplier=channel))

            link(nc.gpsimd.memset(shifted[:, 0, :, :], 0.0))
            link(nc.gpsimd.memset(neg_half[:, :], -0.5))
            link(nc.gpsimd.memset(kz[:, :, :], 0.0))
            link(nc.gpsimd.memset(zk[:, :, :], 0.0))
            link(nc.gpsimd.memset(state[:, :, :], 0.0))
            link(nc.gpsimd.memset(selection[:, :], 0.0))
            link(nc.gpsimd.memset(ones[:, :].bitcast(F32), 1.0))
            link(nc.gpsimd.memset(v_s[:, :, :, HEAD:], 1.0))
            link(nc.gpsimd.memset(v_w[:, :, :, HEAD:], 1.0))
            for t in (qa_w, qa_s):
                link(nc.gpsimd.memset(t[64:, :, :, :].bitcast(F32), 0.0))
            link(nc.gpsimd.memset(ka_w[64:, :, :].bitcast(F32), 0.0))
            link(nc.gpsimd.memset(ka_w[MAX_ROW:MAX_ROW + 1, :, :].bitcast(F32), 1.0))
            link(nc.gpsimd.memset(ka_s[MAX_ROW:MAX_ROW + 1, :, :].bitcast(F32), 1.0))
            mask(cmp_mask, [[1, S]], -(CMP_LEN - 1), -STRIDE)
            mask(causal, [[1, P]], 0, -1)
            mask(beyond, [[-1, P]], -1, 1)
            link(nc.gpsimd.memset(ident_bf[:, :], 0.0))
            nc.gpsimd.affine_select(out=ident_bf[:, :], in_=ident_bf[:, :], compare_op=ALU.not_equal,
                                    fill=1.0, base=0, pattern=[[-1, P]], channel_multiplier=1)\
                .then_inc(const_set, 1)
            pool.wait_ge(const_in, 16 * CONSTS)
            pool.wait_ge(const_set, 1)

            def bc(ap, n):
                return ap.unsqueeze(2).to_broadcast([P, ap.shape[1], n])

            for i in range(NT):
                b, qr = i % 2, i % QR
                tile_loaded(pool, i)
                if i >= WR:
                    last_use(pool, GROUPS * (i - WR + WIN_TILES) - 1, WIN)
                nc.gpsimd.tensor_copy(v_w[:, i % WR, :, 0:HEAD],
                                      zt[:, b, NVW:NVW + P].rearrange("p (g d) -> p g d", g=GROUPS))\
                    .then_inc(v_ready, 1)
                nc.gpsimd.tensor_copy(v_s[:, i, :, 0:HEAD],
                                      zt[:, b, NVS:NVS + P].rearrange("p (g d) -> p g d", g=GROUPS))\
                    .then_inc(v_ready, 1)
                if i >= 1:
                    pool.wait_ge(prep_sum, fill_n(i - 1, "output") + 1)
                x = zt[:, b, 0:2 * RW].rearrange("p (h d) -> p h d", d=HEAD)
                xp = x.rearrange("p h (e two) -> p h e two", two=2)
                cos = rot[:, b, 0, :].unsqueeze(1).to_broadcast([P, 8, HEAD])
                sin = rot[:, b, 1, :].rearrange("p (e two) -> p e two", two=2)
                link(nc.gpsimd.tensor_tensor(r1[:, :, :], x, cos, ALU.mult))
                r2p = r2[:, :, :].rearrange("p h (e two) -> p h e two", two=2)
                for a in range(2):
                    link(nc.gpsimd.tensor_tensor(r2p[:, :, :, a], xp[:, :, :, 1 - a],
                                                 sin[:, :, a].unsqueeze(1).to_broadcast([P, 8, HEAD // 2]),
                                                 ALU.mult))
                link(nc.gpsimd.tensor_tensor(qq[:, :, 0:HEAD], r1[:, 0:4, :], r2[:, 0:4, :], ALU.add))
                link(nc.gpsimd.tensor_tensor(kz[:, :, 0:HEAD], r1[:, 4:8, :], r2[:, 4:8, :], ALU.add))
                link(nc.gpsimd.tensor_tensor(qq[:, :, HEAD:], qq[:, :, 0:HEAD], bc(row_decay[:, 0, :], HEAD), ALU.mult))
                nc.gpsimd.tensor_tensor(zk[:, :, HEAD:], kz[:, :, 0:HEAD], bc(row_decay[:, 1, :], HEAD), ALU.mult)\
                    .then_inc(rot_ready, 1)
                pool.wait_ge(ssq_ready, i + 1)
                if i >= 1:
                    pool.wait_ge(normed, i)
                link(nc.gpsimd.tensor_scalar(mean[:, :], ssq[:, :], 1.0 / HEAD, EPS, ALU.mult, ALU.add))
                nc.gpsimd.tensor_tensor(rstd[:, :], mean[:, :], neg_half[:, 0:NSA_HEADS + 2 * GROUPS],
                                        ALU.pow).then_inc(rstd_ready, 1)
                for k in range(3):
                    src = zt[:, b, CC:CC + 2 * CW] if k == 2 else shifted[:, b, 1 - k, :]
                    link(nc.gpsimd.tensor_tensor(taps[:, k, :], src[:, 0:CW], src[:, CW:], ALU.mult))
                link(nc.gpsimd.tensor_tensor(taps[:, :, :], taps[:, :, :], conv_taps[:, :, :], ALU.mult))
                link(nc.gpsimd.tensor_tensor(taps[:, 0, :], taps[:, 0, :], taps[:, 1, :], ALU.add))
                link(nc.gpsimd.tensor_tensor(taps[:, 0, :], taps[:, 0, :], taps[:, 2, :], ALU.add))
                if i >= QR:
                    pool.wait_ge(mixed_stored[qr], 16 * (i // QR))
                link(nc.gpsimd.tensor_tensor(mixed[:, qr, RW:RW + CW], taps[:, 0, :], zt[:, b, CB_:CB_ + CW], ALU.mult))
                pool.wait_ge(o_ready, i + 1)
                nc.gpsimd.tensor_tensor(o_sq[:, :, :], o_ret[:, :, :], o_ret[:, :, :], ALU.mult).then_inc(o_squared, 1)
                pool.wait_ge(o_ssq_ready, i + 1)
                link(nc.gpsimd.tensor_scalar(o_mean[:, :], o_ssq[:, :], 1.0 / HEAD, EPS, ALU.mult, ALU.add))
                link(nc.gpsimd.tensor_tensor(o_rstd[:, :], o_mean[:, :], neg_half[:, 0:RET_HEADS], ALU.pow))
                link(nc.gpsimd.tensor_tensor(o_sq[:, :, :], o_ret[:, :, :], bc(o_rstd[:, :], HEAD), ALU.mult))
                pool.wait_ge(gates_ready, i + 1)
                nc.gpsimd.tensor_tensor(mixed[:, qr, 0:RW], o_sq[:, :, :].rearrange("p h d -> p (h d)"),
                                        swish[:, qr, :], ALU.mult).then_inc(pool_mixed, 1)

        @block.scalar
        def _(act):
            act.wait_ge(const_in, 16 * CONSTS)
            act.wait_ge(const_set, 1)
            for g in range(GROUPS):
                nc.scalar.copy(ka_s[64:64 + NBLK, g, :], block_rows)
            nc.scalar.mul(q_gains[:, :], q_gains[:, :], HEAD ** -0.5).then_inc(const_cast, 1)
            act.wait_ge(const_cast, 1)

            for step in plan.steps:
                kind, u = step[0], step[1]
                if kind == "prep":
                    i, piece = step[1:]
                    b, qr = i % 2, i % QR
                    if piece == "squares":
                        tile_loaded(act, i)
                        if i >= 1:
                            act.wait_ge(ssq_ready, i)
                        nc.scalar.activation(sq[:, 0:NSA_HEADS, :].rearrange("p h d -> p (h d)"),
                                             zt[:, b, NQ:NQ + NSA_HEADS * HEAD], ACT.Square)
                        nc.scalar.activation(
                            sq[:, NSA_HEADS:, :].rearrange("p (k g) d -> p k (g d)", k=2),
                            zt[:, b, NKS:NKS + 4 * P].rearrange("p (k c) -> p k c", k=2)[:, :, 0:P],
                            ACT.Square).then_inc(squared, 1)
                        if i >= QR:
                            act.wait_ge(pool_mixed, i - QR + 1)
                            act.wait_ge(nsa_mixed, GROUPS * (i - QR + 1))
                        nc.scalar.activation(swish[:, qr, :], zt[:, b, RG:RG + RW], ACT.Exp, scale=-1.0)
                        nc.scalar.activation(gates[:, qr, :], zt[:, b, NG:NG + 3 * NSA_HEADS], ACT.Exp,
                                             scale=-1.0).then_inc(exps_ready, 1)
                    elif piece == "high":
                        act.wait_ge(normed, i + 1)
                        if i >= 1:
                            act.wait_ge(prep_sum, fill_n(i - 1, "q1") + 1)
                        nc.scalar.copy(q_pack[:, :, 0:HEAD].bitcast(F32R), qn[:, :, :])
                        nc.scalar.copy(k_pack[:, :, HEAD:].bitcast(F32R), kn[:, :, :]).then_inc(high_ready, 1)
                    elif piece in ("read qq", "read kz"):
                        name = piece[5:]
                        act.wait_ge(prep_sum, fill_n(i, name) + 1)
                        dst = qqT if name == "qq" else kzT
                        nc.scalar.copy(dst[:, :, :].rearrange("p h c -> p (h c)"), prep_ps[:, :])\
                            .then_inc(prep_read_act, 1)
                    elif piece == "read k":
                        act.wait_ge(prep_sum, fill_n(i, "k") + 1)
                        if i >= WR:
                            last_use(act, GROUPS * (i - WR + WIN_TILES) - 1, WIN)
                        bank = prep_ps[:, :].rearrange("p (k g c) -> p k g c", k=2, g=GROUPS)
                        s, w = slice(i * P, (i + 1) * P), slice(i % WR * P, (i % WR + 1) * P)
                        nc.scalar.copy(kb_s[:, :, s], bank[:, 0, :, :])
                        nc.scalar.copy(kb_w[:, :, w], bank[:, 1, :, :])
                        nc.scalar.copy(ka_s[0:HEAD, :, s], bank[HEAD:, 0, :, :])
                        nc.scalar.copy(ka_w[0:HEAD, :, w], bank[HEAD:, 1, :, :]).then_inc(prep_read_act, 1)
                    elif piece in ("read q0", "read q1"):
                        name = piece[5:]
                        act.wait_ge(prep_sum, fill_n(i, name) + 1)
                        if i >= QR:
                            last_use(act, GROUPS * (i - QR) + GROUPS - 1, SLC)
                        bank = prep_ps[:, :].rearrange("p (h c) -> p h c", h=HPG)
                        g = FILLS.index(name) - FILLS.index("q0")
                        h = slice(g * HPG, (g + 1) * HPG)
                        nc.scalar.copy(qb[:, qr, h, :], bank)
                        nc.scalar.copy(qa_w[0:HEAD, qr, h, :], bank[0:HEAD, :, :])
                        nc.scalar.copy(qa_s[0:HEAD, qr, h, :], bank[0:HEAD, :, :]).then_inc(prep_read_act, 1)
                elif kind == "weights":
                    act.wait_ge(cmp_max_ready, u + 1)
                    if u >= 1:
                        act.wait_ge(score_sum, plan.scores_n[u - 1, CMP, 0] + 1)
                        act.wait_ge(front_read, 2 * u - 1)
                    for h in range(HPG):
                        exp = nc.scalar.activation(cmp_weights[:, h, :], front_ps[:, h * P:(h + 1) * P], ACT.Exp,
                                                   bias=neg_max[:, CMP, h:h + 1], accum_out=cmp_sum[:, h:h + 1])
                    exp.then_inc(cmp_weighted, 1)
                elif kind == "row":
                    branch = step[2]
                    n = plan.scores_n[u, branch, "row"]
                    qr, g = u // GROUPS % QR, u % GROUPS
                    q = qa_s if branch == SLC else qa_w
                    act.wait_ge(score_sum, n + 1)
                    nc.scalar.copy(q[MAX_ROW:MAX_ROW + 1, qr, g * HPG:(g + 1) * HPG, :],
                                   score_ps[n % 2][MAX_ROW:MAX_ROW + 1, :].rearrange("p (h c) -> p h c", h=HPG))\
                        .then_inc(score_read, 1)
                elif kind == "scores":
                    n, p = plan.scores_n[step[1:]], plan.probs_n[step[1:]]
                    act.wait_ge(score_sum, n + 1)
                    if p >= PR:
                        act.wait_ge(probs_used, plan.values_n[plan.probs_by[p - PR]] + 1)
                    if step[2] == CMP:
                        ins = nc.scalar.copy(probs[:, p % PR, :], score_ps[n % 2][:, :])
                    else:
                        ins = nc.scalar.activation(probs[:, p % PR, :], score_ps[n % 2][:, :], ACT.Exp)
                    ins.then_inc(score_read, 1)

        @block.vector
        def _(dve):
            link = chain(dve, dve_done)
            dve.wait_ge(const_set, 1)
            dve.wait_ge(const_cast, 1)

            def bc(ap, n):
                return ap.unsqueeze(2).to_broadcast([P, ap.shape[1], n])

            def maxima_done(u, branch):
                link(nc.vector.tensor_scalar(neg_max[:, branch, :], top[:, branch, :], MASKED / 10, -1.0,
                                             ALU.max, ALU.mult))
                if u >= 1:
                    dve.wait_ge(score_sum, plan.scores_n[u - 1, branch, "row"] + 1)
                nc.vector.tensor_tensor(diag[branch][:, :, :], ident[:, :].unsqueeze(1).to_broadcast([P, HPG, P]),
                                        bc(neg_max[:, branch, :], P), ALU.mult).then_inc(diag_ready[branch], 1)

            for step in plan.steps:
                kind, u = step[0], step[1]
                if kind == "prep":
                    i, piece = step[1:]
                    b, qr = i % 2, i % QR
                    if piece == "sums":
                        dve.wait_ge(squared, i + 1)
                        if i >= 1:
                            dve.wait_ge(rstd_ready, i)
                        nc.vector.tensor_reduce(ssq[:, :], sq[:, :, :], AX_X, ALU.add).then_inc(ssq_ready, 1)
                        dve.wait_ge(exps_ready, i + 1)
                        for t in (swish, gates):
                            link(nc.vector.tensor_scalar(t[:, qr, :], t[:, qr, :], 1.0, None, ALU.add))
                            link(nc.vector.reciprocal(t[:, qr, :], t[:, qr, :]))
                        nc.vector.tensor_tensor(swish[:, qr, :], swish[:, qr, :], zt[:, b, RG:RG + RW],
                                                ALU.mult).then_inc(gates_ready, 1)
                    elif piece == "normalise":
                        dve.wait_ge(rstd_ready, i + 1)
                        H = NSA_HEADS
                        q = zt[:, b, NQ:NQ + H * HEAD].rearrange("p (h d) -> p h d", h=H)
                        if i >= 1:
                            dve.wait_ge(packs_ready, i)
                        link(nc.vector.tensor_tensor(qn[:, :, :], q, bc(rstd[:, 0:H], HEAD), ALU.mult))
                        for k, c in enumerate((NKS, NKW)):
                            part = slice(GROUPS * k, GROUPS * (k + 1))
                            link(nc.vector.tensor_tensor(
                                kn[:, part, :], zt[:, b, c:c + P].rearrange("p (g d) -> p g d", g=GROUPS),
                                bc(rstd[:, H + GROUPS * k:H + GROUPS * (k + 1)], HEAD), ALU.mult))
                        link(nc.vector.tensor_tensor(kn[:, :, :], kn[:, :, :],
                                                     k_gains[:, :].unsqueeze(1).to_broadcast([P, 2 * GROUPS, HEAD]),
                                                     ALU.mult))
                        nc.vector.tensor_tensor(qn[:, :, :], qn[:, :, :],
                                                q_gains[:, :].unsqueeze(1).to_broadcast([P, H, HEAD]),
                                                ALU.mult).then_inc(normed, 1)
                    elif piece == "low":
                        dve.wait_ge(normed, i + 1)
                        dve.wait_ge(high_ready, i + 1)
                        nc.vector.tensor_tensor(k_pack[:, :, 0:HEAD].bitcast(F32R), kn[:, :, :], k_pack[:, :, HEAD:],
                                                ALU.subtract)
                        nc.vector.tensor_tensor(q_pack[:, :, HEAD:].bitcast(F32R), qn[:, :, :], q_pack[:, :, 0:HEAD],
                                                ALU.subtract).then_inc(packs_ready, 1)
                    elif piece == "read scores":
                        dve.wait_ge(prep_sum, fill_n(i, "scores") + 1)
                        nc.vector.tensor_tensor(ret_scores[:, :, :].rearrange("p h c -> p (h c)"),
                                                prep_ps[:, :], decay[:, :, :].rearrange("p h c -> p (h c)"),
                                                ALU.mult).then_inc(prep_read_dve, 1)
                    elif piece == "read output":
                        dve.wait_ge(prep_sum, fill_n(i, "output") + 1)
                        bank = prep_ps[:, :].rearrange("p (two h d) -> p two h d", two=2, h=RET_HEADS)
                        if i >= 1:
                            dve.wait_ge(prep_read_dve, 2 * i)
                            dve.wait_ge(pool_mixed, i)
                        nc.vector.tensor_copy(o_ret[:, :, :], bank[:, 0, :, :]).then_inc(o_ready, 1)
                        link(nc.vector.tensor_tensor(state[:, :, :], state[:, :, :], bc(row_decay[:, 2, :], HEAD),
                                                     ALU.mult))
                        nc.vector.tensor_tensor(state[:, :, :], state[:, :, :], bank[:, 1, :, :],
                                                ALU.add).then_inc(prep_read_dve, 1)
                    elif piece == "output sums":
                        dve.wait_ge(o_squared, i + 1)
                        nc.vector.tensor_reduce(o_ssq[:, :], o_sq[:, :, :], AX_X, ALU.add).then_inc(o_ssq_ready, 1)
                elif kind == "compressed":
                    dve.wait_ge(compressed_sum, u + 1)
                    link(nc.vector.tensor_reduce(top[:, CMP, :], front_ps[:, :].rearrange("p (h n) -> p h n", h=HPG),
                                                 AX_X, ALU.max))
                    if u >= 1:
                        dve.wait_ge(cmp_weighted, u)
                    nc.vector.tensor_scalar(neg_max[:, CMP, :], top[:, CMP, :], MASKED / 10, -1.0,
                                            ALU.max, ALU.mult).then_inc(cmp_max_ready, 1)
                elif kind == "maximum":
                    branch, (h, c) = step[2:]
                    i = u // GROUPS
                    n = plan.maxima_n[u, branch, (h, c)]
                    bank = maxima_ps[n % 2]
                    dve.wait_ge(maxima_sum, n + 1)
                    keys = (len(plan.key_tiles(u, branch)) if branch == WIN else min(4, i + 1 - 4 * c)) * P
                    dst = top[:, WIN, h:h + 1] if branch == WIN else part_max[:, h, c:c + 1]
                    nc.vector.tensor_reduce(dst, bank[:, 0:keys], AX_X, ALU.max).then_inc(maxima_read, 1)
                    if (h, c) == plan.max_fills(u, branch)[-1]:
                        dve.wait_ge(maxima_read, n + 1)
                        if branch == SLC:
                            link(nc.vector.tensor_reduce(top[:, SLC, :], part_max[:, :, 0:c + 1], AX_X, ALU.max))
                        maxima_done(u, branch)
                elif kind == "selected":
                    qr, g = u // GROUPS % QR, u % GROUPS
                    dve.wait_ge(select_sum, u + 1)
                    nc.vector.tensor_copy(qa_s[64:64 + NBLK, qr, g * HPG:(g + 1) * HPG, :],
                                          front_ps[64:64 + NBLK, BANK - P:].unsqueeze(1)
                                          .to_broadcast([NBLK, HPG, P])).then_inc(rows_set, 1)
                elif kind == "post":
                    branch = step[2]
                    i, g = divmod(u, GROUPS)
                    qr = i % QR
                    last_use(dve, u, branch)
                    out = (selected_ps[u % 2] if branch == SLC else front_ps)[:, 0:HPG * VCOLS[branch]]\
                        .rearrange("p (h c) -> p h c", h=HPG)
                    dst = mixed[:, qr, 2 * RW + g * HPG * HEAD:2 * RW + (g + 1) * HPG * HEAD]\
                        .rearrange("p (h d) -> p h d", h=HPG)
                    gate = gates[:, qr, :].rearrange("p (h c) -> p h c", c=3)[:, g * HPG:(g + 1) * HPG, branch]
                    if branch == CMP:
                        dve.wait_ge(cmp_weighted, u + 1)
                        link(nc.vector.tensor_scalar(den[:, :], cmp_sum[:, :], 1e-30, None, ALU.max))
                        link(nc.vector.reciprocal(den[:, :], den[:, :]))
                        link(nc.vector.tensor_tensor(importance[:, :, :], out[:, :, HEAD:],
                                                     bc(den[:, :], NBLK), ALU.mult))
                        link(nc.vector.tensor_tensor(weight[:, :], den[:, :], gate, ALU.mult))
                        if i >= QR and g == 0:
                            dve.wait_ge(mixed_stored[qr], 16 * (i // QR))
                        nc.vector.tensor_tensor(dst, out[:, :, 0:HEAD], bc(weight[:, :], HEAD), ALU.mult)\
                            .then_inc(front_read, 1)
                        dve.wait_ge(front_read, 2 * u + 1)
                        link(nc.vector.tensor_reduce(sel_score[:, :],
                                                     importance[:, :, :].rearrange("p h j -> p j h"),
                                                     AX_X, ALU.add))
                        for t, op in ((0, ALU.add), (1, ALU.mult), (2, ALU.add)):
                            link(nc.vector.tensor_tensor(sel_score[:, :], sel_score[:, :],
                                                         sel_table[:, i % SR, t, :], op))
                        link(nc.vector.max(best[:, :], sel_score[:, :]))
                        link(nc.vector.match_replace(chosen[:, :], best[:, :], sel_score[:, :], -3e38))
                        if u >= 1:
                            dve.wait_ge(select_sum, u)
                        nc.vector.tensor_scalar(selection[:, 64:64 + NBLK], chosen[:, :], -1e38, MASKED,
                                                ALU.is_gt, ALU.mult).then_inc(sel_ready, 1)
                        dve.wait_ge(sel_ready, u + 1)
                    else:
                        read, count = (selected_read, u + 1) if branch == SLC else (front_read, 2 * u + 2)
                        link(nc.vector.tensor_scalar(den[:, :], out[:, :, HEAD], 1e-30, None, ALU.max))
                        link(nc.vector.reciprocal(den[:, :], den[:, :]))
                        link(nc.vector.tensor_tensor(weight[:, :], den[:, :], gate, ALU.mult))
                        nc.vector.tensor_tensor(weighted[:, :, :], out[:, :, 0:HEAD], bc(weight[:, :], HEAD),
                                                ALU.mult).then_inc(read, 1)
                        dve.wait_ge(read, count)
                        add = nc.vector.tensor_tensor(dst, dst, weighted[:, :, :], ALU.add)
                        if branch == SLC:
                            add.then_inc(nsa_mixed, 1)
                            dve.wait_ge(nsa_mixed, u + 1)
                        else:
                            link(add)

        @block.tensor
        def _(pe):
            pe.wait_ge(const_in, 16 * CONSTS)
            pe.wait_ge(const_set, 1)
            pe.wait_ge(const_cast, 1)

            for step in plan.steps:
                kind, u = step[0], step[1]
                i, g = divmod(u, GROUPS)
                qr = i % QR
                if kind == "prep":
                    i, piece = step[1:]
                    b = i % 2
                    if not piece.startswith("fill"):
                        continue
                    name = piece[5:]
                    if name != FILLS[0]:
                        prep_read(pe, i, FILLS[FILLS.index(name) - 1])
                    elif i >= 1:
                        prep_read(pe, i - 1, FILLS[-1])
                    if name in ("qq", "kz"):
                        pe.wait_ge(rot_ready, i + 1)
                        for h in range(RET_HEADS):
                            mm = nc.tensor.transpose(prep_ps[:, h * P:(h + 1) * P], (qq if name == "qq" else kz)[:, h, :],
                                                     ident[:, :])
                    elif name == "scores":
                        for h in range(RET_HEADS):
                            mm = nc.tensor.matmul(prep_ps[:, h * P:(h + 1) * P], kzT[:, h, :], qqT[:, h, :],
                                                  start=True, stop=True)
                    elif name == "output":
                        for h in range(RET_HEADS):
                            v = zt[:, b, RV + h * HEAD:RV + (h + 1) * HEAD]
                            o = prep_ps[:, h * HEAD:(h + 1) * HEAD]
                            nc.tensor.matmul(o, ret_scores[:, h, :], v, start=True, stop=False)
                            nc.tensor.matmul(o, qqT[:, h, :], state[:, h, :], start=False, stop=True)
                            mm = nc.tensor.matmul(prep_ps[:, RW + h * HEAD:RW + (h + 1) * HEAD], zk[:, h, :], v,
                                                  start=True, stop=True)
                    else:
                        pe.wait_ge(packs_ready, i + 1)
                        for h in range(HPG):
                            src = {"k": k_pack[:, h, :], "q0": q_pack[:, h, :], "q1": q_pack[:, HPG + h, :]}[name]
                            mm = nc.tensor.transpose(prep_ps[:, h * P:(h + 1) * P], src, ident[:, :])
                    mm.then_inc(prep_sum, 1)
                elif kind == "compressed":
                    prep_read(pe, i, "q1")
                    if u >= 1:
                        pe.wait_ge(rows_set, u)
                    nc.tensor.matmul(front_ps[:, :], cmp_mask[:, i * P:(i + 1) * P],
                                     ident_bf[:, :].unsqueeze(1).to_broadcast([P, HPG, P]),
                                     start=True, stop=False, skip_group_check=True)
                    for h in range(HPG):
                        out = front_ps[:, h * P:(h + 1) * P]
                        nc.tensor.matmul(out, qb[0:HEAD, qr, g * HPG + h, :], cmp_a[0:HEAD, g, :],
                                         start=False, stop=False, skip_group_check=True)
                        mm = nc.tensor.matmul(out, qb[:, qr, g * HPG + h, :], cmp_b[:, g, :],
                                              start=False, stop=h == HPG - 1, skip_group_check=True)
                    mm.then_inc(compressed_sum, 1)
                elif kind == "maximum":
                    branch, (h, c) = step[2:]
                    n = plan.maxima_n[u, branch, (h, c)]
                    bank = maxima_ps[n % 2]
                    if n >= 2:
                        pe.wait_ge(maxima_read, n - 1)
                    if branch == WIN:
                        for s, j in enumerate(plan.key_tiles(u, WIN)):
                            out = bank[:, s * P:(s + 1) * P]
                            mask = {i: causal, i - 2: beyond}.get(j)
                            mm = nc.tensor.matmul(out, qb[0:HEAD, qr, g * HPG + h, :],
                                                  ka_w[0:HEAD, g, j % WR * P:(j % WR + 1) * P],
                                                  start=True, stop=mask is None)
                            if mask is not None:
                                mm = nc.tensor.matmul(out, mask[:, :], ident_bf[:, :], start=False, stop=True)
                    else:
                        if (h, c) == (0, 0):
                            pe.wait_ge(rows_set, u + 1)
                        keys = min(4, i + 1 - 4 * c) * P
                        own = i // 4 == c
                        mm = nc.tensor.matmul(bank[:, 0:keys], qa_s[0:96, qr, g * HPG + h, :],
                                              ka_s[0:96, g, 4 * c * P:4 * c * P + keys],
                                              start=True, stop=not own, skip_group_check=True)
                        if own:
                            mm = nc.tensor.matmul(bank[:, keys - P:keys], causal[:, :], ident_bf[:, :],
                                                  start=False, stop=True, skip_group_check=True)
                    mm.then_inc(maxima_sum, 1)
                elif kind == "select":
                    pe.wait_ge(sel_ready, u + 1)
                    pe.wait_ge(front_read, 2 * u + 2)
                    nc.tensor.transpose(front_ps[:, BANK - P:], selection[:, :], ident[:, :]).then_inc(select_sum, 1)
                elif kind == "row":
                    branch = step[2]
                    n = plan.scores_n[u, branch, "row"]
                    if n >= 2:
                        pe.wait_ge(score_read, n - 1)
                    pe.wait_ge(diag_ready[branch], u + 1)
                    nc.tensor.matmul(score_ps[n % 2][:, :], ones[:, :], diag[branch][:, :, :],
                                     start=True, stop=True).then_inc(score_sum, 1)
                elif kind == "scores":
                    branch, j = step[2:]
                    n = plan.scores_n[u, branch, j]
                    bank = score_ps[n % 2]
                    if n >= 2:
                        pe.wait_ge(score_read, n - 1)
                    if branch == CMP:
                        pe.wait_ge(cmp_weighted, u + 1)
                        for h in range(HPG):
                            mm = nc.tensor.transpose(bank[:, h * P:(h + 1) * P], cmp_weights[:, h, :], ident[:, :])
                        mm.then_inc(score_sum, 1)
                        continue
                    pe.wait_ge(score_read, plan.scores_n[u, branch, "row"] + 1)
                    heads = slice(g * HPG, (g + 1) * HPG)
                    if branch == WIN:
                        ka, kb, cols, qa = ka_w, kb_w, slice(j % WR * P, (j % WR + 1) * P), qa_w
                        mask = {i: causal[:, :], i - 2: beyond[:, :]}.get(j)
                    else:
                        ka, kb, cols, qa = ka_s, kb_s, slice(j * P, (j + 1) * P), qa_s
                        mask = causal[:, :] if j == i else None
                    nc.tensor.matmul(bank[:, :], ka[0:MAX_ROW + 1, g, cols], qa[0:MAX_ROW + 1, qr, heads, :],
                                     start=True, stop=False)
                    mm = nc.tensor.matmul(bank[:, :], kb[:, g, cols], qb[:, qr, heads, :], start=False,
                                          stop=mask is None)
                    if mask is not None:
                        mm = nc.tensor.matmul(bank[:, :], ident_bf[:, :], mask.unsqueeze(1).to_broadcast([P, HPG, P]),
                                              start=False, stop=True)
                    mm.then_inc(score_sum, 1)
                elif kind == "values":
                    branch, j = step[2:]
                    n, p = plan.scores_n[u, branch, j], plan.probs_n[u, branch, j]
                    tiles = plan.key_tiles(u, branch)
                    pe.wait_ge(score_read, n + 1)
                    if j == tiles[0]:
                        if branch == SLC and u >= 2:
                            pe.wait_ge(selected_read, u - 1)
                        elif branch == CMP:
                            pe.wait_ge(cmp_weighted, u + 1)
                        elif branch == WIN:
                            pe.wait_ge(front_read, 2 * u + 1)
                    if branch != CMP:
                        pe.wait_ge(v_ready, 2 * (j + 1))
                    v = {CMP: cmp_v[:, g, :], WIN: v_w[:, j % WR, g, :], SLC: v_s[:, j, g, :]}[branch]
                    out = (selected_ps[u % 2] if branch == SLC else front_ps)[:, 0:HPG * VCOLS[branch]]\
                        .rearrange("p (h c) -> p h c", h=HPG)
                    for h in range(HPG):
                        mm = nc.tensor.matmul(out[:, h, :], probs[:, p % PR, h * P:(h + 1) * P], v,
                                              start=j == tiles[0] and h == 0, stop=j == tiles[-1],
                                              skip_group_check=True)
                    mm.then_inc(probs_used, 1)


def output_phase(nc, mixed, x, w_out, identity, x2):
    S, D = x.shape
    M = mixed.shape[1]
    KT = M // P
    NT = S // P
    CB = D // BANK
    GB = M // BANK

    with ExitStack() as stack:
        m = Space(nc, stack, "out")
        ident = m.sb("ident", [P, P])
        w_raw = m.sb("w_raw", [P, 2, D])
        w_hi = m.sb("w_hi", [P, KT, D], F32R)
        w_lo = m.sb("w_lo", [P, KT, D], F32R)
        mt = m.sb("mixed", [P, 2, M])
        xt = m.sb("x", [P, 2, D])
        t_hi = m.sb("mixedT_hi", [P, 2, KT, P], F32R)
        t_lo = m.sb("mixedT_lo", [P, 2, KT, P], F32R)
        tp = [m.ps(f"transposed{i}", [P, BANK]) for i in range(2 * GB)]
        acc = [m.ps(f"acc{i}", [P, BANK]) for i in range(2 * CB)]

        ident_in = m.sem("ident_in")
        w_loaded = m.sems("w_loaded", 2)
        w_hi_done = m.sem("w_hi_done")
        w_lo_done = m.sem("w_lo_done")
        mixed_in = m.sems("mixed_in", 2)
        x_in = m.sems("x_in", 2)
        transposed = m.sem("transposed")
        hi_done = m.sem("hi_done")
        lo_done = m.sem("lo_done")
        product = m.sem("product")
        added = m.sem("added")
        stored = m.sems("stored", 2)
        block = stack.enter_context(nc.Block())

        @block.sync
        def _(sp):
            sp.dma_start(ident[:, :], identity).then_inc(ident_in, 16)
            for k in range(KT):
                if k >= 2:
                    sp.wait_ge(w_lo_done, k - 1)
                sp.dma_start(w_raw[:, k % 2, :], w_out[k * P:(k + 1) * P, :]).then_inc(w_loaded[k % 2], 16)
            for b in range(2):
                sp.sem_inc(stored[b], 16)
            with sp.Fori(0, NT // 2) as r:
                for b in range(2):
                    i = r * 2
                    sp.wait_ge(transposed, i + (b + 1))
                    sp.dma_start(mt[:, b, :], mixed[bass.ds((i + b) * P, P), :]).then_inc(mixed_in[b], 16)
                    sp.wait_ge(stored[b], i * 8 + 16)
                    sp.dma_start(xt[:, b, :], x[bass.ds((i + b) * P, P), :]).then_inc(x_in[b], 16)

        @block.gpsimd
        def _(pool):
            for k in range(KT):
                pool.wait_ge(w_hi_done, k + 1)
                nc.gpsimd.tensor_tensor(w_lo[:, k, :], w_raw[:, k % 2, :], w_hi[:, k, :].bitcast(F32),
                                        ALU.subtract).then_inc(w_lo_done, 1)

        @block.scalar
        def _(act):
            for k in range(KT):
                act.wait_ge(w_loaded[k % 2], 16 * (k // 2 + 1))
                nc.scalar.copy(w_hi[:, k, :], w_raw[:, k % 2, :]).then_inc(w_hi_done, 1)
            act.sem_inc(hi_done, 2)

            def high(i, b):
                act.wait_ge(transposed, i + (b + 3))
                act.wait_ge(product, i + (b + 1))
                for q in range(GB):
                    copy = nc.scalar.copy(t_hi[:, b, 4 * q:4 * q + 4, :],
                                          tp[b * GB + q][:, :].rearrange("p (k c) -> p k c", c=P))
                copy.then_inc(hi_done, 1)

            def store(i, b):
                act.wait_ge(added, i + (b + 3))
                act.dma_start(x2[bass.ds((i + b) * P, P), :], xt[:, b, :]).then_inc(stored[b], 16)

            high(0, 0)
            with act.Fori(0, NT // 2 - 1) as r:
                high(r * 2, 1)
                store(r * 2, 0)
                high(r * 2 + 2, 0)
                store(r * 2, 1)
            high(NT - 2, 1)
            store(NT - 2, 0)
            store(NT - 2, 1)
            for b in range(2):
                act.wait_ge(stored[b], 16 * (NT // 2 + 1))

        @block.vector
        def _(dve):
            def low(i, b):
                dve.wait_ge(hi_done, i + (b + 3))
                for q in range(GB):
                    sub = nc.vector.tensor_tensor(t_lo[:, b, 4 * q:4 * q + 4, :],
                                                  tp[b * GB + q][:, :].rearrange("p (k c) -> p k c", c=P),
                                                  t_hi[:, b, 4 * q:4 * q + 4, :].bitcast(F32), ALU.subtract)
                sub.then_inc(lo_done, 1)

            def add(i, b):
                dve.wait_ge(product, i + (b + 3))
                dve.wait_ge(x_in[b], i * 8 + 16)
                for c in range(CB):
                    cols = slice(c * BANK, (c + 1) * BANK)
                    ins = nc.vector.tensor_tensor(xt[:, b, cols], xt[:, b, cols], acc[b * CB + c][:, :], ALU.add)
                ins.then_inc(added, 1)

            dve.sem_inc(lo_done, 2)
            dve.sem_inc(added, 2)
            low(0, 0)
            with dve.Fori(0, NT - 2, 2) as i:
                low(i, 1)
                add(i, 0)
                low(i + 2, 0)
                add(i, 1)
            low(NT - 2, 1)
            add(NT - 2, 0)
            add(NT - 2, 1)

        @block.tensor
        def _(pe):
            def transpose(i, b):
                pe.wait_ge(mixed_in[b], i * 8 + 16)
                pe.wait_ge(lo_done, i + (b + 1))
                for k in range(KT):
                    mm = nc.tensor.transpose(tp[b * GB + k // 4][:, k % 4 * P:k % 4 * P + P],
                                             mt[:, b, k * P:(k + 1) * P], ident[:, :])
                mm.then_inc(transposed, 1)

            def multiply(i, b):
                pe.wait_ge(lo_done, i + (b + 3))
                pe.wait_ge(added, i + (b + 1))
                for c in range(CB):
                    for k in range(KT):
                        for a, w in ((t_hi, w_hi), (t_lo, w_hi), (t_hi, w_lo)):
                            mm = nc.tensor.matmul(acc[b * CB + c][:, :], a[:, b, k, :],
                                                  w[:, k, c * BANK:(c + 1) * BANK],
                                                  start=k == 0 and a is t_hi and w is w_hi,
                                                  stop=k == KT - 1 and w is w_lo)
                mm.then_inc(product, 1)

            pe.wait_ge(ident_in, 16)
            pe.sem_inc(transposed, 2)
            pe.sem_inc(product, 2)
            transpose(0, 0)
            pe.wait_ge(w_lo_done, KT)
            with pe.Fori(0, NT - 2, 2) as i:
                transpose(i, 1)
                multiply(i, 0)
                transpose(i + 2, 0)
                multiply(i, 1)
            transpose(NT - 2, 1)
            multiply(NT - 2, 0)
            multiply(NT - 2, 1)


def mlp_phase(nc, x2, norm_mlp, w_up, w_down, identity, out):
    S, D = x2.shape
    FF = w_up.shape[1]
    KT = D // P
    T = BANK
    TT = T // P
    GROUPS = S // T
    FB = 2 * P
    FT = FB // P
    NB = FF // FB
    CB = D // BANK
    GB = D // BANK
    SUMS = TT * CB
    AR = 4

    with ExitStack() as stack:
        m = Space(nc, stack, "mlp")
        ident = m.sb("ident", [P, P])
        gain = m.sb("gain", [P, D])
        neg_half = m.sb("neg_half", [P, 1])
        y = m.sb("y", [P, 2, TT, D])
        xn = m.sb("x_normed", [P, TT, D])
        squares = m.sb("squares", [P, TT, D], BF16)
        sum_sq = m.sb("sum_sq", [P, TT])
        mean_sq = m.sb("mean_sq", [P, TT])
        rstd = m.sb("rstd", [P, TT])
        h_hi = m.sb("hT_hi", [P, KT, T], F32R)
        h_lo = m.sb("hT_lo", [P, KT, T], F32R)
        up_raw = m.sb("up_raw", [P, KT, FB])
        up_hi = m.sb("up_hi", [P, 2, KT, FB], F32R)
        up_lo = m.sb("up_lo", [P, 2, KT, FB], F32R)
        dn_raw = m.sb("down_raw", [P, FT, D])
        dn_hi = m.sb("down_hi", [P, 2, FT, D], F32R)
        dn_lo = m.sb("down_lo", [P, 2, FT, D], F32R)
        relu = m.sb("relu", [P, 2, T])
        f = m.sb("f", [P, 2, T])
        f_hi = m.sb("f_hi", [P, 2, FT, T], F32R)
        f_lo = m.sb("f_lo", [P, 2, FT, T], F32R)
        tp = [m.ps(f"transposed{i}", [P, BANK]) for i in range(GB)]
        up_ps = [m.ps(f"up{i}", [P, BANK]) for i in range(2)]
        acc = [m.ps(f"acc{i}", [P, BANK]) for i in range(AR)]

        const_in = m.sem("const_in")
        const_set = m.sem("const_set")
        y_in = m.sems("y_in", 2)
        y_out = m.sems("y_out", 2)
        squared = m.sem("squared")
        mean_done = m.sem("mean_done")
        rstd_done = m.sem("rstd_done")
        normed = m.sem("normed")
        transposed = m.sem("transposed")
        hi_done = m.sem("hi_done")
        lo_done = m.sem("lo_done")
        up_loaded = m.sem("up_loaded")
        dn_loaded = m.sem("down_loaded")
        up_hi_done = m.sem("up_hi_done")
        dn_hi_done = m.sem("down_hi_done")
        up_lo_done = m.sem("up_lo_done")
        dn_lo_done = m.sem("down_lo_done")
        up_sum = m.sem("up_sum")
        relu_done = m.sem("relu_done")
        f_done = m.sem("f_done")
        f_hi_done = m.sem("f_hi_done")
        f_lo_done = m.sem("f_lo_done")
        dn_sum = m.sem("down_sum")
        added = m.sem("added")

        up_view = w_up.rearrange("(k p) f -> p k f", p=P)
        dn_view = w_down.rearrange("(k p) n -> p k n", p=P)
        block = stack.enter_context(nc.Block())

        @block.sync
        def _(sp):
            def load_y(g):
                b = g % 2
                sp.wait_ge(y_out[b], 16 * (g // 2 + 1))
                sp.dma_start(y[:, b, :, :], x2[g * T:(g + 1) * T, :].rearrange("(t p) d -> p t d", p=P))\
                    .then_inc(y_in[b], 16)

            def store_y(g):
                sp.wait_ge(added, (g + 1) * NB * SUMS + AR)
                sp.dma_start(out[g * T:(g + 1) * T, :].rearrange("(t p) d -> p t d", p=P), y[:, g % 2, :, :])\
                    .then_inc(y_out[g % 2], 16)

            AHEAD = 3
            sp.dma_start(ident[:, :], identity).then_inc(const_in, 16)
            sp.dma_start(gain[:, :], norm_mlp.partition_broadcast(P)).then_inc(const_in, 16)
            for b in range(2):
                sp.sem_inc(y_out[b], 16)
            load_y(0)
            def load_w(n, c):
                sp.wait_ge(up_lo_done, n + 1)
                sp.dma_start(up_raw[:, :, :], up_view[:, :, bass.ds(c * FB, FB)]).then_inc(up_loaded, 16)
                sp.wait_ge(dn_lo_done, n + 1)
                sp.dma_start(dn_raw[:, :, :], dn_view[:, bass.ds(c * FT, FT), :]).then_inc(dn_loaded, 16)

            for g in range(GROUPS):
                for c in range(AHEAD):
                    load_w(g * NB + c, c)
                if g > 0:
                    store_y(g - 1)
                if g + 1 < GROUPS:
                    load_y(g + 1)
                with sp.Fori(0, NB - AHEAD) as r:
                    load_w(r + (g * NB + AHEAD), r + AHEAD)
            store_y(GROUPS - 1)
            sp.wait_ge(y_out[0], 16 * (GROUPS // 2 + 1))
            sp.wait_ge(y_out[1], 16 * (GROUPS // 2 + 1))

        @block.gpsimd
        def _(pool):
            pool.sem_inc(up_lo_done, 1)
            pool.sem_inc(dn_lo_done, 1)
            nc.gpsimd.memset(neg_half[:, :], -0.5).then_inc(const_set, 1)
            pool.wait_ge(const_set, 1)

            def split_up(n, b):
                pool.wait_ge(up_hi_done, n + 1)
                nc.gpsimd.tensor_tensor(up_lo[:, b, :, :], up_raw[:, :, :], up_hi[:, b, :, :].bitcast(F32),
                                        ALU.subtract).then_inc(up_lo_done, 1)

            def split_down(n, b):
                pool.wait_ge(dn_hi_done, n + 1)
                nc.gpsimd.tensor_tensor(dn_lo[:, b, :, :], dn_raw[:, :, :], dn_hi[:, b, :, :].bitcast(F32),
                                        ALU.subtract).then_inc(dn_lo_done, 1)

            def root(g):
                if g >= 1:
                    pool.wait_ge(normed, g * TT)
                for t in range(TT):
                    pool.wait_ge(squared, g * TT + t + 1)
                    nc.gpsimd.tensor_scalar(mean_sq[:, t:t + 1], sum_sq[:, t:t + 1], 1.0 / D, EPS,
                                            ALU.mult, ALU.add).then_inc(mean_done, 1)
                    pool.wait_ge(mean_done, g * TT + t + 1)
                    nc.gpsimd.tensor_tensor(rstd[:, t:t + 1], mean_sq[:, t:t + 1], neg_half[:, :],
                                            ALU.pow).then_inc(rstd_done, 1)

            root(0)
            for g in range(GROUPS):
                with pool.Fori(0, NB - 2, 2) as c:
                    for b in range(2):
                        split_up(c + (g * NB + b), b)
                        split_down(c + (g * NB + b), b)
                n = (g + 1) * NB - 2
                split_up(n, 0)
                split_down(n, 0)
                if g + 1 < GROUPS:
                    root(g + 1)
                split_up(n + 1, 1)
                split_down(n + 1, 1)

        @block.scalar
        def _(act):
            def split_up(n, b):
                act.wait_ge(up_loaded, n * 16 + 16)
                act.wait_ge(up_sum, (n + 1) * FT)
                nc.scalar.copy(up_hi[:, b, :, :], up_raw[:, :, :]).then_inc(up_hi_done, 1)

            def split_down(n, b):
                act.wait_ge(dn_loaded, n * 16 + 16)
                act.wait_ge(dn_sum, (n + 1) * SUMS)
                nc.scalar.copy(dn_hi[:, b, :, :], dn_raw[:, :, :]).then_inc(dn_hi_done, 1)

            def relu_and_hi(n, b):
                for t in range(FT):
                    k = n * FT + t
                    act.wait_ge(up_sum, k + (2 * FT + 1))
                    act.wait_ge(f_done, k + 1)
                    nc.scalar.activation(relu[:, t % 2, :], up_ps[t % 2][:, :], ACT.Relu).then_inc(relu_done, 1)
                for t in range(FT):
                    k = n * FT + t
                    act.wait_ge(f_done, k + 3)
                    if t == 0:
                        act.wait_ge(dn_sum, (n + 1) * SUMS)
                    nc.scalar.copy(f_hi[:, b, t, :], f[:, t % 2, :]).then_inc(f_hi_done, 1)

            act.sem_inc(up_sum, 2 * FT)
            act.sem_inc(dn_sum, 2 * SUMS)

            def square(g):
                act.wait_ge(y_in[g % 2], 16 * (g // 2 + 1))
                if g >= 1:
                    act.wait_ge(mean_done, g * TT)
                for t in range(TT):
                    nc.scalar.activation(squares[:, t, :], y[:, g % 2, t, :], ACT.Square,
                                         accum_out=sum_sq[:, t:t + 1]).then_inc(squared, 1)

            def high(g, t):
                act.wait_ge(transposed, g * TT + t + 1)
                for q in range(GB):
                    copy = nc.scalar.copy(h_hi[:, 4 * q:4 * q + 4, t * P:(t + 1) * P],
                                          tp[q][:, :].rearrange("p (k c) -> p k c", c=P))
                copy.then_inc(hi_done, 1)

            square(0)
            split_up(0, 0)
            for t in range(TT):
                high(0, t)
            split_down(0, 0)
            for g in range(GROUPS):
                with act.Fori(0, NB - 2, 2) as c:
                    for b in range(2):
                        n = c + (g * NB + b)
                        split_up(n + 1, 1 - b)
                        relu_and_hi(n, b)
                        split_down(n + 1, 1 - b)
                n = (g + 1) * NB - 2
                if g + 1 < GROUPS:
                    square(g + 1)
                split_up(n + 1, 1)
                relu_and_hi(n, 0)
                split_down(n + 1, 1)
                relu_and_hi(n + 1, 1)
                if g + 1 < GROUPS:
                    split_up(n + 2, 0)
                    high(g + 1, 0)
                    high(g + 1, 1)
                    split_down(n + 2, 0)
                    high(g + 1, 2)
                    high(g + 1, 3)

        @block.vector
        def _(dve):
            def square_and_lo(n, b):
                for t in range(FT):
                    k = n * FT + t
                    dve.wait_ge(relu_done, k + 3)
                    dve.wait_ge(f_lo_done, k + 1)
                    nc.vector.tensor_tensor(f[:, t % 2, :], relu[:, t % 2, :], relu[:, t % 2, :],
                                            ALU.mult).then_inc(f_done, 1)
                for t in range(FT):
                    dve.wait_ge(f_hi_done, n * FT + (t + 1))
                    nc.vector.tensor_tensor(f_lo[:, b, t, :], f[:, t % 2, :], f_hi[:, b, t, :].bitcast(F32),
                                            ALU.subtract).then_inc(f_lo_done, 1)

            def add(n, yb, sums=range(SUMS)):
                for i in sums:
                    tt, c = divmod(i, CB)
                    cols = slice(c * BANK, (c + 1) * BANK)
                    dve.wait_ge(dn_sum, n * SUMS + (2 * SUMS + i + 1))
                    dve.wait_ge(added, n * SUMS + (i + 1))
                    nc.vector.tensor_tensor(y[:, yb, tt, cols], acc[i % AR][:, :], y[:, yb, tt, cols],
                                            ALU.add).then_inc(added, 1)

            dve.sem_inc(f_done, 2)
            dve.sem_inc(relu_done, 2)
            dve.sem_inc(f_lo_done, 2)
            dve.sem_inc(added, AR)
            dve.wait_ge(const_in, 32)

            def norm(g):
                if g >= 1:
                    dve.wait_ge(transposed, g * TT)
                for t in range(TT):
                    dve.wait_ge(rstd_done, g * TT + t + 1)
                    nc.vector.scalar_tensor_tensor(
                        out=xn[:, t, :], in0=y[:, g % 2, t, :], scalar=rstd[:, t:t + 1],
                        in1=gain[:, :], op0=ALU.mult, op1=ALU.mult).then_inc(normed, 1)

            def low(g, t):
                dve.wait_ge(hi_done, g * TT + t + 1)
                for q in range(GB):
                    part = h_hi[:, 4 * q:4 * q + 4, t * P:(t + 1) * P]
                    sub = nc.vector.tensor_tensor(h_lo[:, 4 * q:4 * q + 4, t * P:(t + 1) * P],
                                                  tp[q][:, :].rearrange("p (k c) -> p k c", c=P),
                                                  part.bitcast(F32), ALU.subtract)
                sub.then_inc(lo_done, 1)

            norm(0)
            for t in range(TT):
                low(0, t)
            for g in range(GROUPS):
                square_and_lo(g * NB, 0)
                with dve.Fori(0, NB - 2, 2) as c:
                    for b in range(2):
                        n = c + (g * NB + b)
                        square_and_lo(n + 1, 1 - b)
                        add(n, g % 2)
                n = (g + 1) * NB - 2
                if g + 1 < GROUPS:
                    norm(g + 1)
                square_and_lo(n + 1, 1)
                for t in range(TT):
                    if g + 1 < GROUPS:
                        low(g + 1, t)
                    half = t % 2
                    add(n + t // 2, g % 2, range(half * SUMS // 2, (half + 1) * SUMS // 2))

        @block.tensor
        def _(pe):
            def up(n, b):
                pe.wait_ge(up_lo_done, n + 2)
                for t in range(FT):
                    pe.wait_ge(relu_done, n * FT + (t + 1))
                    cols = slice(t * P, (t + 1) * P)
                    for k in range(KT):
                        for w, h in ((up_hi, h_hi), (up_lo, h_hi), (up_hi, h_lo)):
                            mm = nc.tensor.matmul(up_ps[t % 2][:, :], w[:, b, k, cols], h[:, k, :],
                                                  start=k == 0 and w is up_hi and h is h_hi,
                                                  stop=k == KT - 1 and h is h_lo)
                    mm.then_inc(up_sum, 1)

            def transpose(g, t):
                pe.wait_ge(normed, g * TT + t + 1)
                if g * TT + t >= 1:
                    pe.wait_ge(lo_done, g * TT + t)
                for k in range(KT):
                    mm = nc.tensor.transpose(tp[k // 4][:, k % 4 * P:k % 4 * P + P],
                                             xn[:, t, k * P:(k + 1) * P], ident[:, :])
                mm.then_inc(transposed, 1)

            def down(n, b, sums=range(SUMS)):
                pe.wait_ge(dn_lo_done, n + 2)
                pe.wait_ge(f_lo_done, n * FT + (FT + 2))
                for i in sums:
                    tt, c = divmod(i, CB)
                    pe.wait_ge(added, n * SUMS + (i + 1))
                    for k in range(FT):
                        for a, w in ((f_hi, dn_hi), (f_lo, dn_hi), (f_hi, dn_lo)):
                            mm = nc.tensor.matmul(acc[i % AR][:, :], a[:, b, k, tt * P:(tt + 1) * P],
                                                  w[:, b, k, c * BANK:(c + 1) * BANK],
                                                  start=k == 0 and a is f_hi and w is dn_hi,
                                                  stop=k == FT - 1 and w is dn_lo)
                    mm.then_inc(dn_sum, 1)

            pe.wait_ge(const_in, 32)
            for t in range(TT):
                transpose(0, t)
            for g in range(GROUPS):
                pe.wait_ge(lo_done, (g + 1) * TT)
                up(g * NB, 0)
                with pe.Fori(0, NB - 2, 2) as c:
                    for b in range(2):
                        n = c + (g * NB + b)
                        up(n + 1, 1 - b)
                        down(n, b)
                n = (g + 1) * NB - 2
                up(n + 1, 1)
                for t in range(TT):
                    if g + 1 < GROUPS:
                        transpose(g + 1, t)
                    half = t % 2
                    down(n + t // 2, t // 2, range(half * SUMS // 2, (half + 1) * SUMS // 2))


def shape_tables(S, D):
    f = np.float32
    inv_freq = (f(1) / (f(10000) ** np.linspace(0, 1, HEAD // 2, dtype=f))).astype(f)
    angle = (np.arange(S, dtype=f)[:, None] * inv_freq[None, :]).astype(f)
    cos, sin = np.cos(angle), np.sin(angle)
    rotation = np.stack([np.repeat(cos, 2, axis=1), np.stack([-sin, sin], axis=-1).reshape(S, HEAD)], axis=1)
    log_gamma = np.log(f(1) - f(2) ** (f(-5) - np.arange(RET_HEADS, dtype=f))).astype(f)
    idx = np.arange(P, dtype=f)
    rel = idx[None, :] - idx[:, None]
    scale = f(HEAD ** -0.5)
    decay = np.where(rel[:, None, :] >= 0, np.exp(log_gamma[None, :, None] * np.maximum(rel, 0)[:, None, :]), 0) * scale
    row_decay = np.stack([np.exp(log_gamma[None, :] * (idx[:, None] + 1)),
                          np.exp(log_gamma[None, :] * (P - 1 - idx[:, None])) * scale,
                          np.broadcast_to(np.exp(log_gamma * P)[None, :], (P, RET_HEADS))], axis=1)
    windows = (S - CMP_LEN) // STRIDE + 1
    blocks = S // SLC_LEN
    cs = np.arange(windows)[:, None] * STRIDE
    ss = np.arange(blocks)[None, :] * SLC_LEN
    overlap = np.zeros((P, blocks), f)
    overlap[:windows] = np.clip(np.minimum(cs + CMP_LEN, ss + SLC_LEN) - np.maximum(cs, ss), 0, None) / CMP_LEN
    t_blk = (np.arange(S) // SLC_LEN)[:, None]
    j = np.arange(blocks)[None, :]
    forced = (j == 0) | (j == t_blk) | (j == t_blk - 1)
    eligible = (j <= t_blk).astype(f)
    selection = np.stack([1e4 * forced, eligible, eligible - 1], axis=1)
    block_rows = (np.arange(S)[None, :] // SLC_LEN == np.arange(blocks)[:, None])
    tables = {"identity": np.eye(P), "rotation": rotation, "decay": decay, "row_decay": row_decay,
              "overlap": overlap, "selection": selection, "block_rows": block_rows}
    return {name: np.ascontiguousarray(t, dtype=f) for name, t in tables.items()}


def build_layer(nc, a, out):
    _, S, D = a["x"].shape
    N = a["w_in"].shape[2]
    x = a["x"][0]
    z = nc.dram_tensor("z_scratch", (S, N), F32, kind="Internal").ap()
    mixed = nc.dram_tensor("mixed_scratch", (S, a["w_out"].shape[1]), F32, kind="Internal").ap()
    x2 = nc.dram_tensor("x2_scratch", (S, D), F32, kind="Internal").ap()
    ident = a["identity"]
    projection_phase(nc, x, a["norm_mix"][0], a["w_in"][0], ident, z)
    with ExitStack() as stack:
        m = Space(nc, stack, "keys")
        cmp_a = m.sb("cmp_a", [P, GROUPS, P], F32R)
        cmp_b = m.sb("cmp_b", [P, GROUPS, P], F32R)
        cmp_v = m.sb("cmp_v", [P, GROUPS, HEAD + S // SLC_LEN])
        compress_phase(nc, z, [(a["cmp_pe_k"][0], a["cmp_w1_k"][0], a["cmp_w2_k"][0]),
                               (a["cmp_pe_v"][0], a["cmp_w1_v"][0], a["cmp_w2_v"][0])],
                       a["nsa_k_norm"][0], ident, a["overlap"], cmp_a, cmp_b, cmp_v)
        mixers_phase(nc, z, a["conv_w"][0], a["nsa_q_norm"][0], a["nsa_k_norm"][0], a, cmp_a, cmp_b, cmp_v, mixed)
    output_phase(nc, mixed, x, a["w_out"][0], ident, x2)
    mlp_phase(nc, x2, a["norm_mlp"][0], a["w_up"][0], a["w_down"][0], ident, out[0])


def kernel(**inputs):
    import concourse.bacc as bacc
    from concourse.bass_utils import run_bass_kernel_spmd

    nc = bacc.Bacc("TRN2", target_bir_lowering=False, num_devices=1)
    assert inputs["x"].shape[0] == 1 and inputs["w_in"].shape[0] == 1
    arrays = {name: np.ascontiguousarray(value) for name, value in inputs.items()}
    arrays.update(shape_tables(*arrays["x"].shape[1:]))
    aps = {name: nc.dram_tensor(f"in_{name}", a.shape, mybir.dt.from_np(a.dtype), kind="ExternalInput").ap()
           for name, a in arrays.items()}
    out = nc.dram_tensor("result", arrays["x"].shape, F32, kind="ExternalOutput").ap()
    build_layer(nc, aps, out)
    r = run_bass_kernel_spmd(nc, [{f"in_{name}": a for name, a in arrays.items()}], core_ids=[0])
    return r.results[0]["result"]
```

```python
from contextlib import ExitStack

import numpy as np

import concourse.bass as bass
from concourse import mybir

ALU = mybir.AluOpType
ACT = mybir.ActivationFunctionType
F32 = mybir.dt.float32
F32R = mybir.dt.float32r
BF16 = mybir.dt.bfloat16
AX_X = mybir.AxisListType.X

P = 128
BANK = 512
EPS = 1e-6


class Space:

    def __init__(self, nc, stack, phase):
        self.nc, self.stack, self.phase = nc, stack, phase

    def sb(self, name, shape, dt=F32):
        return self.stack.enter_context(self.nc.sbuf_tensor(f"{self.phase}_{name}", shape, dt))

    def ps(self, name, shape, dt=F32):
        return self.stack.enter_context(self.nc.psum_tensor(f"{self.phase}_{name}", shape, dt))

    def sem(self, name):
        return self.stack.enter_context(self.nc.semaphore(f"{self.phase}_{name}"))

    def sems(self, name, n):
        return [self.sem(f"{name}{i}") for i in range(n)]


def projection_phase(nc, x, norm_mix, w_in, identity, z):
    S, D = x.shape
    N = w_in.shape[1]
    KT = D // P
    HALVES = 2
    TT = S // P // HALVES
    NB = 9
    BW = N // NB
    RING = 3
    GB = D // BANK
    ZR = 4
    XR = 4
    assert HALVES == 2 and NB // RING == 3
    assert BW * NB == N and BW % 2 == 0 and NB % RING == 0 and TT % ZR == 0

    with ExitStack() as stack:
        m = Space(nc, stack, "proj")
        ident = m.sb("ident", [P, P])
        gain = m.sb("gain", [P, D])
        neg_half = m.sb("neg_half", [P, 1])
        xt = m.sb("x_tile", [P, XR, D])
        xn = m.sb("x_normed", [P, 2, D])
        squares = m.sb("squares", [P, 2, D], BF16)
        sum_sq = m.sb("sum_sq", [P, 2])
        mean_sq = m.sb("mean_sq", [P, 2])
        rstd = m.sb("rstd", [P, 2])
        h_hi = m.sb("hT_hi", [P, KT, TT * P], F32R)
        h_lo = m.sb("hT_lo", [P, KT, TT * P], F32R)
        w_raw = m.sb("w_raw", [P, RING, KT, BW])
        w_hi = m.sb("w_hi", [P, RING, KT, BW], F32R)
        w_lo = m.sb("w_lo", [P, RING, KT, BW], F32R)
        z_out = m.sb("z_out", [P, ZR, BW])
        tp = [m.ps(f"transposed{i}", [P, BANK]) for i in range(2 * GB)]
        acc = [m.ps(f"acc{i}", [P, BANK]) for i in range(ZR)]

        const_in = m.sem("const_in")
        const_set = m.sem("const_set")
        x_in = m.sems("x_in", XR)
        squared = m.sem("squared")
        mean_done = m.sem("mean_done")
        rstd_done = m.sem("rstd_done")
        normed = m.sem("normed")
        transposed = m.sem("transposed")
        hi_done = m.sem("hi_done")
        lo_done = m.sem("lo_done")
        w_loaded = m.sems("w_loaded", RING)
        w_hi_done = m.sem("w_hi_done")
        w_lo_done = m.sem("w_lo_done")
        product = m.sem("product")
        copied = m.sem("copied")
        z_free = m.sems("z_free", ZR)

        w_view = w_in.rearrange("(k p) n -> p k n", p=P)
        block = stack.enter_context(nc.Block())

        def split_after(t):
            return {1: (1, None), 3: (None, NB + 1), 4: (2, None)}.get(t, (None, None))

        @block.sync
        def _(sp):
            AHEAD = RING - 1

            def load_w(n, u, col):
                if not isinstance(n, int) or n >= RING:
                    sp.wait_ge(w_lo_done, n - RING + 1)
                sp.dma_start(w_raw[:, u, :, :], w_view[:, :, bass.ds(col, BW)]).then_inc(w_loaded[u], 16)

            def store_z(n, half, col):
                for t in range(TT):
                    s = t % ZR
                    sp.wait_ge(copied, n * TT + (t + 1 + ZR))
                    sp.dma_start(z[(half * TT + t) * P:(half * TT + t + 1) * P, bass.ds(col, BW)],
                                 z_out[:, s, :]).then_inc(z_free[s], 16)

            sp.dma_start(ident[:, :], identity).then_inc(const_in, 16)
            sp.dma_start(gain[:, :], norm_mix.partition_broadcast(P)).then_inc(const_in, 16)
            for n in range(AHEAD):
                load_w(n, n, n * BW)
            for half in range(HALVES):
                first = half * NB
                load_w(first + AHEAD, AHEAD, AHEAD * BW)
                store_z(first, half, 0)
                with sp.Fori(0, (NB - RING) // RING) as r:
                    for u in range(1, 1 + RING):
                        load_w(r * RING + (first + u + AHEAD), (u + AHEAD) % RING, r * (RING * BW) + (u + AHEAD) * BW)
                        store_z(r * RING + (first + u), half, r * (RING * BW) + u * BW)
                for c in range(NB - AHEAD, NB):
                    if half + 1 < HALVES:
                        load_w(first + c + AHEAD, (c + AHEAD) % RING, (c + AHEAD - NB) * BW)
                    store_z(first + c, half, c * BW)
            for s in range(ZR):
                sp.wait_ge(z_free[s], 16 + 16 * HALVES * NB * TT // ZR)

        @block.scalar
        def _(act):
            def split_hi(n, u, j):
                act.wait_ge(w_loaded[u], j * 16 + 16)
                act.wait_ge(product, (n + 1) * TT)
                nc.scalar.copy(w_hi[:, u, :, :], w_raw[:, u, :, :]).then_inc(w_hi_done, 1)

            def load_x(n):
                if n < HALVES * TT:
                    if n >= XR:
                        act.wait_ge(normed, n - XR + 1)
                    act.dma_start(xt[:, n % XR, :], x[n * P:(n + 1) * P, :]).then_inc(x_in[n % XR], 16)

            def square(n):
                act.wait_ge(x_in[n % XR], 16 * (n // XR + 1))
                if n >= 2:
                    act.wait_ge(mean_done, n - 1)
                nc.scalar.activation(squares[:, n % 2, :], xt[:, n % XR, :], ACT.Square,
                                     accum_out=sum_sq[:, n % 2:n % 2 + 1]).then_inc(squared, 1)

            def high(n):
                act.wait_ge(transposed, n + 1)
                c = n % TT * P
                for g in range(GB):
                    copy = nc.scalar.copy(h_hi[:, 4 * g:4 * g + 4, c:c + P],
                                          tp[n % 2 * GB + g][:, :].rearrange("p (k c) -> p k c", c=P))
                copy.then_inc(hi_done, 1)

            act.sem_inc(product, RING * TT)
            for n in range(XR):
                load_x(n)
            for half in range(HALVES):
                first = half * TT
                square(first)
                square(first + 1)
                split_hi(half * NB, 0, half * NB // RING)
                for t in range(TT):
                    high(first + t)
                    load_x(first + t + XR)
                    if t + 2 < TT:
                        square(first + t + 2)
                    n = split_after(t)[half]
                    if n is not None:
                        split_hi(n, n % RING, n // RING)
                if half == 1:
                    split_hi(NB + 2, 2, NB // RING)
                with act.Fori(0, NB // RING - 1) as r:
                    for u in range(RING):
                        split_hi(r * RING + (half * NB + RING + u), u, r + (half * NB // RING + 1))

        @block.gpsimd
        def _(pool):
            def split_lo(n, u):
                pool.wait_ge(w_hi_done, n + 1)
                nc.gpsimd.tensor_tensor(w_lo[:, u, :, :], w_raw[:, u, :, :], w_hi[:, u, :, :].bitcast(F32),
                                        ALU.subtract).then_inc(w_lo_done, 1)

            nc.gpsimd.memset(neg_half[:, :], -0.5).then_inc(const_set, 1)
            pool.wait_ge(const_set, 1)

            def root(n):
                b = n % 2
                pool.wait_ge(squared, n + 1)
                if n >= 2:
                    pool.wait_ge(normed, n - 1)
                nc.gpsimd.tensor_scalar(mean_sq[:, b:b + 1], sum_sq[:, b:b + 1], 1.0 / D, EPS,
                                        ALU.mult, ALU.add).then_inc(mean_done, 1)
                pool.wait_ge(mean_done, n + 1)
                nc.gpsimd.tensor_tensor(rstd[:, b:b + 1], mean_sq[:, b:b + 1], neg_half[:, :],
                                        ALU.pow).then_inc(rstd_done, 1)

            for half in range(HALVES):
                first = half * TT
                root(first)
                root(first + 1)
                split_lo(half * NB, 0)
                for t in range(TT):
                    if t + 2 < TT:
                        root(first + t + 2)
                    n = split_after(t)[half]
                    if n is not None:
                        split_lo(n, n % RING)
                if half == 1:
                    split_lo(NB + 2, 2)
                with pool.Fori(0, NB // RING - 1) as r:
                    for u in range(RING):
                        split_lo(r * RING + (half * NB + RING + u), u)

        @block.vector
        def _(dve):
            def evacuate(n, t):
                s = t % ZR
                dve.wait_ge(product, (n + RING) * TT + (t + 1))
                dve.wait_ge(z_free[s], n * (16 * TT // ZR) + 16 * (t // ZR + 1))
                nc.vector.tensor_copy(z_out[:, s, :], acc[s][:, 0:BW]).then_inc(copied, 1)

            def norm(n):
                b = n % 2
                dve.wait_ge(rstd_done, n + 1)
                if n >= 2:
                    dve.wait_ge(transposed, n - 1)
                nc.vector.scalar_tensor_tensor(
                    out=xn[:, b, :], in0=xt[:, n % XR, :], scalar=rstd[:, b:b + 1], in1=gain[:, :],
                    op0=ALU.mult, op1=ALU.mult).then_inc(normed, 1)

            def low(n):
                dve.wait_ge(hi_done, n + 1)
                c = n % TT * P
                for g in range(GB):
                    sub = nc.vector.tensor_tensor(
                        h_lo[:, 4 * g:4 * g + 4, c:c + P],
                        tp[n % 2 * GB + g][:, :].rearrange("p (k c) -> p k c", c=P),
                        h_hi[:, 4 * g:4 * g + 4, c:c + P].bitcast(F32), ALU.subtract)
                sub.then_inc(lo_done, 1)

            dve.sem_inc(copied, ZR)
            for s in range(ZR):
                dve.sem_inc(z_free[s], 16)
            dve.wait_ge(const_in, 32)
            norm(0)
            norm(1)
            for t in range(TT):
                low(t)
                if t + 2 < TT:
                    norm(t + 2)
                if t >= 1:
                    evacuate(0, t - 1)
            evacuate(0, TT - 1)
            with dve.Fori(0, NB - 2) as r:
                for t in range(TT):
                    evacuate(r + 1, t)
            norm(TT)
            norm(TT + 1)
            for t in range(TT):
                evacuate(NB - 1, t)
                if t >= 1:
                    low(TT + t - 1)
                    if t + 1 < TT:
                        norm(TT + t + 1)
            low(2 * TT - 1)
            with dve.Fori(0, NB) as r:
                for t in range(TT):
                    evacuate(r + NB, t)

        @block.tensor
        def _(pe):
            def multiply(n, u, t):
                if t == 0:
                    pe.wait_ge(w_lo_done, n + 1)
                s = t % ZR
                pe.wait_ge(copied, n * TT + (t + 1))
                rows = slice(t * P, (t + 1) * P)
                for k in range(KT):
                    for a, w in ((h_hi, w_hi), (h_lo, w_hi), (h_hi, w_lo)):
                        mm = nc.tensor.matmul(acc[s][:, 0:BW], a[:, k, rows], w[:, u, k, :],
                                              start=k == 0 and a is h_hi and w is w_hi,
                                              stop=k == KT - 1 and w is w_lo)
                mm.then_inc(product, 1)

            def transpose(n):
                pe.wait_ge(normed, n + 1)
                if n >= 2:
                    pe.wait_ge(lo_done, n - 1)
                for k in range(KT):
                    mm = nc.tensor.transpose(tp[n % 2 * GB + k // 4][:, k % 4 * P:k % 4 * P + P],
                                             xn[:, n % 2, k * P:(k + 1) * P], ident[:, :])
                mm.then_inc(transposed, 1)

            pe.wait_ge(const_in, 32)
            transpose(0)
            transpose(1)
            for half in range(HALVES):
                first = half * NB
                for t in range(TT):
                    pe.wait_ge(lo_done, half * TT + t + 1)
                    multiply(first, 0, t)
                    if half == 0 and t + 2 < TT:
                        transpose(t + 2)
                with pe.Fori(0, NB // RING - 1) as r:
                    for u in range(1, 1 + RING):
                        for t in range(TT):
                            multiply(r * RING + (first + u), u % RING, t)
                for t in range(TT):
                    multiply(first + NB - 2, (NB - 2) % RING, t)
                for t in range(TT):
                    multiply(first + NB - 1, (NB - 1) % RING, t)
                    if half == 0 and t >= 1:
                        transpose(TT + t - 1)
                if half == 0:
                    transpose(2 * TT - 1)

def chain(eng, done):
    count = [0]

    def link(instruction):
        count[0] += 1
        instruction.then_inc(done, 1)
        eng.wait_ge(done, count[0])

    return link


MASKED = -1e30
HEAD = 64
RET_HEADS = 4
GROUPS = 2
HPG = 4
NSA_HEADS = GROUPS * HPG
STRIDE, CMP_LEN, SLC_LEN, TOPK = 16, 32, 64, 8

RQ, RK, RV, RG = 0, 256, 512, 768
CB_, CC, CH = 1024, 1280, 1536
NQ = 1792
NKC, NVC, NKS, NVS, NKW, NVW = 2304, 2432, 2560, 2688, 2816, 2944
NG = 3072


WIN_TILES = 256 // P + 1
WR = WIN_TILES + 1
QR = 3
MAX_ROW = 96
BLOCK_ROWS = 64


class Constants:

    def __init__(self, m, S, conv_width):
        self.ident = m.sb("ident", [P, P])
        self.ident_bf = m.sb("ident_bf", [P, P], BF16)
        self.ones = m.sb("ones", [P, P], F32R)
        self.cmp_mask = m.sb("cmp_mask", [P, S], BF16)
        self.causal = m.sb("causal", [P, P], BF16)
        self.beyond = m.sb("beyond", [P, P], BF16)
        self.decay = m.sb("decay", [P, RET_HEADS, P])
        self.row_decay = m.sb("row_decay", [P, 3, RET_HEADS])
        self.conv_taps = m.sb("conv_taps", [P, 3, conv_width])
        self.q_gains = m.sb("q_gains", [P, HEAD])
        self.k_gains = m.sb("k_gains", [P, HEAD])
        self.kz = m.sb("kz", [P, RET_HEADS, P])
        self.zk = m.sb("zk", [P, RET_HEADS, P])
        self.qa_w = m.sb("qa_w", [P, QR, NSA_HEADS, P], F32R)
        self.qa_s = m.sb("qa_s", [P, QR, NSA_HEADS, P], F32R)
        self.ka_s = m.sb("ka_s", [P, GROUPS, S], F32R)
        self.ka_w = m.sb("ka_w", [P, GROUPS, WR * P], F32R)
        self.v_s = m.sb("v_s", [P, S // P, GROUPS, HEAD + 1])
        self.v_w = m.sb("v_w", [P, WR, GROUPS, HEAD + 1])


def compress_phase(nc, z, weights, conv_w, q_gain, k_gain, tables, consts, keys_a, keys_b, values):
    S = z.shape[0]
    NT = S // P
    NBLK = S // SLC_LEN
    NW = (S - CMP_LEN) // STRIDE + 1
    KINDS = 2

    with ExitStack() as stack:
        m = Space(nc, stack, "cmp")
        ident = consts.ident
        block_rows = m.sb("block_rows", [P, S])
        kv = m.sb("kv", [P, NT, KINDS * P])
        kvT = m.sb("kvT", [P, KINDS, S])
        w1 = m.sb("w1", [P, KINDS, CMP_LEN, P])
        w2 = m.sb("w2", [P, KINDS, P])
        pe_rows = m.sb("pe_rows", [P, KINDS, GROUPS, HEAD])
        peT = m.sb("peT", [P, KINDS, CMP_LEN])
        bias = m.sb("bias", [P, KINDS])
        gain = consts.k_gains
        pre = m.sb("pre", [P, KINDS, P])
        den = m.sb("den", [P, KINDS, P])
        act_out = m.sb("silu", [P, KINDS, P])
        kc = m.sb("kc", [P, GROUPS, HEAD])
        sq = m.sb("sq", [P, GROUPS, HEAD])
        ssq = m.sb("ssq", [P, GROUPS])
        mean = m.sb("mean", [P, GROUPS])
        rstd = m.sb("rstd", [P, GROUPS])
        neg_half = m.sb("neg_half", [P, GROUPS])
        pack = m.sb("pack", [P, GROUPS, P])
        banks = [m.ps(f"bank{i}", [P, BANK]) for i in range(7)]
        bias_ps = m.ps("bias_ps", [P, BANK])

        ident_in = m.sem("ident_in")
        kv_in = m.sem("kv_in")
        loaded = m.sem("loaded")
        overlap_in = m.sem("overlap_in")
        consts_in = m.sem("consts_in")
        cleared = m.sem("cleared")
        values_cleared = m.sem("values_cleared")
        transposed = m.sem("transposed")
        copied = m.sem("copied")
        pe_T = m.sem("pe_T")
        pe_copied = m.sem("pe_copied")
        bias_sum = m.sem("bias_sum")
        bias_set = m.sem("bias_set")
        first = m.sem("first_product")
        biased = m.sem("biased")
        exp_done = m.sem("exp_done")
        silu_done = m.sem("silu_done")
        second = m.sem("second_product")
        squares = m.sem("squares")
        powered = m.sem("powered")
        packed = m.sem("packed")
        packT = m.sem("packT")
        out_a = m.sem("keys_a_set")
        dve_done = m.sem("dve_done")
        pool_done = m.sem("pool_done")
        block = stack.enter_context(nc.Block())
        TOTAL = 16 * KINDS * 3 * GROUPS
        CONSTS = 8

        @block.sync
        def _(sp):
            sp.dma_start(ident[:, :], tables["identity"]).then_inc(ident_in, 16)
            sp.dma_start(kv[:, :, :], z[:, NKC:NKC + KINDS * P].rearrange("(t p) c -> p t c", p=P)).then_inc(kv_in, 16)
            sp.wait_ge(cleared, 1)
            for j, (pe_, w1_, w2_) in enumerate(weights):
                for g in range(GROUPS):
                    rows = slice(g * HEAD, (g + 1) * HEAD)
                    sp.dma_start(w1[rows, j, :, rows], w1_.rearrange("(l d) e -> d l e", d=HEAD)).then_inc(loaded, 16)
                    sp.dma_start(w2[rows, j, rows], w2_).then_inc(loaded, 16)
                    sp.dma_start(pe_rows[0:CMP_LEN, j, g, :], pe_).then_inc(loaded, 16)
            sp.dma_start(block_rows[BLOCK_ROWS:BLOCK_ROWS + NBLK, :], tables["block_rows"]).then_inc(consts_in, 16)
            sp.dma_start(consts.decay[:, :, :], tables["decay"]).then_inc(consts_in, 16)
            sp.dma_start(consts.row_decay[:, :, :], tables["row_decay"]).then_inc(consts_in, 16)
            for k in range(3):
                sp.dma_start(consts.conv_taps[:, k, :], conv_w[k].partition_broadcast(P)).then_inc(consts_in, 16)
            sp.dma_start(consts.q_gains[:, :], q_gain.partition_broadcast(P)).then_inc(consts_in, 16)
            sp.dma_start(consts.k_gains[:, :], k_gain.partition_broadcast(P)).then_inc(consts_in, 16)
            sp.wait_ge(values_cleared, 1)
            for g in range(GROUPS):
                sp.dma_start(values[:, g, HEAD:], tables["overlap"]).then_inc(overlap_in, 16)
            sp.wait_ge(overlap_in, 16 * GROUPS)
            sp.wait_ge(consts_in, 16 * CONSTS)

        @block.gpsimd
        def _(pool):
            link = chain(pool, pool_done)

            def mask(tensor, pattern, base, channel):
                link(nc.gpsimd.memset(tensor[:, :], 0.0))
                link(nc.gpsimd.affine_select(out=tensor[:, :], in_=tensor[:, :], compare_op=ALU.is_ge,
                                             fill=MASKED, base=base, pattern=pattern,
                                             channel_multiplier=channel))

            link(nc.gpsimd.memset(values[:, :, :], 0.0))
            link(nc.gpsimd.memset(pack[:, :, :], 0.0))
            nc.gpsimd.memset(neg_half[:, :], -0.5).then_inc(values_cleared, 1)
            pool.wait_ge(values_cleared, 1)
            link(nc.gpsimd.memset(consts.kz[:, :, :], 0.0))
            link(nc.gpsimd.memset(consts.zk[:, :, :], 0.0))
            link(nc.gpsimd.memset(consts.ones[:, :].bitcast(F32), 1.0))
            link(nc.gpsimd.memset(consts.v_s[:, :, :, HEAD:], 1.0))
            link(nc.gpsimd.memset(consts.v_w[:, :, :, HEAD:], 1.0))
            for t in (consts.qa_w, consts.qa_s):
                link(nc.gpsimd.memset(t[64:, :, :, :].bitcast(F32), 0.0))
            link(nc.gpsimd.memset(consts.ka_w[64:, :, :].bitcast(F32), 0.0))
            for t in (consts.ka_w, consts.ka_s):
                link(nc.gpsimd.memset(t[MAX_ROW:MAX_ROW + 1, :, :].bitcast(F32), 1.0))
            mask(consts.cmp_mask, [[1, S]], -(CMP_LEN - 1), -STRIDE)
            mask(consts.causal, [[1, P]], 0, -1)
            mask(consts.beyond, [[-1, P]], -1, 1)
            link(nc.gpsimd.memset(consts.ident_bf[:, :], 0.0))
            link(nc.gpsimd.affine_select(out=consts.ident_bf[:, :], in_=consts.ident_bf[:, :],
                                         compare_op=ALU.not_equal, fill=1.0, base=0, pattern=[[-1, P]],
                                         channel_multiplier=1))
            pool.wait_ge(squares, 1)
            link(nc.gpsimd.tensor_scalar(mean[:, :], ssq[:, :], 1.0 / HEAD, EPS, ALU.mult, ALU.add))
            nc.gpsimd.tensor_tensor(rstd[:, :], mean[:, :], neg_half[:, :], ALU.pow).then_inc(powered, 1)

        @block.tensor
        def _(pe):
            pe.wait_ge(ident_in, 16)
            pe.wait_ge(kv_in, 16)
            for q in range(KINDS * NT // 4):
                j, t0 = divmod(4 * q, NT)
                if q == len(banks):
                    pe.wait_ge(copied, 1)
                for t in range(4):
                    mm = nc.tensor.transpose(banks[q % len(banks)][:, t * P:(t + 1) * P],
                                             kv[:, t0 + t, j * P:(j + 1) * P], ident[:, :])
                mm.then_inc(transposed, 1)
            pe.wait_ge(loaded, TOTAL)
            for j in range(KINDS):
                mm = nc.tensor.transpose(bias_ps[:, j * P:(j + 1) * P], pe_rows[:, j, :, :].rearrange("p g d -> p (g d)"),
                                         ident[:, :])
            mm.then_inc(pe_T, 1)
            pe.wait_ge(copied, KINDS * NT // 4)
            for j in range(KINDS):
                for l in range(CMP_LEN):
                    mm = nc.tensor.matmul(banks[1 + j][:, 0:NW], w1[:, j, l, :],
                                          kvT[:, j, l:l + (NW - 1) * STRIDE + 1:STRIDE],
                                          start=l == 0, stop=l == CMP_LEN - 1)
                mm.then_inc(first, 1)
                if j == 0:
                    pe.wait_ge(pe_copied, 1)
                    for kind in range(KINDS):
                        for l in range(CMP_LEN):
                            mm = nc.tensor.matmul(bias_ps[:, 2 * P + kind:2 * P + kind + 1], w1[:, kind, l, :],
                                                  peT[:, kind, l:l + 1], start=l == 0, stop=l == CMP_LEN - 1)
                    mm.then_inc(bias_sum, 1)
            pe.wait_ge(silu_done, 1)
            for j in range(KINDS):
                mm = nc.tensor.matmul(banks[5][0:NW, j * P:(j + 1) * P], act_out[:, j, 0:NW], w2[:, j, :],
                                      start=True, stop=True)
            mm.then_inc(second, 1)
            pe.wait_ge(packed, 1)
            for g in range(GROUPS):
                mm = nc.tensor.transpose(banks[6][:, g * P:(g + 1) * P], pack[:, g, :], ident[:, :])
            mm.then_inc(packT, 1)

        @block.scalar
        def _(act):
            for n in range(KINDS * NT // 4):
                act.wait_ge(transposed, n + 1)
                j, t0 = divmod(4 * n, NT)
                nc.scalar.copy(kvT[:, j, t0 * P:(t0 + 4) * P], banks[n % len(banks)][:, :]).then_inc(copied, 1)
            act.wait_ge(consts_in, 16 * CONSTS)
            for g in range(GROUPS):
                nc.scalar.copy(consts.ka_s[BLOCK_ROWS:BLOCK_ROWS + NBLK, g, :],
                               block_rows[BLOCK_ROWS:BLOCK_ROWS + NBLK, :])
            nc.scalar.mul(consts.q_gains[:, :], consts.q_gains[:, :], HEAD ** -0.5)
            act.wait_ge(bias_set, 1)
            for j in range(KINDS):
                act.wait_ge(first, j + 1)
                nc.scalar.activation(pre[:, j, 0:NW], banks[1 + j][:, 0:NW], ACT.Identity,
                                     bias=bias[:, j:j + 1]).then_inc(biased, 1)
                act.wait_ge(biased, j + 1)
                nc.scalar.activation(den[:, j, 0:NW], pre[:, j, 0:NW], ACT.Exp, scale=-1.0).then_inc(exp_done, 1)

        @block.vector
        def _(dve):
            link = chain(dve, dve_done)
            nc.vector.memset(w1[:, :, :, :], 0.0)
            nc.vector.memset(w2[:, :, :], 0.0)
            nc.vector.memset(pe_rows[:, :, :, :], 0.0).then_inc(cleared, 1)
            dve.wait_ge(pe_T, 1)
            for j in range(KINDS):
                copy = nc.vector.tensor_copy(peT[:, j, :], bias_ps[:, j * P:j * P + CMP_LEN])
            copy.then_inc(pe_copied, 1)
            dve.wait_ge(bias_sum, 1)
            nc.vector.tensor_copy(bias[:, :], bias_ps[:, 2 * P:2 * P + KINDS]).then_inc(bias_set, 1)
            dve.wait_ge(exp_done, KINDS)
            link(nc.vector.tensor_scalar(den[:, :, 0:NW], den[:, :, 0:NW], 1.0, None, ALU.add))
            link(nc.vector.reciprocal(den[:, :, 0:NW], den[:, :, 0:NW]))
            nc.vector.tensor_tensor(act_out[:, :, 0:NW], den[:, :, 0:NW], pre[:, :, 0:NW], ALU.mult)\
                .then_inc(silu_done, 1)
            dve.wait_ge(second, 1)
            dve.wait_ge(values_cleared, 1)
            dve.wait_ge(consts_in, 16 * CONSTS)
            out = banks[5][0:NW, 0:KINDS * GROUPS * HEAD].rearrange("p (j g d) -> p j g d", j=KINDS, g=GROUPS)
            nc.vector.tensor_copy(values[0:NW, :, 0:HEAD], out[:, 1, :, :])
            link(nc.vector.tensor_copy(kc[0:NW, :, :], out[:, 0, :, :]))
            link(nc.vector.memset(ssq[:, :], 1.0))
            link(nc.vector.tensor_tensor(sq[0:NW, :, :], kc[0:NW, :, :], kc[0:NW, :, :], ALU.mult))
            nc.vector.tensor_reduce(ssq[0:NW, :], sq[0:NW, :, :], AX_X, ALU.add).then_inc(squares, 1)
            dve.wait_ge(powered, 1)
            link(nc.vector.tensor_tensor(kc[0:NW, :, :], kc[0:NW, :, :],
                                         rstd[0:NW, :].unsqueeze(2).to_broadcast([NW, GROUPS, HEAD]), ALU.mult))
            link(nc.vector.tensor_tensor(kc[0:NW, :, :], kc[0:NW, :, :],
                                         gain[0:NW, :].unsqueeze(1).to_broadcast([NW, GROUPS, HEAD]), ALU.mult))
            link(nc.vector.tensor_copy(pack[0:NW, :, HEAD:].bitcast(F32R), kc[0:NW, :, :]))
            nc.vector.tensor_tensor(pack[0:NW, :, 0:HEAD].bitcast(F32R), kc[0:NW, :, :], pack[0:NW, :, HEAD:],
                                    ALU.subtract).then_inc(packed, 1)
            dve.wait_ge(packT, 1)
            bank = banks[6][:, 0:GROUPS * P].rearrange("p (g n) -> p g n", g=GROUPS)
            nc.vector.tensor_copy(keys_b[:, :, :], bank)
            link(nc.vector.tensor_copy(keys_a[0:HEAD, :, :], bank[HEAD:P, :, :]))


CMP, SLC, WIN = 0, 1, 2
NBLKS = 32
VCOLS = {CMP: HEAD + NBLKS, WIN: HEAD + 1, SLC: HEAD + 1}

PIECES = ("squares", "fill qq", "sums", "read qq", "gates", "fill kz", "normalise k", "read kz",
          "normalise q", "high", "low", "fill scores", "read scores", "fill output", "read output", "fill k", "read k",
          "fill q0", "read q0", "fill q1", "read q1", "output sums")
FILLS = [piece[5:] for piece in PIECES if piece.startswith("fill")]
DVE_FILLS = ("scores", "output")


def merge(a, b):
    done_a = done_b = 0
    merged = []
    while done_a < len(a) or done_b < len(b):
        if done_b == len(b) or (done_a < len(a) and (2 * done_a + 1) * len(b) <= (2 * done_b + 1) * len(a)):
            merged.append(a[done_a])
            done_a += 1
        else:
            merged.append(b[done_b])
            done_b += 1
    return merged


class Plan:

    def __init__(self, tiles):
        units = tiles * GROUPS
        first = self.front(0) + self.select(0) + self.front(1) + self.selected_maxima(0)
        self.steps = self.prep(0) + merge(first, self.prep(1))
        for u in range(units):
            i, g = divmod(u, GROUPS)
            own = [("scores", u, SLC, 0)]
            for j in range(1, i + 1):
                own += [("scores", u, SLC, j), ("values", u, SLC, j - 1)]
            ahead = []
            if u + 2 < units:
                pieces = self.prep(i + 2) if i + 2 < tiles else []
                half = len(pieces) // GROUPS
                ahead = merge(self.front(u + 2), pieces[g * half:(g + 1) * half])
            self.steps += own[:1]
            if u + 1 < units:
                self.steps += self.select(u + 1)
                ahead = merge(self.selected_maxima(u + 1), ahead)
            if u >= 1:
                self.steps.append(("post", u - 1, SLC))
            self.steps += own[1:5] + merge(own[5:], ahead) + [("values", u, SLC, i)]
        self.steps.append(("post", units - 1, SLC))

        self.scores_n = {}
        self.maxima_n = {}
        self.probs_n = {}
        self.values_n = {}
        for s in self.steps:
            if s[0] == "row":
                self.scores_n[s[1], s[2], "row"] = len(self.scores_n)
            elif s[0] == "scores":
                self.scores_n[s[1:]] = len(self.scores_n)
                self.probs_n[s[1:]] = len(self.probs_n)
            elif s[0] == "maximum":
                self.maxima_n[s[1:]] = len(self.maxima_n)
            elif s[0] == "values":
                self.values_n[s[1:]] = len(self.values_n)
        self.probs_by = list(self.probs_n)

    @staticmethod
    def prep(i):
        return [("prep", i, piece) for piece in PIECES]

    @staticmethod
    def max_fills(u, branch):
        i = u // GROUPS
        if branch == SLC:
            return [(h, c) for h in range(HPG) for c in range(i // 4 + 1)]
        return [(h, 0) for h in range(HPG)]

    @staticmethod
    def key_tiles(u, branch):
        i = u // GROUPS
        return [0] if branch == CMP else range(max(0, i - WIN_TILES + 1) if branch == WIN else 0, i + 1)

    def selected_maxima(self, u):
        return [("maximum", u, SLC, fill) for fill in self.max_fills(u, SLC)] + [("row", u, SLC)]

    @staticmethod
    def select(u):
        return [("select", u), ("selected", u)]

    def front(self, u):
        steps = [("compressed", u)] + [("maximum", u, WIN, fill) for fill in self.max_fills(u, WIN)]
        steps.insert(3, ("weights", u))
        window = list(self.key_tiles(u, WIN))
        steps += [("scores", u, CMP, 0), ("row", u, WIN), ("values", u, CMP, 0), ("post", u, CMP),
                  ("scores", u, WIN, window[0])]
        for a, b in zip(window, window[1:]):
            steps += [("scores", u, WIN, b), ("values", u, WIN, a)]
        return steps + [("values", u, WIN, window[-1]), ("post", u, WIN)]


def mixers_phase(nc, z, tables, consts, cmp_a, cmp_b, cmp_v, mixed_out):
    S = z.shape[0]
    NT = S // P
    NBLK = S // SLC_LEN
    assert NBLK == NBLKS
    plan = Plan(NT)
    RW = RET_HEADS * HEAD
    CW = CC - CB_
    PR = 6
    SR = 4
    LOADS = 5

    with ExitStack() as stack:
        m = Space(nc, stack, "mix")
        ident, ident_bf, ones = consts.ident, consts.ident_bf, consts.ones
        cmp_mask, causal, beyond = consts.cmp_mask, consts.causal, consts.beyond
        decay, row_decay, conv_taps = consts.decay, consts.row_decay, consts.conv_taps
        q_gains, k_gains = consts.q_gains, consts.k_gains
        kz, zk, v_s, v_w = consts.kz, consts.zk, consts.v_s, consts.v_w
        qa_w, qa_s, ka_s, ka_w = consts.qa_w, consts.qa_s, consts.ka_s, consts.ka_w
        neg_half = m.sb("neg_half", [P, 16])
        zt = m.sb("z", [P, 2, z.shape[1]])
        shifted = m.sb("shifted", [P, 2, 2, 2 * CW])
        rot = m.sb("rot", [P, 2, 2, HEAD])
        sel_table = m.sb("sel_table", [P, SR, 3, NBLK])
        mixed = m.sb("mixed", [P, QR, 2 * RW + NSA_HEADS * HEAD])
        r1 = m.sb("r1", [P, 8, HEAD])
        r2 = m.sb("r2", [P, 8, HEAD])
        qq = m.sb("qq", [P, RET_HEADS, P])
        qqT = m.sb("qqT", [P, RET_HEADS, P])
        kzT = m.sb("kzT", [P, RET_HEADS, P])
        ret_scores = m.sb("ret_scores", [P, RET_HEADS, P])
        state = m.sb("state", [P, RET_HEADS, HEAD])
        o_ret = m.sb("o_ret", [P, RET_HEADS, HEAD])
        o_sq = m.sb("o_sq", [P, RET_HEADS, HEAD])
        o_mean = m.sb("o_mean", [P, RET_HEADS])
        o_ssq = m.sb("o_ssq", [P, RET_HEADS])
        o_rstd = m.sb("o_rstd", [P, RET_HEADS])
        swish = m.sb("swish", [P, QR, RW])
        gates = m.sb("gates", [P, QR, 3 * NSA_HEADS])
        taps = m.sb("taps", [P, 3, CW])
        sq = m.sb("sq", [P, NSA_HEADS + 2 * GROUPS, HEAD])
        ssq = m.sb("ssq", [P, NSA_HEADS + 2 * GROUPS])
        mean = m.sb("mean", [P, NSA_HEADS + 2 * GROUPS])
        rstd = m.sb("rstd", [P, NSA_HEADS + 2 * GROUPS])
        qn = m.sb("qn", [P, NSA_HEADS, HEAD])
        kn = m.sb("kn", [P, 2 * GROUPS, HEAD])
        q_pack = m.sb("q_pack", [P, NSA_HEADS, P])
        k_pack = m.sb("k_pack", [P, 2 * GROUPS, P])
        qb = m.sb("qb", [P, QR, NSA_HEADS, P], F32R)
        kb_s = m.sb("kb_s", [P, GROUPS, S], F32R)
        kb_w = m.sb("kb_w", [P, GROUPS, WR * P], F32R)
        probs = m.sb("probs", [P, PR, HPG * P])
        part_max = m.sb("part_max", [P, HPG, NT // 4])
        top = m.sb("top", [P, 3, HPG])
        neg_max = m.sb("neg_max", [P, 3, HPG])
        diag = {SLC: m.sb("diag_selected", [P, HPG, P], F32R), WIN: m.sb("diag_window", [P, HPG, P], F32R)}
        cmp_weights = m.sb("cmp_weights", [P, HPG, P])
        cmp_sum = m.sb("cmp_sum", [P, HPG])
        den = m.sb("den", [P, HPG])
        weight = m.sb("weight", [P, HPG])
        importance = m.sb("importance", [P, HPG, NBLK])
        sel_score = m.sb("sel_score", [P, NBLK])
        best = m.sb("best", [P, TOPK])
        chosen = m.sb("chosen", [P, NBLK])
        selection = m.sb("selection", [P, P])
        weighted = m.sb("weighted", [P, HPG, HEAD])

        score_ps = [m.ps(f"score{b}", [P, BANK]) for b in range(2)]
        maxima_ps = [m.ps(f"maxima{b}", [P, BANK]) for b in range(2)]
        selected_ps = [m.ps(f"selected{b}", [P, BANK]) for b in range(2)]
        front_ps = m.ps("front", [P, BANK])
        prep_ps = m.ps("prep", [P, BANK])

        cleared = m.sem("cleared")
        tile_in = m.sems("tile_in", 2)
        mixed_stored = m.sems("mixed_stored", QR)
        v_ready = m.sem("v_ready")
        rot_ready = m.sem("rot_ready")
        squared = m.sem("squared")
        exps_ready = m.sem("exps_ready")
        ssq_ready = m.sem("ssq_ready")
        gates_ready = m.sem("gates_ready")
        rstd_ready = m.sem("rstd_ready")
        normed = m.sem("normed")
        high_ready = m.sem("high_ready")
        packs_ready = m.sem("packs_ready")
        prep_sum = m.sem("prep_sum")
        prep_read_act = m.sem("prep_read_act")
        prep_read_dve = m.sem("prep_read_dve")
        o_ready = m.sem("o_ready")
        o_squared = m.sem("o_squared")
        o_ssq_ready = m.sem("o_ssq_ready")
        pool_mixed = m.sem("pool_mixed")
        compressed_sum = m.sem("compressed_sum")
        cmp_max_ready = m.sem("cmp_max_ready")
        cmp_weighted = m.sem("cmp_weighted")
        diag_ready = {SLC: m.sem("diag_selected_ready"), WIN: m.sem("diag_window_ready")}
        score_sum = m.sem("score_sum")
        score_read = m.sem("score_read")
        maxima_sum = m.sem("maxima_sum")
        maxima_read = m.sem("maxima_read")
        probs_used = m.sem("probs_used")
        front_read = m.sem("front_read")
        selected_read = m.sem("selected_read")
        sel_ready = m.sem("sel_ready")
        select_sum = m.sem("select_sum")
        rows_set = m.sem("rows_set")
        nsa_mixed = m.sem("nsa_mixed")
        dve_done = m.sem("dve_done")
        pool_done = m.sem("pool_done")

        block = stack.enter_context(nc.Block())

        def tile_loaded(eng, i):
            eng.wait_ge(tile_in[i % 2], 16 * LOADS * (i // 2 + 1))

        def fill_n(i, name):
            return len(FILLS) * i + FILLS.index(name)

        def prep_read(eng, i, name):
            mine, sem = (True, prep_read_dve) if name in DVE_FILLS else (False, prep_read_act)
            same = [f for f in FILLS if (f in DVE_FILLS) == mine]
            eng.wait_ge(sem, len(same) * i + same.index(name) + 1)

        def last_use(eng, u, branch):
            eng.wait_ge(probs_used, plan.values_n[u, branch, plan.key_tiles(u, branch)[-1]] + 1)

        @block.sync
        def _(sp):
            def load(i):
                b, rows = i % 2, slice(i * P, (i + 1) * P)
                if i >= 2:
                    sp.wait_ge(pool_mixed, i - 1)
                    sp.wait_ge(packs_ready, i - 1)
                    sp.wait_ge(gates_ready, i - 1)
                    sp.wait_ge(exps_ready, i - 1)
                    sp.wait_ge(prep_sum, fill_n(i - 2, "output") + 1)
                if i >= SR:
                    sp.wait_ge(sel_ready, GROUPS * (i - SR + 1))
                sp.dma_start(zt[:, b, :], z[rows, :]).then_inc(tile_in[b], 16)
                if i == 0:
                    sp.wait_ge(cleared, 1)
                for s in (1, 2):
                    cut = s if i == 0 else 0
                    sp.dma_start(shifted[cut:, b, s - 1, :], z[i * P - s + cut:(i + 1) * P - s, CC:CC + 2 * CW])\
                        .then_inc(tile_in[b], 16)
                sp.dma_start(rot[:, b, :, :], tables["rotation"][rows, :, :]).then_inc(tile_in[b], 16)
                sp.dma_start(sel_table[:, i % SR, :, :], tables["selection"][rows, :, :]).then_inc(tile_in[b], 16)

            for i in range(3):
                load(i)
            for i in range(NT):
                if i + 3 < NT:
                    load(i + 3)
                sp.wait_ge(pool_mixed, i + 1)
                sp.wait_ge(nsa_mixed, GROUPS * (i + 1))
                sp.dma_start(mixed_out[i * P:(i + 1) * P, :], mixed[:, i % QR, :]).then_inc(mixed_stored[i % QR], 16)
            for b in range(QR):
                sp.wait_ge(mixed_stored[b], 16 * len(range(b, NT, QR)))

        @block.gpsimd
        def _(pool):
            link = chain(pool, pool_done)

            link(nc.gpsimd.memset(shifted[0:2, 0, :, :], 0.0))
            link(nc.gpsimd.memset(neg_half[:, :], -0.5))
            link(nc.gpsimd.memset(state[:, :, :], 0.0))
            nc.gpsimd.memset(selection[:, :], 0.0).then_inc(cleared, 1)
            pool.wait_ge(cleared, 1)

            def bc(ap, n):
                return ap.unsqueeze(2).to_broadcast([P, ap.shape[1], n])

            for i in range(NT):
                b, qr = i % 2, i % QR
                tile_loaded(pool, i)
                if i >= WR:
                    last_use(pool, GROUPS * (i - WR + WIN_TILES) - 1, WIN)
                nc.gpsimd.tensor_copy(v_w[:, i % WR, :, 0:HEAD],
                                      zt[:, b, NVW:NVW + P].rearrange("p (g d) -> p g d", g=GROUPS))\
                    .then_inc(v_ready, 1)
                nc.gpsimd.tensor_copy(v_s[:, i, :, 0:HEAD],
                                      zt[:, b, NVS:NVS + P].rearrange("p (g d) -> p g d", g=GROUPS))\
                    .then_inc(v_ready, 1)
                if i >= 1:
                    pool.wait_ge(prep_sum, fill_n(i - 1, "output") + 1)
                x = zt[:, b, 0:2 * RW].rearrange("p (h d) -> p h d", d=HEAD)
                xp = x.rearrange("p h (e two) -> p h e two", two=2)
                cos = rot[:, b, 0, :].unsqueeze(1).to_broadcast([P, 8, HEAD])
                sin = rot[:, b, 1, :].rearrange("p (e two) -> p e two", two=2)
                link(nc.gpsimd.tensor_tensor(r1[:, :, :], x, cos, ALU.mult))
                r2p = r2[:, :, :].rearrange("p h (e two) -> p h e two", two=2)
                for a in range(2):
                    link(nc.gpsimd.tensor_tensor(r2p[:, :, :, a], xp[:, :, :, 1 - a],
                                                 sin[:, :, a].unsqueeze(1).to_broadcast([P, 8, HEAD // 2]),
                                                 ALU.mult))
                link(nc.gpsimd.tensor_tensor(qq[:, :, 0:HEAD], r1[:, 0:4, :], r2[:, 0:4, :], ALU.add))
                link(nc.gpsimd.tensor_tensor(kz[:, :, 0:HEAD], r1[:, 4:8, :], r2[:, 4:8, :], ALU.add))
                link(nc.gpsimd.tensor_tensor(qq[:, :, HEAD:], qq[:, :, 0:HEAD], bc(row_decay[:, 0, :], HEAD), ALU.mult))
                nc.gpsimd.tensor_tensor(zk[:, :, HEAD:], kz[:, :, 0:HEAD], bc(row_decay[:, 1, :], HEAD), ALU.mult)\
                    .then_inc(rot_ready, 1)
                pool.wait_ge(ssq_ready, i + 1)
                if i >= 1:
                    pool.wait_ge(normed, i)
                link(nc.gpsimd.tensor_scalar(mean[:, :], ssq[:, :], 1.0 / HEAD, EPS, ALU.mult, ALU.add))
                nc.gpsimd.tensor_tensor(rstd[:, :], mean[:, :], neg_half[:, 0:NSA_HEADS + 2 * GROUPS],
                                        ALU.pow).then_inc(rstd_ready, 1)
                for k in range(3):
                    src = zt[:, b, CC:CC + 2 * CW] if k == 2 else shifted[:, b, 1 - k, :]
                    link(nc.gpsimd.tensor_tensor(taps[:, k, :], src[:, 0:CW], src[:, CW:], ALU.mult))
                link(nc.gpsimd.tensor_tensor(taps[:, :, :], taps[:, :, :], conv_taps[:, :, :], ALU.mult))
                link(nc.gpsimd.tensor_tensor(taps[:, 0, :], taps[:, 0, :], taps[:, 1, :], ALU.add))
                link(nc.gpsimd.tensor_tensor(taps[:, 0, :], taps[:, 0, :], taps[:, 2, :], ALU.add))
                if i >= QR:
                    pool.wait_ge(mixed_stored[qr], 16 * (i // QR))
                link(nc.gpsimd.tensor_tensor(mixed[:, qr, RW:RW + CW], taps[:, 0, :], zt[:, b, CB_:CB_ + CW], ALU.mult))
                pool.wait_ge(o_ready, i + 1)
                nc.gpsimd.tensor_tensor(o_sq[:, :, :], o_ret[:, :, :], o_ret[:, :, :], ALU.mult).then_inc(o_squared, 1)
                pool.wait_ge(o_ssq_ready, i + 1)
                link(nc.gpsimd.tensor_scalar(o_mean[:, :], o_ssq[:, :], 1.0 / HEAD, EPS, ALU.mult, ALU.add))
                link(nc.gpsimd.tensor_tensor(o_rstd[:, :], o_mean[:, :], neg_half[:, 0:RET_HEADS], ALU.pow))
                link(nc.gpsimd.tensor_tensor(o_sq[:, :, :], o_ret[:, :, :], bc(o_rstd[:, :], HEAD), ALU.mult))
                pool.wait_ge(gates_ready, i + 1)
                nc.gpsimd.tensor_tensor(mixed[:, qr, 0:RW], o_sq[:, :, :].rearrange("p h d -> p (h d)"),
                                        swish[:, qr, :], ALU.mult).then_inc(pool_mixed, 1)

        @block.scalar
        def _(act):
            for step in plan.steps:
                kind, u = step[0], step[1]
                if kind == "prep":
                    i, piece = step[1:]
                    b, qr = i % 2, i % QR
                    if piece == "squares":
                        tile_loaded(act, i)
                        if i >= 1:
                            act.wait_ge(ssq_ready, i)
                        nc.scalar.activation(sq[:, 0:NSA_HEADS, :].rearrange("p h d -> p (h d)"),
                                             zt[:, b, NQ:NQ + NSA_HEADS * HEAD], ACT.Square)
                        nc.scalar.activation(
                            sq[:, NSA_HEADS:, :].rearrange("p (k g) d -> p k (g d)", k=2),
                            zt[:, b, NKS:NKS + 4 * P].rearrange("p (k c) -> p k c", k=2)[:, :, 0:P],
                            ACT.Square).then_inc(squared, 1)
                        if i >= QR:
                            act.wait_ge(pool_mixed, i - QR + 1)
                            act.wait_ge(nsa_mixed, GROUPS * (i - QR + 1))
                        nc.scalar.activation(swish[:, qr, :], zt[:, b, RG:RG + RW], ACT.Exp, scale=-1.0)
                        nc.scalar.activation(gates[:, qr, :], zt[:, b, NG:NG + 3 * NSA_HEADS], ACT.Exp,
                                             scale=-1.0).then_inc(exps_ready, 1)
                    elif piece == "high":
                        act.wait_ge(normed, i + 1)
                        if i >= 1:
                            act.wait_ge(prep_sum, fill_n(i - 1, "q1") + 1)
                        nc.scalar.copy(q_pack[:, :, 0:HEAD].bitcast(F32R), qn[:, :, :])
                        nc.scalar.copy(k_pack[:, :, HEAD:].bitcast(F32R), kn[:, :, :]).then_inc(high_ready, 1)
                    elif piece in ("read qq", "read kz"):
                        name = piece[5:]
                        act.wait_ge(prep_sum, fill_n(i, name) + 1)
                        dst = qqT if name == "qq" else kzT
                        nc.scalar.copy(dst[:, :, :].rearrange("p h c -> p (h c)"), prep_ps[:, :])\
                            .then_inc(prep_read_act, 1)
                    elif piece == "read k":
                        act.wait_ge(prep_sum, fill_n(i, "k") + 1)
                        if i >= WR:
                            last_use(act, GROUPS * (i - WR + WIN_TILES) - 1, WIN)
                        bank = prep_ps[:, :].rearrange("p (k g c) -> p k g c", k=2, g=GROUPS)
                        s, w = slice(i * P, (i + 1) * P), slice(i % WR * P, (i % WR + 1) * P)
                        nc.scalar.copy(kb_s[:, :, s], bank[:, 0, :, :])
                        nc.scalar.copy(kb_w[:, :, w], bank[:, 1, :, :])
                        nc.scalar.copy(ka_s[0:HEAD, :, s], bank[HEAD:, 0, :, :])
                        nc.scalar.copy(ka_w[0:HEAD, :, w], bank[HEAD:, 1, :, :]).then_inc(prep_read_act, 1)
                    elif piece in ("read q0", "read q1"):
                        name = piece[5:]
                        act.wait_ge(prep_sum, fill_n(i, name) + 1)
                        if i >= QR:
                            last_use(act, GROUPS * (i - QR) + GROUPS - 1, SLC)
                        bank = prep_ps[:, :].rearrange("p (h c) -> p h c", h=HPG)
                        g = FILLS.index(name) - FILLS.index("q0")
                        h = slice(g * HPG, (g + 1) * HPG)
                        nc.scalar.copy(qb[:, qr, h, :], bank)
                        nc.scalar.copy(qa_w[0:HEAD, qr, h, :], bank[0:HEAD, :, :])
                        nc.scalar.copy(qa_s[0:HEAD, qr, h, :], bank[0:HEAD, :, :]).then_inc(prep_read_act, 1)
                elif kind == "weights":
                    act.wait_ge(cmp_max_ready, u + 1)
                    if u >= 1:
                        act.wait_ge(score_sum, plan.scores_n[u - 1, CMP, 0] + 1)
                        act.wait_ge(front_read, 2 * u - 1)
                    for h in range(HPG):
                        exp = nc.scalar.activation(cmp_weights[:, h, :], front_ps[:, h * P:(h + 1) * P], ACT.Exp,
                                                   bias=neg_max[:, CMP, h:h + 1], accum_out=cmp_sum[:, h:h + 1])
                    exp.then_inc(cmp_weighted, 1)
                elif kind == "row":
                    branch = step[2]
                    n = plan.scores_n[u, branch, "row"]
                    qr, g = u // GROUPS % QR, u % GROUPS
                    q = qa_s if branch == SLC else qa_w
                    act.wait_ge(score_sum, n + 1)
                    nc.scalar.copy(q[MAX_ROW:MAX_ROW + 1, qr, g * HPG:(g + 1) * HPG, :],
                                   score_ps[n % 2][MAX_ROW:MAX_ROW + 1, :].rearrange("p (h c) -> p h c", h=HPG))\
                        .then_inc(score_read, 1)
                elif kind == "scores":
                    n, p = plan.scores_n[step[1:]], plan.probs_n[step[1:]]
                    act.wait_ge(score_sum, n + 1)
                    if p >= PR:
                        act.wait_ge(probs_used, plan.values_n[plan.probs_by[p - PR]] + 1)
                    if step[2] == CMP:
                        ins = nc.scalar.copy(probs[:, p % PR, :], score_ps[n % 2][:, :])
                    else:
                        ins = nc.scalar.activation(probs[:, p % PR, :], score_ps[n % 2][:, :], ACT.Exp)
                    ins.then_inc(score_read, 1)

        @block.vector
        def _(dve):
            link = chain(dve, dve_done)
            dve.wait_ge(cleared, 1)

            def bc(ap, n):
                return ap.unsqueeze(2).to_broadcast([P, ap.shape[1], n])

            def maxima_done(u, branch):
                link(nc.vector.tensor_scalar(neg_max[:, branch, :], top[:, branch, :], MASKED / 10, -1.0,
                                             ALU.max, ALU.mult))
                if u >= 1:
                    dve.wait_ge(score_sum, plan.scores_n[u - 1, branch, "row"] + 1)
                nc.vector.tensor_tensor(diag[branch][:, :, :], ident[:, :].unsqueeze(1).to_broadcast([P, HPG, P]),
                                        bc(neg_max[:, branch, :], P), ALU.mult).then_inc(diag_ready[branch], 1)

            for step in plan.steps:
                kind, u = step[0], step[1]
                if kind == "prep":
                    i, piece = step[1:]
                    b, qr = i % 2, i % QR
                    if piece == "sums":
                        dve.wait_ge(squared, i + 1)
                        if i >= 1:
                            dve.wait_ge(rstd_ready, i)
                        nc.vector.tensor_reduce(ssq[:, :], sq[:, :, :], AX_X, ALU.add).then_inc(ssq_ready, 1)
                    elif piece == "gates":
                        dve.wait_ge(exps_ready, i + 1)
                        for t in (swish, gates):
                            link(nc.vector.tensor_scalar(t[:, qr, :], t[:, qr, :], 1.0, None, ALU.add))
                            link(nc.vector.reciprocal(t[:, qr, :], t[:, qr, :]))
                        nc.vector.tensor_tensor(swish[:, qr, :], swish[:, qr, :], zt[:, b, RG:RG + RW],
                                                ALU.mult).then_inc(gates_ready, 1)
                    elif piece == "normalise k":
                        dve.wait_ge(rstd_ready, i + 1)
                        if i >= 1:
                            dve.wait_ge(packs_ready, i)
                        for k, c in enumerate((NKS, NKW)):
                            part = slice(GROUPS * k, GROUPS * (k + 1))
                            heads = slice(NSA_HEADS + GROUPS * k, NSA_HEADS + GROUPS * (k + 1))
                            link(nc.vector.tensor_tensor(
                                kn[:, part, :], zt[:, b, c:c + P].rearrange("p (g d) -> p g d", g=GROUPS),
                                bc(rstd[:, heads], HEAD), ALU.mult))
                        link(nc.vector.tensor_tensor(kn[:, :, :], kn[:, :, :],
                                                     k_gains[:, :].unsqueeze(1).to_broadcast([P, 2 * GROUPS, HEAD]),
                                                     ALU.mult))
                    elif piece == "normalise q":
                        q = zt[:, b, NQ:NQ + NSA_HEADS * HEAD].rearrange("p (h d) -> p h d", d=HEAD)
                        link(nc.vector.tensor_tensor(qn[:, :, :], q, bc(rstd[:, 0:NSA_HEADS], HEAD), ALU.mult))
                        nc.vector.tensor_tensor(qn[:, :, :], qn[:, :, :],
                                                q_gains[:, :].unsqueeze(1).to_broadcast([P, NSA_HEADS, HEAD]),
                                                ALU.mult).then_inc(normed, 1)
                    elif piece == "low":
                        dve.wait_ge(normed, i + 1)
                        dve.wait_ge(high_ready, i + 1)
                        nc.vector.tensor_tensor(k_pack[:, :, 0:HEAD].bitcast(F32R), kn[:, :, :], k_pack[:, :, HEAD:],
                                                ALU.subtract)
                        nc.vector.tensor_tensor(q_pack[:, :, HEAD:].bitcast(F32R), qn[:, :, :], q_pack[:, :, 0:HEAD],
                                                ALU.subtract).then_inc(packs_ready, 1)
                    elif piece == "read scores":
                        dve.wait_ge(prep_sum, fill_n(i, "scores") + 1)
                        nc.vector.tensor_tensor(ret_scores[:, :, :].rearrange("p h c -> p (h c)"),
                                                prep_ps[:, :], decay[:, :, :].rearrange("p h c -> p (h c)"),
                                                ALU.mult).then_inc(prep_read_dve, 1)
                    elif piece == "read output":
                        dve.wait_ge(prep_sum, fill_n(i, "output") + 1)
                        bank = prep_ps[:, :].rearrange("p (two h d) -> p two h d", two=2, h=RET_HEADS)
                        if i >= 1:
                            dve.wait_ge(prep_read_dve, 2 * i)
                            dve.wait_ge(pool_mixed, i)
                        nc.vector.tensor_copy(o_ret[:, :, :], bank[:, 0, :, :]).then_inc(o_ready, 1)
                        link(nc.vector.tensor_tensor(state[:, :, :], state[:, :, :], bc(row_decay[:, 2, :], HEAD),
                                                     ALU.mult))
                        nc.vector.tensor_tensor(state[:, :, :], state[:, :, :], bank[:, 1, :, :],
                                                ALU.add).then_inc(prep_read_dve, 1)
                    elif piece == "output sums":
                        dve.wait_ge(o_squared, i + 1)
                        nc.vector.tensor_reduce(o_ssq[:, :], o_sq[:, :, :], AX_X, ALU.add).then_inc(o_ssq_ready, 1)
                elif kind == "compressed":
                    dve.wait_ge(compressed_sum, u + 1)
                    link(nc.vector.tensor_reduce(top[:, CMP, :], front_ps[:, :].rearrange("p (h n) -> p h n", h=HPG),
                                                 AX_X, ALU.max))
                    if u >= 1:
                        dve.wait_ge(cmp_weighted, u)
                    nc.vector.tensor_scalar(neg_max[:, CMP, :], top[:, CMP, :], MASKED / 10, -1.0,
                                            ALU.max, ALU.mult).then_inc(cmp_max_ready, 1)
                elif kind == "maximum":
                    branch, (h, c) = step[2:]
                    i = u // GROUPS
                    n = plan.maxima_n[u, branch, (h, c)]
                    bank = maxima_ps[n % 2]
                    dve.wait_ge(maxima_sum, n + 1)
                    keys = (len(plan.key_tiles(u, branch)) if branch == WIN else min(4, i + 1 - 4 * c)) * P
                    dst = top[:, WIN, h:h + 1] if branch == WIN else part_max[:, h, c:c + 1]
                    nc.vector.tensor_reduce(dst, bank[:, 0:keys], AX_X, ALU.max).then_inc(maxima_read, 1)
                    if (h, c) == plan.max_fills(u, branch)[-1]:
                        dve.wait_ge(maxima_read, n + 1)
                        if branch == SLC:
                            link(nc.vector.tensor_reduce(top[:, SLC, :], part_max[:, :, 0:c + 1], AX_X, ALU.max))
                        maxima_done(u, branch)
                elif kind == "selected":
                    qr, g = u // GROUPS % QR, u % GROUPS
                    dve.wait_ge(select_sum, u + 1)
                    nc.vector.tensor_copy(qa_s[64:64 + NBLK, qr, g * HPG:(g + 1) * HPG, :],
                                          front_ps[64:64 + NBLK, BANK - P:].unsqueeze(1)
                                          .to_broadcast([NBLK, HPG, P])).then_inc(rows_set, 1)
                elif kind == "post":
                    branch = step[2]
                    i, g = divmod(u, GROUPS)
                    qr = i % QR
                    last_use(dve, u, branch)
                    out = (selected_ps[u % 2] if branch == SLC else front_ps)[:, 0:HPG * VCOLS[branch]]\
                        .rearrange("p (h c) -> p h c", h=HPG)
                    dst = mixed[:, qr, 2 * RW + g * HPG * HEAD:2 * RW + (g + 1) * HPG * HEAD]\
                        .rearrange("p (h d) -> p h d", h=HPG)
                    gate = gates[:, qr, :].rearrange("p (h c) -> p h c", c=3)[:, g * HPG:(g + 1) * HPG, branch]
                    if branch == CMP:
                        dve.wait_ge(cmp_weighted, u + 1)
                        link(nc.vector.tensor_scalar(den[:, :], cmp_sum[:, :], 1e-30, None, ALU.max))
                        link(nc.vector.reciprocal(den[:, :], den[:, :]))
                        link(nc.vector.tensor_tensor(importance[:, :, :], out[:, :, HEAD:],
                                                     bc(den[:, :], NBLK), ALU.mult))
                        link(nc.vector.tensor_tensor(weight[:, :], den[:, :], gate, ALU.mult))
                        if i >= QR and g == 0:
                            dve.wait_ge(mixed_stored[qr], 16 * (i // QR))
                        nc.vector.tensor_tensor(dst, out[:, :, 0:HEAD], bc(weight[:, :], HEAD), ALU.mult)\
                            .then_inc(front_read, 1)
                        dve.wait_ge(front_read, 2 * u + 1)
                        link(nc.vector.tensor_reduce(sel_score[:, :],
                                                     importance[:, :, :].rearrange("p h j -> p j h"),
                                                     AX_X, ALU.add))
                        for t, op in ((0, ALU.add), (1, ALU.mult), (2, ALU.add)):
                            link(nc.vector.tensor_tensor(sel_score[:, :], sel_score[:, :],
                                                         sel_table[:, i % SR, t, :], op))
                        link(nc.vector.max(best[:, :], sel_score[:, :]))
                        link(nc.vector.match_replace(chosen[:, :], best[:, :], sel_score[:, :], -3e38))
                        if u >= 1:
                            dve.wait_ge(select_sum, u)
                        nc.vector.tensor_scalar(selection[:, 64:64 + NBLK], chosen[:, :], -1e38, MASKED,
                                                ALU.is_gt, ALU.mult).then_inc(sel_ready, 1)
                        dve.wait_ge(sel_ready, u + 1)
                    else:
                        read, count = (selected_read, u + 1) if branch == SLC else (front_read, 2 * u + 2)
                        link(nc.vector.tensor_scalar(den[:, :], out[:, :, HEAD], 1e-30, None, ALU.max))
                        link(nc.vector.reciprocal(den[:, :], den[:, :]))
                        link(nc.vector.tensor_tensor(weight[:, :], den[:, :], gate, ALU.mult))
                        nc.vector.tensor_tensor(weighted[:, :, :], out[:, :, 0:HEAD], bc(weight[:, :], HEAD),
                                                ALU.mult).then_inc(read, 1)
                        dve.wait_ge(read, count)
                        add = nc.vector.tensor_tensor(dst, dst, weighted[:, :, :], ALU.add)
                        if branch == SLC:
                            add.then_inc(nsa_mixed, 1)
                            dve.wait_ge(nsa_mixed, u + 1)
                        else:
                            link(add)

        @block.tensor
        def _(pe):
            pe.wait_ge(cleared, 1)

            for step in plan.steps:
                kind, u = step[0], step[1]
                i, g = divmod(u, GROUPS)
                qr = i % QR
                if kind == "prep":
                    i, piece = step[1:]
                    b = i % 2
                    if not piece.startswith("fill"):
                        continue
                    name = piece[5:]
                    if name != FILLS[0]:
                        prep_read(pe, i, FILLS[FILLS.index(name) - 1])
                    elif i >= 1:
                        prep_read(pe, i - 1, FILLS[-1])
                    if name in ("qq", "kz"):
                        pe.wait_ge(rot_ready, i + 1)
                        for h in range(RET_HEADS):
                            mm = nc.tensor.transpose(prep_ps[:, h * P:(h + 1) * P], (qq if name == "qq" else kz)[:, h, :],
                                                     ident[:, :])
                    elif name == "scores":
                        for h in range(RET_HEADS):
                            mm = nc.tensor.matmul(prep_ps[:, h * P:(h + 1) * P], kzT[:, h, :], qqT[:, h, :],
                                                  start=True, stop=True)
                    elif name == "output":
                        for h in range(RET_HEADS):
                            v = zt[:, b, RV + h * HEAD:RV + (h + 1) * HEAD]
                            o = prep_ps[:, h * HEAD:(h + 1) * HEAD]
                            nc.tensor.matmul(o, ret_scores[:, h, :], v, start=True, stop=False)
                            nc.tensor.matmul(o, qqT[:, h, :], state[:, h, :], start=False, stop=True)
                            mm = nc.tensor.matmul(prep_ps[:, RW + h * HEAD:RW + (h + 1) * HEAD], zk[:, h, :], v,
                                                  start=True, stop=True)
                    else:
                        pe.wait_ge(packs_ready, i + 1)
                        for h in range(HPG):
                            src = {"k": k_pack[:, h, :], "q0": q_pack[:, h, :], "q1": q_pack[:, HPG + h, :]}[name]
                            mm = nc.tensor.transpose(prep_ps[:, h * P:(h + 1) * P], src, ident[:, :])
                    mm.then_inc(prep_sum, 1)
                elif kind == "compressed":
                    prep_read(pe, i, "q1")
                    if u >= 1:
                        pe.wait_ge(rows_set, u)
                    nc.tensor.matmul(front_ps[:, :], cmp_mask[:, i * P:(i + 1) * P],
                                     ident_bf[:, :].unsqueeze(1).to_broadcast([P, HPG, P]),
                                     start=True, stop=False, skip_group_check=True)
                    for h in range(HPG):
                        out = front_ps[:, h * P:(h + 1) * P]
                        nc.tensor.matmul(out, qb[0:HEAD, qr, g * HPG + h, :], cmp_a[0:HEAD, g, :],
                                         start=False, stop=False, skip_group_check=True)
                        mm = nc.tensor.matmul(out, qb[:, qr, g * HPG + h, :], cmp_b[:, g, :],
                                              start=False, stop=h == HPG - 1, skip_group_check=True)
                    mm.then_inc(compressed_sum, 1)
                elif kind == "maximum":
                    branch, (h, c) = step[2:]
                    n = plan.maxima_n[u, branch, (h, c)]
                    bank = maxima_ps[n % 2]
                    if n >= 2:
                        pe.wait_ge(maxima_read, n - 1)
                    if branch == WIN:
                        slots = sorted(j % WR for j in plan.key_tiles(u, WIN))
                        runs = [(at, slot) for at, slot in enumerate(slots) if slot - 1 not in slots]
                        for (first, slot), (end, _) in zip(runs, runs[1:] + [(len(slots), None)]):
                            mm = nc.tensor.matmul(bank[:, first * P:end * P], qb[0:HEAD, qr, g * HPG + h, :],
                                                  ka_w[0:HEAD, g, slot * P:(slot + end - first) * P],
                                                  start=first == 0, stop=False, skip_group_check=True)
                        for mask, j in ((beyond, i - 2), (causal, i)):
                            if j >= 0:
                                s = slots.index(j % WR)
                                mm = nc.tensor.matmul(bank[:, s * P:(s + 1) * P], mask[:, :], ident_bf[:, :],
                                                      start=False, stop=j == i, skip_group_check=True)
                    else:
                        if (h, c) == (0, 0):
                            pe.wait_ge(rows_set, u + 1)
                        keys = min(4, i + 1 - 4 * c) * P
                        own = i // 4 == c
                        mm = nc.tensor.matmul(bank[:, 0:keys], qa_s[0:96, qr, g * HPG + h, :],
                                              ka_s[0:96, g, 4 * c * P:4 * c * P + keys],
                                              start=True, stop=not own, skip_group_check=True)
                        if own:
                            mm = nc.tensor.matmul(bank[:, keys - P:keys], causal[:, :], ident_bf[:, :],
                                                  start=False, stop=True, skip_group_check=True)
                    mm.then_inc(maxima_sum, 1)
                elif kind == "select":
                    pe.wait_ge(sel_ready, u + 1)
                    pe.wait_ge(front_read, 2 * u + 2)
                    nc.tensor.transpose(front_ps[:, BANK - P:], selection[:, :], ident[:, :]).then_inc(select_sum, 1)
                elif kind == "row":
                    branch = step[2]
                    n = plan.scores_n[u, branch, "row"]
                    if n >= 2:
                        pe.wait_ge(score_read, n - 1)
                    pe.wait_ge(diag_ready[branch], u + 1)
                    nc.tensor.matmul(score_ps[n % 2][:, :], ones[:, :], diag[branch][:, :, :],
                                     start=True, stop=True).then_inc(score_sum, 1)
                elif kind == "scores":
                    branch, j = step[2:]
                    n = plan.scores_n[u, branch, j]
                    bank = score_ps[n % 2]
                    if n >= 2:
                        pe.wait_ge(score_read, n - 1)
                    if branch == CMP:
                        pe.wait_ge(cmp_weighted, u + 1)
                        for h in range(HPG):
                            mm = nc.tensor.transpose(bank[:, h * P:(h + 1) * P], cmp_weights[:, h, :], ident[:, :])
                        mm.then_inc(score_sum, 1)
                        continue
                    pe.wait_ge(score_read, plan.scores_n[u, branch, "row"] + 1)
                    heads = slice(g * HPG, (g + 1) * HPG)
                    if branch == WIN:
                        ka, kb, cols, qa = ka_w, kb_w, slice(j % WR * P, (j % WR + 1) * P), qa_w
                        mask = {i: causal[:, :], i - 2: beyond[:, :]}.get(j)
                    else:
                        ka, kb, cols, qa = ka_s, kb_s, slice(j * P, (j + 1) * P), qa_s
                        mask = causal[:, :] if j == i else None
                    nc.tensor.matmul(bank[:, :], ka[0:MAX_ROW + 1, g, cols], qa[0:MAX_ROW + 1, qr, heads, :],
                                     start=True, stop=False)
                    mm = nc.tensor.matmul(bank[:, :], kb[:, g, cols], qb[:, qr, heads, :], start=False,
                                          stop=mask is None)
                    if mask is not None:
                        mm = nc.tensor.matmul(bank[:, :], ident_bf[:, :], mask.unsqueeze(1).to_broadcast([P, HPG, P]),
                                              start=False, stop=True)
                    mm.then_inc(score_sum, 1)
                elif kind == "values":
                    branch, j = step[2:]
                    n, p = plan.scores_n[u, branch, j], plan.probs_n[u, branch, j]
                    tiles = plan.key_tiles(u, branch)
                    pe.wait_ge(score_read, n + 1)
                    if j == tiles[0]:
                        if branch == SLC and u >= 2:
                            pe.wait_ge(selected_read, u - 1)
                        elif branch == CMP:
                            pe.wait_ge(cmp_weighted, u + 1)
                        elif branch == WIN:
                            pe.wait_ge(front_read, 2 * u + 1)
                    if branch != CMP:
                        pe.wait_ge(v_ready, 2 * (j + 1))
                    v = {CMP: cmp_v[:, g, :], WIN: v_w[:, j % WR, g, :], SLC: v_s[:, j, g, :]}[branch]
                    out = (selected_ps[u % 2] if branch == SLC else front_ps)[:, 0:HPG * VCOLS[branch]]\
                        .rearrange("p (h c) -> p h c", h=HPG)
                    for h in range(HPG):
                        mm = nc.tensor.matmul(out[:, h, :], probs[:, p % PR, h * P:(h + 1) * P], v,
                                              start=j == tiles[0] and h == 0, stop=j == tiles[-1],
                                              skip_group_check=True)
                    mm.then_inc(probs_used, 1)


def output_phase(nc, mixed, x, w_out, identity, x2):
    S, D = x.shape
    M = mixed.shape[1]
    KT = M // P
    NT = S // P
    CB = D // BANK
    GB = M // BANK

    with ExitStack() as stack:
        m = Space(nc, stack, "out")
        ident = m.sb("ident", [P, P])
        w_raw = m.sb("w_raw", [P, KT, D])
        w_hi = m.sb("w_hi", [P, KT, D], F32R)
        w_lo = m.sb("w_lo", [P, KT, D], F32R)
        mt = m.sb("mixed", [P, 2, M])
        xt = m.sb("x", [P, 2, D])
        t_hi = m.sb("mixedT_hi", [P, 2, KT, P], F32R)
        t_lo = m.sb("mixedT_lo", [P, 2, KT, P], F32R)
        tp = [m.ps(f"transposed{i}", [P, BANK]) for i in range(2 * GB)]
        acc = [m.ps(f"acc{i}", [P, BANK]) for i in range(2 * CB)]

        ident_in = m.sem("ident_in")
        w_loaded = m.sems("w_loaded", KT)
        w_hi_done = m.sem("w_hi_done")
        w_lo_even = m.sem("w_lo_even")
        w_lo_odd = m.sem("w_lo_odd")
        mixed_in = m.sems("mixed_in", 2)
        x_in = m.sems("x_in", 2)
        transposed = m.sem("transposed")
        hi_done = m.sem("hi_done")
        lo_done = m.sem("lo_done")
        product = m.sem("product")
        added = m.sem("added")
        stored = m.sems("stored", 2)
        block = stack.enter_context(nc.Block())

        @block.sync
        def _(sp):
            def load_w(k):
                sp.dma_start(w_raw[:, k, :], w_out[k * P:(k + 1) * P, :]).then_inc(w_loaded[k], 16)

            sp.dma_start(ident[:, :], identity).then_inc(ident_in, 16)
            for k in range(2):
                load_w(k)
            sp.dma_start(mt[:, 0, :], mixed[0:P, :]).then_inc(mixed_in[0], 16)
            for k in range(2, KT):
                load_w(k)
            for b in range(2):
                sp.sem_inc(stored[b], 16)
            def load_mixed(i, b):
                sp.wait_ge(transposed, i + (b + 1))
                sp.dma_start(mt[:, b, :], mixed[bass.ds((i + b) * P, P), :]).then_inc(mixed_in[b], 16)

            def load_x(i, b):
                sp.wait_ge(stored[b], i * 8 + 16)
                sp.dma_start(xt[:, b, :], x[bass.ds((i + b) * P, P), :]).then_inc(x_in[b], 16)

            load_x(0, 0)
            load_mixed(0, 1)
            load_x(0, 1)
            with sp.Fori(0, NT // 2 - 1) as r:
                for b in range(2):
                    load_mixed(r * 2 + 2, b)
                    load_x(r * 2 + 2, b)

        @block.gpsimd
        def _(pool):
            for k in range(0, KT, 2):
                pool.wait_ge(w_hi_done, k + 1)
                nc.gpsimd.tensor_tensor(w_lo[:, k, :], w_raw[:, k, :], w_hi[:, k, :].bitcast(F32),
                                        ALU.subtract).then_inc(w_lo_even, 1)

        @block.scalar
        def _(act):
            def weights_high(k):
                act.wait_ge(w_loaded[k], 16)
                nc.scalar.copy(w_hi[:, k, :], w_raw[:, k, :]).then_inc(w_hi_done, 1)

            act.sem_inc(hi_done, 2)

            def high(i, b):
                act.wait_ge(transposed, i + (b + 3))
                act.wait_ge(product, i + (b + 1))
                for q in range(GB):
                    copy = nc.scalar.copy(t_hi[:, b, 4 * q:4 * q + 4, :],
                                          tp[b * GB + q][:, :].rearrange("p (k c) -> p k c", c=P))
                copy.then_inc(hi_done, 1)

            def store(i, b):
                act.wait_ge(added, i + (b + 3))
                act.dma_start(x2[bass.ds((i + b) * P, P), :], xt[:, b, :]).then_inc(stored[b], 16)

            weights_high(0)
            weights_high(1)
            high(0, 0)
            for k in range(2, KT):
                weights_high(k)
            with act.Fori(0, NT // 2 - 1) as r:
                high(r * 2, 1)
                store(r * 2, 0)
                high(r * 2 + 2, 0)
                store(r * 2, 1)
            high(NT - 2, 1)
            store(NT - 2, 0)
            store(NT - 2, 1)
            for b in range(2):
                act.wait_ge(stored[b], 16 * (NT // 2 + 1))

        @block.vector
        def _(dve):
            def low(i, b):
                dve.wait_ge(hi_done, i + (b + 3))
                for q in range(GB):
                    sub = nc.vector.tensor_tensor(t_lo[:, b, 4 * q:4 * q + 4, :],
                                                  tp[b * GB + q][:, :].rearrange("p (k c) -> p k c", c=P),
                                                  t_hi[:, b, 4 * q:4 * q + 4, :].bitcast(F32), ALU.subtract)
                sub.then_inc(lo_done, 1)

            def add(i, b):
                dve.wait_ge(product, i + (b + 3))
                dve.wait_ge(x_in[b], i * 8 + 16)
                for c in range(CB):
                    cols = slice(c * BANK, (c + 1) * BANK)
                    ins = nc.vector.tensor_tensor(xt[:, b, cols], xt[:, b, cols], acc[b * CB + c][:, :], ALU.add)
                ins.then_inc(added, 1)

            dve.sem_inc(lo_done, 2)
            dve.sem_inc(added, 2)
            for k in range(1, KT, 2):
                dve.wait_ge(w_hi_done, k + 1)
                nc.vector.tensor_tensor(w_lo[:, k, :], w_raw[:, k, :], w_hi[:, k, :].bitcast(F32),
                                        ALU.subtract).then_inc(w_lo_odd, 1)
                if k == 1:
                    low(0, 0)
            with dve.Fori(0, NT - 2, 2) as i:
                low(i, 1)
                add(i, 0)
                low(i + 2, 0)
                add(i, 1)
            low(NT - 2, 1)
            add(NT - 2, 0)
            add(NT - 2, 1)

        @block.tensor
        def _(pe):
            def transpose(i, b):
                pe.wait_ge(mixed_in[b], i * 8 + 16)
                pe.wait_ge(lo_done, i + (b + 1))
                for k in range(KT):
                    mm = nc.tensor.transpose(tp[b * GB + k // 4][:, k % 4 * P:k % 4 * P + P],
                                             mt[:, b, k * P:(k + 1) * P], ident[:, :])
                mm.then_inc(transposed, 1)

            def multiply(i, b, order=[(c, k) for c in range(CB) for k in range(KT)]):
                pe.wait_ge(lo_done, i + (b + 3))
                pe.wait_ge(added, i + (b + 1))
                for c, k in order:
                    if order is by_weights and c == 0:
                        pe.wait_ge((w_lo_even, w_lo_odd)[k % 2], k // 2 + 1)
                    for a, w in ((t_hi, w_hi), (t_lo, w_hi), (t_hi, w_lo)):
                        mm = nc.tensor.matmul(acc[b * CB + c][:, :], a[:, b, k, :],
                                              w[:, k, c * BANK:(c + 1) * BANK],
                                              start=k == 0 and a is t_hi and w is w_hi,
                                              stop=k == KT - 1 and w is w_lo)
                mm.then_inc(product, 1)

            pe.wait_ge(ident_in, 16)
            pe.sem_inc(transposed, 2)
            pe.sem_inc(product, 2)
            transpose(0, 0)
            by_weights = [(c, k) for k in range(KT) for c in range(CB)]
            multiply(0, 0, by_weights)
            transpose(0, 1)
            transpose(2, 0)
            multiply(0, 1)
            with pe.Fori(2, NT - 2, 2) as i:
                transpose(i, 1)
                multiply(i, 0)
                transpose(i + 2, 0)
                multiply(i, 1)
            transpose(NT - 2, 1)
            multiply(NT - 2, 0)
            multiply(NT - 2, 1)


def mlp_phase(nc, x2, norm_mlp, w_up, w_down, identity, out):
    S, D = x2.shape
    FF = w_up.shape[1]
    KT = D // P
    T = BANK
    TT = T // P
    GROUPS = S // T
    FB = 2 * P
    FT = FB // P
    NB = FF // FB
    CB = D // BANK
    GB = D // BANK
    SUMS = TT * CB
    AR = 4

    with ExitStack() as stack:
        m = Space(nc, stack, "mlp")
        ident = m.sb("ident", [P, P])
        gain = m.sb("gain", [P, D])
        neg_half = m.sb("neg_half", [P, 1])
        y = m.sb("y", [P, 2, TT, D])
        xn = m.sb("x_normed", [P, TT, D])
        squares = m.sb("squares", [P, TT, D], BF16)
        sum_sq = m.sb("sum_sq", [P, TT])
        mean_sq = m.sb("mean_sq", [P, TT])
        rstd = m.sb("rstd", [P, TT])
        h_hi = m.sb("hT_hi", [P, KT, T], F32R)
        h_lo = m.sb("hT_lo", [P, KT, T], F32R)
        up_raw = m.sb("up_raw", [P, KT, FB])
        up_hi = m.sb("up_hi", [P, 2, KT, FB], F32R)
        up_lo = m.sb("up_lo", [P, 2, KT, FB], F32R)
        dn_raw = m.sb("down_raw", [P, FT, D])
        dn_hi = m.sb("down_hi", [P, 2, FT, D], F32R)
        dn_lo = m.sb("down_lo", [P, 2, FT, D], F32R)
        relu = m.sb("relu", [P, 2, T])
        f = m.sb("f", [P, 2, T])
        f_hi = m.sb("f_hi", [P, 2, FT, T], F32R)
        f_lo = m.sb("f_lo", [P, 2, FT, T], F32R)
        tp = [m.ps(f"transposed{i}", [P, BANK]) for i in range(GB)]
        up_ps = [m.ps(f"up{i}", [P, BANK]) for i in range(2)]
        acc = [m.ps(f"acc{i}", [P, BANK]) for i in range(AR)]

        const_in = m.sem("const_in")
        const_set = m.sem("const_set")
        y_in = m.sems("y_in", 2)
        y_out = m.sems("y_out", 2)
        squared = m.sem("squared")
        mean_done = m.sem("mean_done")
        rstd_done = m.sem("rstd_done")
        normed = m.sem("normed")
        transposed = m.sem("transposed")
        hi_done = m.sem("hi_done")
        lo_done = m.sem("lo_done")
        up_loaded = m.sem("up_loaded")
        dn_loaded = m.sem("down_loaded")
        up_hi_done = m.sem("up_hi_done")
        dn_hi_done = m.sem("down_hi_done")
        up_lo_done = m.sem("up_lo_done")
        dn_lo_done = m.sem("down_lo_done")
        up_sum = m.sem("up_sum")
        relu_done = m.sem("relu_done")
        f_done = m.sem("f_done")
        f_hi_done = m.sem("f_hi_done")
        f_lo_done = m.sem("f_lo_done")
        dn_sum = m.sem("down_sum")
        added = m.sem("added")

        up_view = w_up.rearrange("(k p) f -> p k f", p=P)
        dn_view = w_down.rearrange("(k p) n -> p k n", p=P)
        block = stack.enter_context(nc.Block())

        @block.sync
        def _(sp):
            def load_y(g):
                b = g % 2
                sp.wait_ge(y_out[b], 16 * (g // 2 + 1))
                sp.dma_start(y[:, b, :, :], x2[g * T:(g + 1) * T, :].rearrange("(t p) d -> p t d", p=P))\
                    .then_inc(y_in[b], 16)

            def store_y(g):
                sp.wait_ge(added, (g + 1) * NB * SUMS + AR)
                sp.dma_start(out[g * T:(g + 1) * T, :].rearrange("(t p) d -> p t d", p=P), y[:, g % 2, :, :])\
                    .then_inc(y_out[g % 2], 16)

            AHEAD = 3
            sp.dma_start(ident[:, :], identity).then_inc(const_in, 16)
            sp.dma_start(gain[:, :], norm_mlp.partition_broadcast(P)).then_inc(const_in, 16)
            for b in range(2):
                sp.sem_inc(y_out[b], 16)
            load_y(0)
            def load_w(n, c):
                sp.wait_ge(up_lo_done, n + 1)
                sp.dma_start(up_raw[:, :, :], up_view[:, :, bass.ds(c * FB, FB)]).then_inc(up_loaded, 16)
                sp.wait_ge(dn_lo_done, n + 1)
                sp.dma_start(dn_raw[:, :, :], dn_view[:, bass.ds(c * FT, FT), :]).then_inc(dn_loaded, 16)

            for g in range(GROUPS):
                for c in range(AHEAD):
                    load_w(g * NB + c, c)
                if g > 0:
                    store_y(g - 1)
                if g + 1 < GROUPS:
                    load_y(g + 1)
                with sp.Fori(0, NB - AHEAD) as r:
                    load_w(r + (g * NB + AHEAD), r + AHEAD)
            store_y(GROUPS - 1)
            sp.wait_ge(y_out[0], 16 * (GROUPS // 2 + 1))
            sp.wait_ge(y_out[1], 16 * (GROUPS // 2 + 1))

        @block.gpsimd
        def _(pool):
            pool.sem_inc(up_lo_done, 1)
            pool.sem_inc(dn_lo_done, 1)
            nc.gpsimd.memset(neg_half[:, :], -0.5).then_inc(const_set, 1)
            pool.wait_ge(const_set, 1)

            def split_up(n, b):
                pool.wait_ge(up_hi_done, n + 1)
                nc.gpsimd.tensor_tensor(up_lo[:, b, :, :], up_raw[:, :, :], up_hi[:, b, :, :].bitcast(F32),
                                        ALU.subtract).then_inc(up_lo_done, 1)

            def split_down(n, b):
                pool.wait_ge(dn_hi_done, n + 1)
                nc.gpsimd.tensor_tensor(dn_lo[:, b, :, :], dn_raw[:, :, :], dn_hi[:, b, :, :].bitcast(F32),
                                        ALU.subtract).then_inc(dn_lo_done, 1)

            def root(g):
                if g >= 1:
                    pool.wait_ge(normed, g * TT)
                for t in range(TT):
                    pool.wait_ge(squared, g * TT + t + 1)
                    nc.gpsimd.tensor_scalar(mean_sq[:, t:t + 1], sum_sq[:, t:t + 1], 1.0 / D, EPS,
                                            ALU.mult, ALU.add).then_inc(mean_done, 1)
                    pool.wait_ge(mean_done, g * TT + t + 1)
                    nc.gpsimd.tensor_tensor(rstd[:, t:t + 1], mean_sq[:, t:t + 1], neg_half[:, :],
                                            ALU.pow).then_inc(rstd_done, 1)

            root(0)
            for g in range(GROUPS):
                with pool.Fori(0, NB - 2, 2) as c:
                    for b in range(2):
                        split_up(c + (g * NB + b), b)
                        split_down(c + (g * NB + b), b)
                n = (g + 1) * NB - 2
                split_up(n, 0)
                split_down(n, 0)
                if g + 1 < GROUPS:
                    root(g + 1)
                split_up(n + 1, 1)
                split_down(n + 1, 1)

        @block.scalar
        def _(act):
            def split_up(n, b):
                act.wait_ge(up_loaded, n * 16 + 16)
                act.wait_ge(up_sum, (n + 1) * FT)
                nc.scalar.copy(up_hi[:, b, :, :], up_raw[:, :, :]).then_inc(up_hi_done, 1)

            def split_down(n, b):
                act.wait_ge(dn_loaded, n * 16 + 16)
                act.wait_ge(dn_sum, (n + 1) * SUMS)
                nc.scalar.copy(dn_hi[:, b, :, :], dn_raw[:, :, :]).then_inc(dn_hi_done, 1)

            def relu_and_hi(n, b):
                for t in range(FT):
                    k = n * FT + t
                    act.wait_ge(up_sum, k + (2 * FT + 1))
                    act.wait_ge(f_done, k + 1)
                    nc.scalar.activation(relu[:, t % 2, :], up_ps[t % 2][:, :], ACT.Relu).then_inc(relu_done, 1)
                for t in range(FT):
                    k = n * FT + t
                    act.wait_ge(f_done, k + 3)
                    if t == 0:
                        act.wait_ge(dn_sum, (n + 1) * SUMS)
                    nc.scalar.copy(f_hi[:, b, t, :], f[:, t % 2, :]).then_inc(f_hi_done, 1)

            act.sem_inc(up_sum, 2 * FT)
            act.sem_inc(dn_sum, 2 * SUMS)

            def square(g):
                act.wait_ge(y_in[g % 2], 16 * (g // 2 + 1))
                if g >= 1:
                    act.wait_ge(mean_done, g * TT)
                for t in range(TT):
                    nc.scalar.activation(squares[:, t, :], y[:, g % 2, t, :], ACT.Square,
                                         accum_out=sum_sq[:, t:t + 1]).then_inc(squared, 1)

            def high(g, t):
                act.wait_ge(transposed, g * TT + t + 1)
                for q in range(GB):
                    copy = nc.scalar.copy(h_hi[:, 4 * q:4 * q + 4, t * P:(t + 1) * P],
                                          tp[q][:, :].rearrange("p (k c) -> p k c", c=P))
                copy.then_inc(hi_done, 1)

            square(0)
            split_up(0, 0)
            for t in range(TT):
                high(0, t)
            split_down(0, 0)
            for g in range(GROUPS):
                with act.Fori(0, NB - 2, 2) as c:
                    for b in range(2):
                        n = c + (g * NB + b)
                        split_up(n + 1, 1 - b)
                        relu_and_hi(n, b)
                        split_down(n + 1, 1 - b)
                n = (g + 1) * NB - 2
                if g + 1 < GROUPS:
                    square(g + 1)
                split_up(n + 1, 1)
                relu_and_hi(n, 0)
                split_down(n + 1, 1)
                relu_and_hi(n + 1, 1)
                if g + 1 < GROUPS:
                    split_up(n + 2, 0)
                    high(g + 1, 0)
                    high(g + 1, 1)
                    split_down(n + 2, 0)
                    high(g + 1, 2)
                    high(g + 1, 3)

        @block.vector
        def _(dve):
            def square_and_lo(n, b):
                for t in range(FT):
                    k = n * FT + t
                    dve.wait_ge(relu_done, k + 3)
                    dve.wait_ge(f_lo_done, k + 1)
                    nc.vector.tensor_tensor(f[:, t % 2, :], relu[:, t % 2, :], relu[:, t % 2, :],
                                            ALU.mult).then_inc(f_done, 1)
                for t in range(FT):
                    dve.wait_ge(f_hi_done, n * FT + (t + 1))
                    nc.vector.tensor_tensor(f_lo[:, b, t, :], f[:, t % 2, :], f_hi[:, b, t, :].bitcast(F32),
                                            ALU.subtract).then_inc(f_lo_done, 1)

            def add(n, yb, sums=range(SUMS)):
                for i in sums:
                    tt, c = divmod(i, CB)
                    cols = slice(c * BANK, (c + 1) * BANK)
                    dve.wait_ge(dn_sum, n * SUMS + (2 * SUMS + i + 1))
                    dve.wait_ge(added, n * SUMS + (i + 1))
                    nc.vector.tensor_tensor(y[:, yb, tt, cols], acc[i % AR][:, :], y[:, yb, tt, cols],
                                            ALU.add).then_inc(added, 1)

            dve.sem_inc(f_done, 2)
            dve.sem_inc(relu_done, 2)
            dve.sem_inc(f_lo_done, 2)
            dve.sem_inc(added, AR)
            dve.wait_ge(const_in, 32)

            def norm(g):
                if g >= 1:
                    dve.wait_ge(transposed, g * TT)
                for t in range(TT):
                    dve.wait_ge(rstd_done, g * TT + t + 1)
                    nc.vector.scalar_tensor_tensor(
                        out=xn[:, t, :], in0=y[:, g % 2, t, :], scalar=rstd[:, t:t + 1],
                        in1=gain[:, :], op0=ALU.mult, op1=ALU.mult).then_inc(normed, 1)

            def low(g, t):
                dve.wait_ge(hi_done, g * TT + t + 1)
                for q in range(GB):
                    part = h_hi[:, 4 * q:4 * q + 4, t * P:(t + 1) * P]
                    sub = nc.vector.tensor_tensor(h_lo[:, 4 * q:4 * q + 4, t * P:(t + 1) * P],
                                                  tp[q][:, :].rearrange("p (k c) -> p k c", c=P),
                                                  part.bitcast(F32), ALU.subtract)
                sub.then_inc(lo_done, 1)

            norm(0)
            for t in range(TT):
                low(0, t)
            for g in range(GROUPS):
                square_and_lo(g * NB, 0)
                with dve.Fori(0, NB - 2, 2) as c:
                    for b in range(2):
                        n = c + (g * NB + b)
                        square_and_lo(n + 1, 1 - b)
                        add(n, g % 2)
                n = (g + 1) * NB - 2
                if g + 1 < GROUPS:
                    norm(g + 1)
                square_and_lo(n + 1, 1)
                for t in range(TT):
                    if g + 1 < GROUPS:
                        low(g + 1, t)
                    half = t % 2
                    add(n + t // 2, g % 2, range(half * SUMS // 2, (half + 1) * SUMS // 2))

        @block.tensor
        def _(pe):
            def up(n, b):
                pe.wait_ge(up_lo_done, n + 2)
                for t in range(FT):
                    pe.wait_ge(relu_done, n * FT + (t + 1))
                    cols = slice(t * P, (t + 1) * P)
                    for k in range(KT):
                        for w, h in ((up_hi, h_hi), (up_lo, h_hi), (up_hi, h_lo)):
                            mm = nc.tensor.matmul(up_ps[t % 2][:, :], w[:, b, k, cols], h[:, k, :],
                                                  start=k == 0 and w is up_hi and h is h_hi,
                                                  stop=k == KT - 1 and h is h_lo)
                    mm.then_inc(up_sum, 1)

            def transpose(g, t):
                pe.wait_ge(normed, g * TT + t + 1)
                if g * TT + t >= 1:
                    pe.wait_ge(lo_done, g * TT + t)
                for k in range(KT):
                    mm = nc.tensor.transpose(tp[k // 4][:, k % 4 * P:k % 4 * P + P],
                                             xn[:, t, k * P:(k + 1) * P], ident[:, :])
                mm.then_inc(transposed, 1)

            def down(n, b, sums=range(SUMS)):
                pe.wait_ge(dn_lo_done, n + 2)
                pe.wait_ge(f_lo_done, n * FT + (FT + 2))
                for i in sums:
                    tt, c = divmod(i, CB)
                    pe.wait_ge(added, n * SUMS + (i + 1))
                    for k in range(FT):
                        for a, w in ((f_hi, dn_hi), (f_lo, dn_hi), (f_hi, dn_lo)):
                            mm = nc.tensor.matmul(acc[i % AR][:, :], a[:, b, k, tt * P:(tt + 1) * P],
                                                  w[:, b, k, c * BANK:(c + 1) * BANK],
                                                  start=k == 0 and a is f_hi and w is dn_hi,
                                                  stop=k == FT - 1 and w is dn_lo)
                    mm.then_inc(dn_sum, 1)

            pe.wait_ge(const_in, 32)
            for t in range(TT):
                transpose(0, t)
            for g in range(GROUPS):
                pe.wait_ge(lo_done, (g + 1) * TT)
                up(g * NB, 0)
                with pe.Fori(0, NB - 2, 2) as c:
                    for b in range(2):
                        n = c + (g * NB + b)
                        up(n + 1, 1 - b)
                        down(n, b)
                n = (g + 1) * NB - 2
                up(n + 1, 1)
                for t in range(TT):
                    if g + 1 < GROUPS:
                        transpose(g + 1, t)
                    half = t % 2
                    down(n + t // 2, t // 2, range(half * SUMS // 2, (half + 1) * SUMS // 2))


def shape_tables(S, D):
    f = np.float32
    inv_freq = (f(1) / (f(10000) ** np.linspace(0, 1, HEAD // 2, dtype=f))).astype(f)
    angle = (np.arange(S, dtype=f)[:, None] * inv_freq[None, :]).astype(f)
    cos, sin = np.cos(angle), np.sin(angle)
    rotation = np.stack([np.repeat(cos, 2, axis=1), np.stack([-sin, sin], axis=-1).reshape(S, HEAD)], axis=1)
    log_gamma = np.log(f(1) - f(2) ** (f(-5) - np.arange(RET_HEADS, dtype=f))).astype(f)
    idx = np.arange(P, dtype=f)
    rel = idx[None, :] - idx[:, None]
    scale = f(HEAD ** -0.5)
    decay = np.where(rel[:, None, :] >= 0, np.exp(log_gamma[None, :, None] * np.maximum(rel, 0)[:, None, :]), 0) * scale
    row_decay = np.stack([np.exp(log_gamma[None, :] * (idx[:, None] + 1)),
                          np.exp(log_gamma[None, :] * (P - 1 - idx[:, None])) * scale,
                          np.broadcast_to(np.exp(log_gamma * P)[None, :], (P, RET_HEADS))], axis=1)
    windows = (S - CMP_LEN) // STRIDE + 1
    blocks = S // SLC_LEN
    cs = np.arange(windows)[:, None] * STRIDE
    ss = np.arange(blocks)[None, :] * SLC_LEN
    overlap = np.zeros((P, blocks), f)
    overlap[:windows] = np.clip(np.minimum(cs + CMP_LEN, ss + SLC_LEN) - np.maximum(cs, ss), 0, None) / CMP_LEN
    t_blk = (np.arange(S) // SLC_LEN)[:, None]
    j = np.arange(blocks)[None, :]
    forced = (j == 0) | (j == t_blk) | (j == t_blk - 1)
    eligible = (j <= t_blk).astype(f)
    selection = np.stack([1e4 * forced, eligible, eligible - 1], axis=1)
    block_rows = (np.arange(S)[None, :] // SLC_LEN == np.arange(blocks)[:, None])
    tables = {"identity": np.eye(P), "rotation": rotation, "decay": decay, "row_decay": row_decay,
              "overlap": overlap, "selection": selection, "block_rows": block_rows}
    return {name: np.ascontiguousarray(t, dtype=f) for name, t in tables.items()}


def build_layer(nc, a, out):
    _, S, D = a["x"].shape
    N = a["w_in"].shape[2]
    x = a["x"][0]
    z = nc.dram_tensor("z_scratch", (S, N), F32, kind="Internal").ap()
    mixed = nc.dram_tensor("mixed_scratch", (S, a["w_out"].shape[1]), F32, kind="Internal").ap()
    x2 = nc.dram_tensor("x2_scratch", (S, D), F32, kind="Internal").ap()
    ident = a["identity"]
    projection_phase(nc, x, a["norm_mix"][0], a["w_in"][0], ident, z)
    with ExitStack() as stack:
        m = Space(nc, stack, "keys")
        cmp_a = m.sb("cmp_a", [P, GROUPS, P], F32R)
        cmp_b = m.sb("cmp_b", [P, GROUPS, P], F32R)
        cmp_v = m.sb("cmp_v", [P, GROUPS, HEAD + S // SLC_LEN])
        consts = Constants(m, S, CC - CB_)
        compress_phase(nc, z, [(a["cmp_pe_k"][0], a["cmp_w1_k"][0], a["cmp_w2_k"][0]),
                               (a["cmp_pe_v"][0], a["cmp_w1_v"][0], a["cmp_w2_v"][0])],
                       a["conv_w"][0], a["nsa_q_norm"][0], a["nsa_k_norm"][0], a, consts, cmp_a, cmp_b, cmp_v)
        mixers_phase(nc, z, a, consts, cmp_a, cmp_b, cmp_v, mixed)
    output_phase(nc, mixed, x, a["w_out"][0], ident, x2)
    mlp_phase(nc, x2, a["norm_mlp"][0], a["w_up"][0], a["w_down"][0], ident, out[0])


def kernel(**inputs):
    import concourse.bacc as bacc
    from concourse.bass_utils import run_bass_kernel_spmd

    nc = bacc.Bacc("TRN2", target_bir_lowering=False, num_devices=1)
    assert inputs["x"].shape[0] == 1 and inputs["w_in"].shape[0] == 1
    arrays = {name: np.ascontiguousarray(value) for name, value in inputs.items()}
    arrays.update(shape_tables(*arrays["x"].shape[1:]))
    aps = {name: nc.dram_tensor(f"in_{name}", a.shape, mybir.dt.from_np(a.dtype), kind="ExternalInput").ap()
           for name, a in arrays.items()}
    out = nc.dram_tensor("result", arrays["x"].shape, F32, kind="ExternalOutput").ap()
    build_layer(nc, aps, out)
    r = run_bass_kernel_spmd(nc, [{f"in_{name}": a for name, a in arrays.items()}], core_ids=[0])
    return r.results[0]["result"]
```
